# Optimizing a Trainium2 kernel written in Bass

```python
import jax, jax.numpy as jnp
from jax import lax
import numpy as np

D_MODEL = 1024
BATCH = 1
SEQ = 512
DEPTH = 1

N_BRANCH = 4
BRANCH_WIDTH = D_MODEL // 4
HEAD_DIM = 64
N_HEADS_SB = BRANCH_WIDTH // HEAD_DIM
N_HEADS_FOX = BRANCH_WIDTH // HEAD_DIM
D_CONV_A = BRANCH_WIDTH
D_SB = N_HEADS_SB * HEAD_DIM
D_FOX = N_HEADS_FOX * HEAD_DIM
D_CONF = BRANCH_WIDTH
CONV_A_WIDTH = 3
CONF_WIDTH = 31
Q_BLOCK = 128
D_IN_PROJ = 3 * D_CONV_A + 3 * D_SB + 3 * D_FOX + N_HEADS_FOX + 2 * D_CONF
N_GROUPS = 4
EXPERTS_PER_GROUP = 8
N_EXPERTS = N_GROUPS * EXPERTS_PER_GROUP
TOP_K_IN_GROUP = 2
D_EXPERT = D_MODEL // 4
EPS = 1e-6

kernel_name = "hybrid_gated_mixers_hmoe"

def rms_norm(x, g):
    xf = x.astype(jnp.float32)
    y = xf * lax.rsqrt(jnp.mean(xf * xf, axis=-1, keepdims=True) + EPS)
    return (y * g.astype(jnp.float32)).astype(x.dtype)

def layer_norm(x, g, b):
    xf = x.astype(jnp.float32)
    mu = jnp.mean(xf, axis=-1, keepdims=True)
    var = jnp.mean(jnp.square(xf - mu), axis=-1, keepdims=True)
    y = (xf - mu) * lax.rsqrt(var + EPS)
    return (y * g.astype(jnp.float32) + b.astype(jnp.float32)).astype(x.dtype)

def causal_depthwise_conv(x, w):
    k_width = w.shape[0]
    return lax.conv_general_dilated(
        x, w[:, None, :].astype(x.dtype), window_strides=(1,), padding=[(k_width - 1, 0)],
        dimension_numbers=("NWC", "WIO", "NWC"), feature_group_count=x.shape[-1])

def split_heads(t, n_heads):
    b, s, _ = t.shape
    return t.reshape(b, s, n_heads, HEAD_DIM).transpose(0, 2, 1, 3).astype(jnp.float32)

def to_query_blocks(q):
    b, h, s, d = q.shape
    return q.reshape(b, h, s // Q_BLOCK, Q_BLOCK, d).transpose(2, 0, 1, 3, 4)

def from_query_blocks(o):
    nb, b, h, qb, d = o.shape
    return o.transpose(1, 0, 3, 2, 4).reshape(b, nb * qb, h * d)

def stick_breaking_attention(q, k, v):
    s_len = k.shape[2]
    scale = HEAD_DIM ** -0.5
    kpos = jnp.arange(s_len)

    def block(args):
        qb, i = args
        qpos = i * Q_BLOCK + jnp.arange(Q_BLOCK)
        z = jnp.einsum("bhqd,bhkd->bhqk", qb, k) * scale
        mask = kpos[None, :] < qpos[:, None]
        log_not = jnp.where(mask, jax.nn.log_sigmoid(-z), 0.0)
        after = lax.cumsum(log_not, axis=3, reverse=True) - log_not
        w = jnp.where(mask, jnp.exp(jax.nn.log_sigmoid(z) + after), 0.0)
        return jnp.einsum("bhqk,bhkd->bhqd", w, v)

    out = lax.map(block, (to_query_blocks(q), jnp.arange(s_len // Q_BLOCK)))
    return from_query_blocks(out)

def forgetting_attention(q, k, v, dcum):
    b, h, s_len, _ = q.shape
    nb = s_len // Q_BLOCK
    scale = HEAD_DIM ** -0.5
    kpos = jnp.arange(s_len)

    def block(args):
        qb, dq, i = args
        qpos = i * Q_BLOCK + jnp.arange(Q_BLOCK)
        logits = jnp.einsum("bhqd,bhkd->bhqk", qb, k) * scale + dq[..., :, None] - dcum[..., None, :]
        logits = jnp.where(kpos[None, :] <= qpos[:, None], logits, -jnp.inf)
        p = jax.nn.softmax(logits, axis=-1)
        return jnp.einsum("bhqk,bhkd->bhqd", p, v)

    dq_blocks = dcum.reshape(b, h, nb, Q_BLOCK).transpose(2, 0, 1, 3)
    out = lax.map(block, (to_query_blocks(q), dq_blocks, jnp.arange(nb)))
    return from_query_blocks(out)

def hybrid_mixer(xn, w_in, b_forget, conv_a_w, conf_dw_w, conf_dw_b, conf_ln_g, conf_ln_b,
                 w_branch, w_gate, b_gate, w_out):
    sizes = (D_CONV_A, D_CONV_A, D_CONV_A, D_SB, D_SB, D_SB, D_FOX, D_FOX, D_FOX, N_HEADS_FOX, 2 * D_CONF)
    split_points = [int(p) for p in np.cumsum(sizes)[:-1]]
    proj = xn @ w_in
    (a_x, a_b, a_c, sb_q, sb_k, sb_v, fx_q, fx_k, fx_v, fx_f, conf_in) = jnp.split(proj, split_points, axis=-1)

    y_a = a_b * causal_depthwise_conv(a_c * a_x, conv_a_w)

    y_sb = stick_breaking_attention(split_heads(sb_q, N_HEADS_SB), split_heads(sb_k, N_HEADS_SB),
                                    split_heads(sb_v, N_HEADS_SB))

    log_f = jax.nn.log_sigmoid((fx_f + b_forget).astype(jnp.float32))
    dcum = lax.cumsum(log_f, axis=1).transpose(0, 2, 1)
    y_fox = forgetting_attention(split_heads(fx_q, N_HEADS_FOX), split_heads(fx_k, N_HEADS_FOX),
                                 split_heads(fx_v, N_HEADS_FOX), dcum)

    u, u_gate = jnp.split(conf_in, 2, axis=-1)
    u = u * jax.nn.sigmoid(u_gate)
    u = causal_depthwise_conv(u, conf_dw_w) + conf_dw_b
    y_conf = jax.nn.silu(layer_norm(u, conf_ln_g, conf_ln_b))

    branches = (y_a, y_sb, y_fox, y_conf)
    h = jnp.zeros_like(xn)
    for g in range(N_BRANCH):
        gate = jax.nn.sigmoid(xn @ w_gate[g] + b_gate[g])
        h = h + gate * (branches[g].astype(xn.dtype) @ w_branch[g])
    return h @ w_out

def hierarchical_moe(xn, w_router_group, w_router_expert, w_expert_gate, w_expert_up, w_expert_down):
    b, s, d = xn.shape
    t = xn.reshape(b * s, d)
    group_probs = jax.nn.softmax((t @ w_router_group).astype(jnp.float32), axis=-1)
    g_idx = jnp.argmax(group_probs, axis=-1)
    p_group = jnp.take_along_axis(group_probs, g_idx[:, None], axis=1)
    expert_logits = jnp.einsum("td,dge->tge", t, w_router_expert).astype(jnp.float32)
    in_group = jnp.take_along_axis(expert_logits, g_idx[:, None, None], axis=1)[:, 0]
    top_p, top_i = lax.top_k(jax.nn.softmax(in_group, axis=-1), TOP_K_IN_GROUP)
    top_p = top_p / jnp.sum(top_p, axis=-1, keepdims=True)
    expert_id = g_idx[:, None] * EXPERTS_PER_GROUP + top_i
    combine = jnp.sum(jax.nn.one_hot(expert_id, N_EXPERTS, dtype=jnp.float32)
                      * (p_group * top_p)[..., None], axis=1).astype(t.dtype)
    out = jnp.zeros_like(t)
    for e in range(N_EXPERTS):
        hid = jax.nn.silu(t @ w_expert_gate[e]) * (t @ w_expert_up[e])
        out = out + combine[:, e:e + 1] * (hid @ w_expert_down[e])
    return out.reshape(b, s, d)

def setup_inputs(seed: int = 0) -> dict:
    key = jax.random.key(seed)
    ks = jax.random.split(key, 24)
    f32 = jnp.float32

    def nrm(k, shape, fan_in):
        return jax.random.normal(k, shape, f32) * (fan_in ** -0.5)

    def gain(k, shape):
        return 1.0 + 0.02 * jax.random.normal(k, shape, f32)

    def small(k, shape):
        return 0.02 * jax.random.normal(k, shape, f32)

    return {
        "x": jax.random.normal(ks[0], (BATCH, SEQ, D_MODEL), f32),
        "mix_norm_g": gain(ks[1], (DEPTH, D_MODEL)),
        "w_in": nrm(ks[2], (DEPTH, D_MODEL, D_IN_PROJ), D_MODEL),
        "b_forget": jax.random.uniform(ks[3], (DEPTH, N_HEADS_FOX), f32, 1.0, 5.0),
        "conv_a_w": nrm(ks[4], (DEPTH, CONV_A_WIDTH, D_CONV_A), CONV_A_WIDTH),
        "conf_dw_w": nrm(ks[5], (DEPTH, CONF_WIDTH, D_CONF), CONF_WIDTH),
        "conf_dw_b": small(ks[6], (DEPTH, D_CONF)),
        "conf_ln_g": gain(ks[7], (DEPTH, D_CONF)),
        "conf_ln_b": small(ks[8], (DEPTH, D_CONF)),
        "w_branch": nrm(ks[9], (DEPTH, N_BRANCH, BRANCH_WIDTH, D_MODEL), BRANCH_WIDTH),
        "w_gate": nrm(ks[10], (DEPTH, N_BRANCH, D_MODEL, D_MODEL), D_MODEL),
        "b_gate": small(ks[11], (DEPTH, N_BRANCH, D_MODEL)),
        "w_out": nrm(ks[12], (DEPTH, D_MODEL, D_MODEL), D_MODEL),
        "ffn_norm_g": gain(ks[13], (DEPTH, D_MODEL)),
        "w_router_group": nrm(ks[14], (DEPTH, D_MODEL, N_GROUPS), D_MODEL),
        "w_router_expert": nrm(ks[15], (DEPTH, D_MODEL, N_GROUPS, EXPERTS_PER_GROUP), D_MODEL),
        "w_expert_gate": nrm(ks[16], (DEPTH, N_EXPERTS, D_MODEL, D_EXPERT), D_MODEL),
        "w_expert_up": nrm(ks[17], (DEPTH, N_EXPERTS, D_MODEL, D_EXPERT), D_MODEL),
        "w_expert_down": nrm(ks[18], (DEPTH, N_EXPERTS, D_EXPERT, D_MODEL), D_EXPERT),
        "final_norm_g": gain(ks[19], (D_MODEL,)),
    }

def reference(x, mix_norm_g, w_in, b_forget, conv_a_w, conf_dw_w, conf_dw_b, conf_ln_g, conf_ln_b,
              w_branch, w_gate, b_gate, w_out, ffn_norm_g, w_router_group, w_router_expert,
              w_expert_gate, w_expert_up, w_expert_down, final_norm_g):
    for layer in range(DEPTH):
        xn = rms_norm(x, mix_norm_g[layer])
        x = x + hybrid_mixer(xn, w_in[layer], b_forget[layer], conv_a_w[layer], conf_dw_w[layer],
                             conf_dw_b[layer], conf_ln_g[layer], conf_ln_b[layer], w_branch[layer],
                             w_gate[layer], b_gate[layer], w_out[layer])
        xn = rms_norm(x, ffn_norm_g[layer])
        x = x + hierarchical_moe(xn, w_router_group[layer], w_router_expert[layer], w_expert_gate[layer],
                                 w_expert_up[layer], w_expert_down[layer])
    return rms_norm(x, final_norm_g)


_drawn_inputs = setup_inputs


def setup_inputs(seed=0):
    import zlib

    import numpy as np

    out = dict(_drawn_inputs(seed))
    spreads = {}
    factors = {'conf_dw_b': 2.875,
     'conf_ln_g': 4.015,
     'conf_ln_b': 11.432,
     'b_gate': 5.959,
     'final_norm_g': 7.978,
     'ffn_norm_g': 3.2}
    for name, (base, spread) in spreads.items():
        noise = np.random.default_rng([zlib.crc32(name.encode()), seed]).standard_normal(out[name].shape)
        drawn = base * np.exp(spread * noise) if base else spread * noise
        out[name] = __import__('jax').numpy.asarray(drawn.astype(out[name].dtype))
    for name, factor in factors.items():
        out[name] = (out[name] * factor).astype(out[name].dtype)
    return out
```

```python
from contextlib import ExitStack

import numpy as np

import concourse.bass as bass
from concourse import mybir
from concourse.alu_op_type import AluOpType as ALU

ACT = mybir.ActivationFunctionType
AX = mybir.AxisListType
F32 = mybir.dt.float32
F32R = mybir.dt.float32r
BF16 = mybir.dt.bfloat16
I32 = mybir.dt.int32


class Steps:

    def __init__(self, eng, sem):
        self.eng, self.sem, self.n = eng, sem, 0

    def mark(self, ins):
        ins.then_inc(self.sem, 1)
        self.n += 1
        return self.n

    def done(self, n=None):
        self.eng.wait_ge(self.sem, self.n if n is None else n)

    def link(self, ins):
        self.mark(ins)
        self.done()


def hybrid_trunk(nc, x, mix_norm_g, w_in, b_forget, conv_a_w, conf_dw_w, conf_dw_b, conf_ln_g,
                 conf_ln_b, w_branch, w_gate, b_gate, w_out, ffn_norm_g, w_router_group,
                 w_router_expert, w_expert_gate, w_expert_up, w_expert_down, final_norm_g, out):
    P = 128
    T, D = x.shape[1], x.shape[2]
    NT = T // P
    KC = D // P
    NB = w_branch.shape[1]
    BW = w_branch.shape[2]
    BJ = BW // P
    NH = b_forget.shape[1]
    HD = BW // NH
    NE = w_expert_gate.shape[1]
    NG = w_router_group.shape[2]
    EG = NE // NG
    FE = w_expert_gate.shape[3]
    CA_W, CF_W = conv_a_w.shape[1], conf_dw_w.shape[1]
    EPS = 1e-6
    SCALE = HD ** -0.5
    MASKED = -float(2 ** 100)
    FAR = -1e30

    COL_AX, COL_AB, COL_AC = 0, BW, 2 * BW
    COL_SQ, COL_SK, COL_SV = 3 * BW, 4 * BW, 5 * BW
    COL_FQ, COL_FK, COL_FV = 6 * BW, 7 * BW, 8 * BW
    COL_U = 9 * BW + NH
    COL_UG = COL_U + BW
    UC = 256
    PROJ = [("u", COL_U, UC), ("ug", COL_UG, UC), ("ax", COL_AX, UC), ("ac", COL_AC, UC),
            ("ab", COL_AB, UC), ("sq", COL_SQ, UC), ("sk", COL_SK, UC), ("sv", COL_SV, UC),
            ("fq", COL_FQ, UC), ("fk", COL_FK, UC), ("fv", COL_FV, UC + NH)]
    NP = len(PROJ)
    CG = D // UC
    GATE0 = NP
    OUT0 = NP + NB * CG
    NMIX = OUT0 + CG
    UNIT = KC * UC + BJ * UC

    x_v = x[0].rearrange("(t p) d -> t p d", p=P)
    out_v = out[0].rearrange("(t p) d -> t p d", p=P)
    w_in_v = w_in[0].rearrange("(p c) n -> p c n", c=KC)
    w_gate_v = w_gate[0].rearrange("g (p c) n -> g p c n", c=KC)
    w_branch_v = w_branch[0].rearrange("g (j p) n -> g p j n", p=P)
    w_out_v = w_out[0].rearrange("(c p) n -> p c n", p=P)
    eg_v = w_expert_gate[0].rearrange("e (p c) f -> e p (c f)", c=KC)
    eu_v = w_expert_up[0].rearrange("e (p c) f -> e p (c f)", c=KC)
    ed_v = w_expert_down[0].rearrange("e (p m) n -> e p (m n)", m=FE // P)
    xn_dram = nc.dram_tensor("xn_dram", (T, D), F32, kind="Internal").ap()
    y_dram = nc.dram_tensor("y_dram", (2 * T, D), F32, kind="Internal").ap()
    slot_dram = nc.dram_tensor("slot_dram", (NE * T, 1), I32, kind="Internal").ap()

    main = ExitStack()
    with main:
        def region():
            return ExitStack()

        def sb(ctx, name, shape, dt=F32):
            return ctx.enter_context(nc.sbuf_tensor(name, [P] + list(shape), dt))

        def sem(name):
            return main.enter_context(nc.semaphore(name))

        ident = sb(main, "ident", [P])
        identb = sb(main, "identb", [P], BF16)
        causal = sb(main, "causal", [T])
        neg_tri = sb(main, "neg_tri", [P])
        neg_one = sb(main, "neg_one", [P])
        avg = sb(main, "avg", [P])
        maskb = sb(main, "maskb", [P], BF16)
        strictb = sb(main, "strictb", [P], BF16)
        oneb = sb(main, "oneb", [P], BF16)
        eps = sb(main, "eps", [1])
        stat = sb(main, "stat", [3, NT])
        NROW = CA_W + CF_W + 3
        ch = sb(main, "ch", [BJ, NROW])
        bg = sb(main, "bg", [NB * KC])
        bf = sb(main, "bf", [NH])
        expert_i = sb(main, "expert_i", [NE])
        from_last = sb(main, "from_last", [NE])
        val = sb(main, "val", [NT, 2], I32)
        pos = sb(main, "pos", [NT, 2], I32)
        cw = sb(main, "cw", [2, NT])
        slots = sb(main, "slots", [NT, NE], I32)
        toks = sb(main, "toks", [NT, NE], I32)
        flag = sb(main, "flag", [1], I32)
        gather_i = sb(main, "gather_i", [2, 1], I32)
        scatter_i = sb(main, "scatter_i", [2, 1], I32)

        short = region()
        sv = sb(short, "sv", [NT, BW])
        fv = sb(short, "fv", [NT, BW])
        ab = sb(short, "ab", [BJ, T])
        cu = sb(short, "cu", [BJ, CF_W - 1 + T])
        ca = sb(short, "ca", [BJ, CA_W - 1 + T])
        sg = sb(short, "sg", [BJ, T])
        axb = sb(short, "axb", [BJ, T])
        rows = sb(short, "rows", [BW])
        gb_rows = sb(short, "gb_rows", [P])
        ff = sb(short, "ff", [4, NT, NH])
        dq = sb(short, "dq", [NT, NH])
        early = region()
        gmix = sb(early, "gmix", [D])
        junk = sb(early, "junk", [D])
        early.close()
        stick = region()
        sp = sb(stick, "sp", [2, NT, T])
        wts = sb(stick, "wts", [2, T])
        tmp = sb(stick, "tmp", [2, T])
        stick.close()
        fox = region()
        lg = sb(fox, "lg", [2, T])
        pt = sb(fox, "pt", [NT, T])
        dcum = sb(fox, "dcum", [NH, T])
        fbc = sb(fox, "fbc", [2, NT, P])
        small = sb(fox, "small", [2, 5])
        fox.close()
        gated = region()
        gs = sb(gated, "gs", [2, T])
        gp = sb(gated, "gp", [2, T])
        gated.close()
        reach = region()
        sb(reach, "reach", [6 * 1024 + 16])
        mix = region()
        xh = sb(mix, "xh", [KC, T], F32R)
        xl = sb(mix, "xl", [KC, T], F32R)
        raw = sb(mix, "raw", [2, UNIT])
        wh = sb(mix, "wh", [2, UNIT], F32R)
        wl = sb(mix, "wl", [2, UNIT], F32R)
        yh = sb(mix, "yh", [NB, BJ, T], F32R)
        yl = sb(mix, "yl", [NB, BJ, T], F32R)
        a1 = region()
        xt = sb(a1, "xt", [NT, D])
        a1.close()
        a2 = region()
        q_s = sb(a2, "q_s", [BJ, T])
        k_s = sb(a2, "k_s", [BJ, T])
        q_f = sb(a2, "q_f", [BJ, T])
        k_f = sb(a2, "k_f", [BJ, T])
        a2.close()
        a3 = region()
        hsum = sb(a3, "hsum", [KC, T])
        a3.close()
        mix.close()
        reach.close()
        short.close()

        moe = region()
        x2 = sb(moe, "x2", [NT, D])
        RS = 4
        HS = 8
        HU = KC * FE // 2
        eraw = sb(moe, "eraw", [RS, 2 * HU])
        gffn = sb(moe, "gffn", [D])
        xn2 = sb(moe, "xn2", [NT, D])
        xt2 = sb(moe, "xt2", [KC, T])
        wr = sb(moe, "wr", [KC, NG + NE])
        rl = sb(moe, "rl", [NT, NG + NE])
        rg = sb(moe, "rg", [6, NT, NG])
        re = sb(moe, "re", [4, NT, NE])
        ro = sb(moe, "ro", [2, NT, NE])
        rs = sb(moe, "rs", [14, NT])
        rposf = sb(moe, "rposf", [NT, 2])
        rmask = sb(moe, "rmask", [NT, NE], BF16)
        gfin = sb(moe, "gfin", [D])
        ewh = sb(moe, "ewh", [HS, HU], F32R)
        ewl = sb(moe, "ewl", [HS, HU], F32R)
        xg = sb(moe, "xg", [2, D])
        xgh = sb(moe, "xgh", [KC, P], F32R)
        xgl = sb(moe, "xgl", [KC, P], F32R)
        act_g = sb(moe, "act_g", [FE])
        hid = sb(moe, "hid", [FE])
        hidh = sb(moe, "hidh", [FE // P, P], F32R)
        hidl = sb(moe, "hidl", [FE // P, P], F32R)
        ye = sb(moe, "ye", [2, D])
        moe.close()
        fill = slots

        bank = [main.enter_context(nc.psum_tensor(f"bank{i}", [P, T], F32)) for i in range(8)]

        S = {name: sem(name) for name in (
            "pool_step act_step dve_step consts small_in tabs_ready x0 x1 x2s x3 sq_done root xn_ready "
            "xt_psum xt_hi xt_ready raw0 raw1 br0 br1 hi_ready split_ready unit_used "
            "tabs_psum free_p0 free_p1 "
            "ln_in ln_mean ln_cent ln_sq ln_var ln_root ln_norm ln_act y_ready ff_abs ff_ln ff_ready "
            "fbc_ready dc_psum dc_out dq_psum dq_out "
            "z_psum sp_ln sp_max sp_mask acc_done w_exp w_mask o_hi o_split wv_done "
            "l_psum l_max l_bias l_exp l_norm pt_psum pt_out fo_psum fo_hi fo_split "
            "h_zero gate_ps br_ps gate_free gate_mul h_add h_hi h_split out_ps x2_in x2_ready "
            "g_in wr_in sq2 root2 xn2_ready xn_out xt2_ps xt2_a xt2_b lg_ps lg_act lg_d lg_e m_ready rank_ps "
            "pos_ready tab_init tab_w tab_r idx_ready turns gather_col scatter_col gf0 gf1 xt_ps xe_h xe_l silu hid_r "
            "ht_ps ht_h ht_l y_out ye_free sc0 sc1 er0 er1 er2 er3 e_hi e_split e_used "
            "yp0 yp1 comb sq3 root3 fin out_done").split()}
        x_in = [S["x0"], S["x1"], S["x2s"], S["x3"]]
        raw_full, br_full = [S["raw0"], S["raw1"]], [S["br0"], S["br1"]]
        proj_free = [S["free_p0"], S["free_p1"]]
        eraw_full = [S["er0"], S["er1"], S["er2"], S["er3"]]
        g_full, scattered = [S["gf0"], S["gf1"]], [S["sc0"], S["sc1"]]
        y_in = [S["yp0"], S["yp1"]]
        N_SMALL = 16 * 6

        UNIT_OF = {name: n for n, (name, _, _) in enumerate(PROJ)}

        def evacuated(eng, name):
            n = UNIT_OF[name]
            eng.wait_ge(proj_free[n % 2], 2 * (n // 2 + 1))

        STEPS = NH * NT

        def stick_step(n):
            h, kt = n // NT, NT - 1 - n % NT
            return h, kt, kt * P

        def fox_step(n):
            return n // NT, n % NT, (n % NT + 1) * P

        def head_rows(h):
            per = P // HD
            return h // per, (h % per) * HD

        BR0 = 4
        LOOPS = NE // 4
        block = main.enter_context(nc.Block())

        @block.sync
        def _(sp_e):
            for t in range(NT):
                sp_e.dma_start(xt[:, t, :], x_v[t]).then_inc(x_in[t], 16)
                if t == 0:
                    sp_e.dma_start(gmix[:, :], mix_norm_g.to_broadcast([P, D])).then_inc(S["g_in"], 16)
            r = 0
            for src, n in ((conv_a_w[0], CA_W), (conf_dw_w[0], CF_W), (conf_dw_b, 1), (conf_ln_g, 1), (conf_ln_b, 1)):
                sp_e.dma_start(rows[r:r + n, :], src).then_inc(S["small_in"], 16)
                r += n
            sp_e.dma_start(gb_rows[0:NB * KC, :], b_gate[0].rearrange("g (c p) -> (g c) p", p=P)).then_inc(S["small_in"], 16)
            sp_e.dma_start(bf[:, :], b_forget.to_broadcast([P, NH])).then_inc(S["ff_abs"], 16)

            def load_unit(u, src_main, src_branch=None, cols=UC):
                s = u % 2
                if u >= 2:
                    sp_e.wait_ge(S["split_ready"], u - 1)
                sp_e.dma_start(raw[:, s, 0:KC * cols].rearrange("p (c n) -> p c n", c=KC), src_main).then_inc(raw_full[s], 16)

            for u, (_, col, cols) in enumerate(PROJ):
                load_unit(u, w_in_v[:, :, col:col + cols], cols=cols)
            sp_e.wait_ge(S["consts"], 1)
            sp_e.dma_start(slot_dram.rearrange("(p a) o -> p (a o)", p=P), fill[:, :, :].rearrange("p t e -> p (t e)")).then_inc(S["tab_init"], 16)
            with sp_e.Fori(0, NB) as g:
                for cg in range(CG):
                    s = (GATE0 + cg) % 2
                    sp_e.wait_ge(S["split_ready"], g * CG + GATE0 + cg - 1)
                    sp_e.dma_start(raw[:, s, 0:KC * UC].rearrange("p (c n) -> p c n", c=KC),
                                   w_gate_v[bass.ds(g, 1), :, :, cg * UC:(cg + 1) * UC].rearrange("o p c n -> (o p) c n")).then_inc(raw_full[s], 16)
                    sp_e.dma_start(raw[:, s, KC * UC:UNIT].rearrange("p (j n) -> p j n", j=BJ),
                                   w_branch_v[bass.ds(g, 1), :, :, cg * UC:(cg + 1) * UC].rearrange("o p j n -> (o p) j n")).then_inc(br_full[s], 16)
            for t in range(NT):
                sp_e.dma_start(x2[:, t, :], x_v[t]).then_inc(S["x2_in"], 16)
            for cg in range(CG):
                load_unit(OUT0 + cg, w_out_v[:, :, cg * UC:(cg + 1) * UC])
            sp_e.wait_ge(S["h_split"], KC // 2)
            sp_e.dma_start(gffn[:, :], ffn_norm_g.to_broadcast([P, D])).then_inc(S["g_in"], 16)

            def load_expert(w, k, e, slot):
                sp_e.wait_ge(S["e_split"], 2 * w + 2)
                src = (eg_v, eu_v, ed_v)[k]
                view = src[bass.ds(e, 1)].rearrange("o p n -> (o p) n") if not isinstance(e, int) else src[e]
                sp_e.dma_start(eraw[:, slot, :], view).then_inc(eraw_full[slot], 16)

            for k in range(3):
                load_expert(k, k, 0, k)
            sp_e.wait_ge(S["out_ps"], 2 * CG)
            sp_e.dma_start(wr[:, :, 0:NG], w_router_group[0].rearrange("(p c) n -> p c n", c=KC)).then_inc(S["wr_in"], 16)
            sp_e.dma_start(wr[:, :, NG:], w_router_expert[0].rearrange("(p c) g n -> p c (g n)", c=KC)).then_inc(S["wr_in"], 16)
            sp_e.dma_start(gfin[:, :], final_norm_g.rearrange("(o d) -> o d", o=1).to_broadcast([P, D])).then_inc(S["g_in"], 16)
            for t in range(NT):
                sp_e.wait_ge(S["xn2_ready"], t + 1)
                sp_e.dma_start(xn_dram[t * P:(t + 1) * P, :], xn2[:, t, :]).then_inc(S["xn_out"], 16)
            sp_e.wait_ge(S["tab_w"], 16 * 2 * NT)
            sp_e.dma_start(slots[:, :, :], slot_dram.rearrange("(t p e) o -> p t (e o)", p=P, e=NE)).then_inc(S["tab_r"], 16)

            def load_four(base, i, skip=0):
                for n in range(skip, 12):
                    load_expert(base * 3 * NE + i * 12 + n, n % 3, i * 4 + n // 3, n % RS)

            load_four(0, 0, 3)
            with sp_e.Fori(1, LOOPS) as i:
                load_four(0, i)
            most = sp_e.value_load(flag[0:1, 0:1], min_val=0, max_val=T)
            sp_e.wait_ge(S["idx_ready"], 1)
            with sp_e.If(most > P):
                with sp_e.Fori(1, NT) as c:
                    with sp_e.Fori(0, LOOPS) as i:
                        load_four(c, i)
                for s in range(2):
                    sp_e.wait_ge(scattered[s], 16 * NE // 2 * NT)
            for s in range(2):
                sp_e.wait_ge(scattered[s], 16 * NE // 2)
            y_v = y_dram.rearrange("(t p j) d -> t p j d", p=P, j=2)
            for t in range(NT):
                if t >= 2:
                    sp_e.wait_ge(S["out_done"], 16 * (t - 1))
                sp_e.dma_start(xn2[:, 2 * (t % 2):2 * (t % 2) + 2, :], y_v[t]).then_inc(y_in[t % 2], 16)
                if t >= 1:
                    sp_e.wait_ge(S["fin"], t)
                    sp_e.dma_start(out_v[t - 1], xn2[:, 2 * ((t - 1) % 2), :]).then_inc(S["out_done"], 16)
            sp_e.wait_ge(S["fin"], NT)
            sp_e.dma_start(out_v[NT - 1], xn2[:, 2 * ((NT - 1) % 2), :]).then_inc(S["out_done"], 16)
            sp_e.wait_ge(S["out_done"], 16 * NT)

        @block.gpsimd
        def _(pool):
            st = Steps(pool, S["pool_step"])

            def select(t, cols, op, fill_v, base, step, mult, view=None):
                ap = t[:, 0:cols] if view is None else view
                return pool.affine_select(out=ap, in_=ap, compare_op=op, fill=fill_v, base=base,
                                          pattern=[[step, cols]], channel_multiplier=mult)

            for t, v in ((ident, 0.0), (causal, 1.0), (neg_tri, -1.0), (neg_one, -1.0), (avg, 1.0 / BW),
                         (maskb, 0.0), (strictb, 1.0), (oneb, 1.0), (eps, EPS)):
                st.mark(pool.memset(t[:], v))
            st.mark(pool.memset(cu[:, :, 0:CF_W - 1], 0.0))
            st.mark(pool.memset(ca[:, :, 0:CA_W - 1], 0.0))
            st.mark(pool.memset(fill[:, :, :], 8 * T))
            st.mark(pool.iota(expert_i[:, :], pattern=[[1, NE]], base=0, channel_multiplier=0, allow_small_or_imprecise_dtypes=True))
            st.mark(pool.iota(from_last[:, :], pattern=[[-1, NE]], base=NE, channel_multiplier=0, allow_small_or_imprecise_dtypes=True))
            st.mark(pool.iota(val[:, :, :], pattern=[[2 * P, NT], [1, 2]], base=0, channel_multiplier=2))
            st.done()
            st.mark(select(ident, P, ALU.not_equal, 1.0, 0, -1, 1))
            st.mark(select(causal, T, ALU.is_ge, 0.0, 0, 1, -1))
            st.mark(select(neg_tri, P, ALU.is_ge, 0.0, 0, -1, 1))
            st.mark(select(maskb, P, ALU.is_ge, MASKED, 0, -1, 1))
            st.mark(select(strictb, P, ALU.is_gt, 0.0, 0, 1, -1))
            st.done()
            st.link(pool.tensor_copy(identb[:, :], ident[:, :]))
            pool.sem_inc(S["consts"], 1)

            for n in range(STEPS + 3):
                if n >= 3:
                    h, kt, q0 = stick_step(n - 3)
                    pool.wait_ge(S["w_exp"], n - 2)
                    select(None, P, ALU.is_gt, 0.0, 0, 1, -1, view=wts[:, (n - 3) % 2, q0:q0 + P]).then_inc(S["w_mask"], 1)
                if n < STEPS:
                    h, kt, q0 = stick_step(n)
                    pool.wait_ge(S["sp_max"], n + 1)
                    select(None, P, ALU.is_gt, 0.0, 0, 1, -1, view=sp[:, h % 2, kt, q0:q0 + P]).then_inc(S["sp_mask"], 1)
            pool.wait_ge(S["wv_done"], STEPS)
            pool.wait_ge(S["l_psum"], STEPS)
            pool.memset(hsum[:, :, :], 0.0).then_inc(S["h_zero"], 1)

            pool.wait_ge(S["out_ps"], 2 * CG)
            pool.memset(xg[:, :, :], 0.0).then_inc(S["pool_step"], 1)
            st.n += 1
            pool.wait_ge(S["tab_init"], 16)
            pool.wait_ge(S["pos_ready"], 1)
            for t in range(NT):
                for j in range(2):
                    pool.indirect_dma_start(out=slot_dram[:, :], out_offset=bass.IndirectOffsetOnAxis(ap=pos[:, t, j:j + 1], axis=0),
                                            in_=val[:, t, j:j + 1], in_offset=None, bounds_check=NE * T - 1,
                                            oob_is_err=False).then_inc(S["tab_w"], 16)
            pool.wait_ge(S["xn_out"], 16 * NT)
            pool.wait_ge(S["idx_ready"], 1)
            st.done()
            pool.sem_inc(S["ye_free"], 2)
            last_token = pool.to_reg(T - 1)
            last_row = pool.to_reg(2 * T - 1)

            def turn():
                pool.sem_inc(S["turns"], 1)

            def gather(E, q):
                s = q % 2
                pool.tensor_copy(gather_i[:, s, :], toks_f[:, bass.ds(E, 1)]).then_inc(S["gather_col"], 1)
                pool.wait_ge(S["gather_col"], E + 1)
                turn()
                pool.indirect_dma_start(out=xg[:, s, :], out_offset=None, in_=xn_dram[:, :],
                                        in_offset=bass.IndirectOffsetOnAxis(ap=gather_i[:, s, :], axis=0),
                                        bounds_check=last_token, oob_is_err=False).then_inc(g_full[s], 16)

            def scatter(E, q):
                s = q % 2
                pool.wait_ge(S["y_out"], E * 2 + 4)
                pool.wait_ge(S["consts"], 1)
                pool.tensor_copy(scatter_i[:, s, :], slots_f[:, bass.ds(E, 1)]).then_inc(S["scatter_col"], 1)
                pool.wait_ge(S["scatter_col"], E + 1)
                turn()
                pool.indirect_dma_start(out=y_dram[:, :], out_offset=bass.IndirectOffsetOnAxis(ap=scatter_i[:, s, :], axis=0),
                                        in_=ye[:, s, :], in_offset=None, bounds_check=last_row,
                                        oob_is_err=False).then_inc(scattered[s], 16)

            toks_f = toks[:, :, :].rearrange("p t e -> p (t e)")
            slots_f = slots[:, :, :].rearrange("p t e -> p (t e)")

            def start_pass(c):
                for q in range(2):
                    if not isinstance(c, int):
                        pool.wait_ge(S["xt_ps"], c * (2 * NE) - 2 * (1 - q))
                        pool.wait_ge(S["consts"], 1)
                    gather(c * NE + q, q)

            def four(c, i, last=False):
                for q in range(4):
                    E = c * NE + i * 4 + q
                    scatter(E, q)
                    if not (last and q >= 2):
                        pool.wait_ge(S["xt_ps"], E * 2 + 2)
                        gather(E + 2, q)
                    pool.wait_ge(scattered[q % 2], (c * (NE // 2) + i * 2 + q // 2 + 1) * 16)
                    pool.sem_inc(S["ye_free"], 1)

            start_pass(0)
            with pool.Fori(0, LOOPS - 1) as i:
                four(0, i)
            four(0, LOOPS - 1, last=True)
            most = pool.value_load(flag[0:1, 0:1], min_val=0, max_val=T)
            with pool.If(most > P):
                with pool.Fori(1, NT) as c:
                    start_pass(c)
                    with pool.Fori(0, LOOPS - 1) as i:
                        four(c, i)
                    four(c, LOOPS - 1, last=True)

        @block.scalar
        def _(act):
            st = Steps(act, S["act_step"])
            act.wait_ge(S["consts"], 1)
            for t in range(NT):
                act.wait_ge(x_in[t], 16)
                if t:
                    act.wait_ge(S["sq_done"], t)
                act.activation(junk[:, :], xt[:, t, :], ACT.Square, accum_out=stat[:, 0, t:t + 1]).then_inc(S["sq_done"], 1)
            act.wait_ge(S["sq_done"], NT)
            act.activation(stat[:, 1, :], stat[:, 0, :], ACT.Sqrt, bias=eps[:, 0:1], scale=1.0 / D).then_inc(S["root"], 1)
            for c in range(KC):
                act.wait_ge(S["xt_psum"], c + 1)
                act.activation(xh[:, c, :], bank[c % 4][:, :], ACT.Copy).then_inc(S["xt_hi"], 1)

            def split_hi(u, n):
                s = u % 2
                act.wait_ge(raw_full[s], 16 * (u // 2 + 1))
                if u >= OUT0 + 2:
                    act.wait_ge(S["out_ps"], 2 * (u - OUT0 - 1))
                elif 2 <= u < NP:
                    act.wait_ge(S["unit_used"], u - 1)
                act.activation(wh[:, s, 0:n], raw[:, s, 0:n], ACT.Copy).then_inc(S["hi_ready"], 1)

            for u in range(2):
                split_hi(u, KC * PROJ[u][2])
            for u, (name, _, cols) in enumerate(PROJ):
                pair = [bank[4 + 2 * (u % 2) + j] for j in range(2)]
                free = proj_free[u % 2]
                act.wait_ge(S["unit_used"], u + 1)
                if name in ("u", "ax", "ab", "sk", "fk"):
                    dst = {"u": cu[:, :, CF_W - 1:], "ax": axb, "ab": ab, "sk": k_s, "fk": k_f}[name]
                    for j in range(BJ):
                        act.activation(dst[:, j, :], pair[j][:, :], ACT.Copy).then_inc(free, 1)
                elif name == "ug":
                    for j in range(BJ):
                        act.activation(sg[:, j, :], pair[j][:, :], ACT.Sigmoid).then_inc(free, 1)
                elif name in ("sq", "fq"):
                    for j in range(BJ):
                        act.activation({"sq": q_s, "fq": q_f}[name][:, j, :], pair[j][:, :], ACT.Copy, scale=SCALE).then_inc(free, 1)
                elif name == "sv":
                    for j in range(2):
                        act.activation(sv[:, 2 * j:2 * j + 2, :], pair[j][:, :].rearrange("p (t n) -> p t n", t=2), ACT.Copy).then_inc(free, 1)
                elif name == "fv":
                    for t in range(NT):
                        act.activation(fv[:, t, :], bank[4 + t][:, 0:BW], ACT.Copy).then_inc(free, 1)
                if u + 2 < NP:
                    split_hi(u + 2, KC * PROJ[u + 2][2])
            for j in range(BJ):
                act.wait_ge(S["ln_cent"], j + 1)
                act.activation(axb[:, j, :], sg[:, j, :], ACT.Square).then_inc(S["ln_sq"], 1)
            act.wait_ge(S["ln_var"], 1)
            act.activation(ab[:, 0, :], bank[1][:, :], ACT.Sqrt, bias=eps[:, 0:1]).then_inc(S["ln_root"], 1)
            lng, lnb = CA_W + CF_W + 1, CA_W + CF_W + 2
            for j in range(BJ):
                act.wait_ge(S["ln_norm"], j + 1)
                act.activation(axb[:, j, :], sg[:, j, :], ACT.Silu, bias=ch[:, j, lnb:lnb + 1], scale=ch[:, j, lng:lng + 1]).then_inc(S["ln_act"], 1)
            act.wait_ge(S["ff_ln"], 1)
            st.link(act.activation(ff[:, 2, :, :], ff[:, 1, :, :], ACT.Exp, scale=-1.0))
            st.mark(act.activation(ff[:, 2, :, :], ff[:, 2, :, :], ACT.Ln, bias=1.0))
            for n in range(STEPS + 4):
                if n < STEPS:
                    h, kt, q0 = stick_step(n)
                    act.wait_ge(S["z_psum"], n + 1)
                    if n >= 2:
                        act.wait_ge(S["sp_max"], n - 1)
                    b = tmp[:, n % 2, q0:]
                    st.link(act.activation(b, bank[n % 4][:, q0:], ACT.Abs))
                    st.link(act.activation(b, b, ACT.Exp, scale=-1.0))
                    act.activation(b, b, ACT.Ln, bias=1.0).then_inc(S["sp_ln"], 1)
                if 2 <= n < STEPS + 2:
                    m = n - 2
                    h, kt, q0 = stick_step(m)
                    act.wait_ge(S["acc_done"], m + 1)
                    if m >= 2:
                        act.wait_ge(S["wv_done"], m - 1)
                    act.activation(wts[:, m % 2, q0:], bank[m % 4][:, q0:], ACT.Exp).then_inc(S["w_exp"], 1)
                if n >= 4 and n % NT == NT - 1:
                    h = n // NT - 1
                    j, r = head_rows(h)
                    act.wait_ge(S["wv_done"], NT * (h + 1))
                    act.activation(yh[r:r + HD, 1, j, :], bank[4 + h % 2][r:r + HD, :], ACT.Copy).then_inc(S["o_hi"], 1)
            for h in range(NH):
                act.wait_ge(S["dc_psum"], h + 1)
                if h == 0:
                    act.wait_ge(S["wv_done"], STEPS)
                act.activation(dcum[:, h, :], bank[6 + h % 2][:, :], ACT.Copy).then_inc(S["dc_out"], 1)
            for n in range(STEPS + 3):
                if n < STEPS:
                    h, qt, m = fox_step(n)
                    act.wait_ge(S["l_bias"], n + 1)
                    act.activation(lg[:, n % 2, 0:m], lg[:, n % 2, 0:m], ACT.Exp, bias=small[:, n % 2, 2:3],
                                   accum_out=small[:, n % 2, 3:4]).then_inc(S["l_exp"], 1)
                if 1 <= n < STEPS + 1:
                    h, qt, m = fox_step(n - 1)
                    act.wait_ge(S["pt_psum"], n)
                    if qt == 0 and h >= 1:
                        act.wait_ge(S["fo_psum"], h)
                    act.activation(pt[:, 0:qt + 1, qt * P:(qt + 1) * P], bank[6 + (n - 1) % 2][:, 0:m].rearrange("p (k q) -> p k q", q=P),
                                   ACT.Copy).then_inc(S["pt_out"], 1)
                if n >= NT and n % NT == 2:
                    h = n // NT - 1
                    j, r = head_rows(h)
                    act.wait_ge(S["fo_psum"], h + 1)
                    act.activation(yh[r:r + HD, 2, j, :], bank[4 + h % 2][r:r + HD, :], ACT.Copy).then_inc(S["fo_hi"], 1)

            def gate_sigmoid(g, cg):
                for m in range(2):
                    d = g * KC + (2 * cg + m)
                    act.wait_ge(S["gate_ps"], d + 1)
                    act.wait_ge(S["gate_free"], d + 1)
                    act.activation(gs[:, m, :], bank[m][:, :], ACT.Sigmoid,
                                   bias=bg[:, bass.ds(d, 1)]).then_inc(S["gate_mul"], 1)

            def gate_hi(g, cg):
                s = (GATE0 + cg) % 2
                act.wait_ge(raw_full[s], (g * (CG // 2) + (GATE0 + cg) // 2 + 1) * 16)
                act.wait_ge(br_full[s], (g * (CG // 2) + cg // 2 + 1) * 16)
                act.wait_ge(S["br_ps"], g * (2 * CG) + 2 * cg + BR0 - 2)
                act.activation(wh[:, s, :], raw[:, s, :], ACT.Copy).then_inc(S["hi_ready"], 1)

            act.wait_ge(S["unit_used"], NP)
            act.wait_ge(S["wv_done"], STEPS)
            with act.Fori(0, NB) as g:
                for cg in range(CG):
                    gate_hi(g, cg)
                    if cg >= 1:
                        gate_sigmoid(g, cg - 1)
                gate_sigmoid(g, CG - 1)

            act.wait_ge(S["br_ps"], BR0 + NB * KC)
            for c in range(0, KC, 2):
                act.wait_ge(S["h_add"], KC * NB)
                act.activation(xh[:, c:c + 2, :], hsum[:, c:c + 2, :], ACT.Copy).then_inc(S["h_hi"], 1)
            for cg in range(CG):
                split_hi(OUT0 + cg, KC * UC)
            act.wait_ge(S["x2_ready"], 2 * CG)
            for t in range(NT):
                act.activation(xn2[:, t, :], x2[:, t, :], ACT.Square, accum_out=stat[:, 0, t:t + 1]).then_inc(S["sq2"], 1)
            act.wait_ge(S["sq2"], NT)
            act.activation(stat[:, 1, :], stat[:, 0, :], ACT.Sqrt, bias=eps[:, 0:1], scale=1.0 / D).then_inc(S["root2"], 1)
            for c in range(0, KC, 2):
                act.wait_ge(S["xt2_ps"], c + 1)
                act.activation(xt2[:, c, :], bank[4 + c % 4][:, :], ACT.Copy).then_inc(S["xt2_a"], 1)
            act.wait_ge(S["lg_d"], 1)
            act.activation(rg[:, 3, :, :], rg[:, 2, :, :], ACT.Exp).then_inc(S["lg_act"], 1)
            act.wait_ge(S["lg_e"], 1)
            act.activation(rs[:, 5, :], rs[:, 4, :], ACT.Exp).then_inc(S["lg_act"], 1)


            def half_hi(h, slot, k, w, raw_slot):
                act.wait_ge(eraw_full[raw_slot], w)
                act.wait_ge(S["e_used"], h + 1)
                act.activation(ewh[:, slot, :], eraw[:, raw_slot, k * HU:(k + 1) * HU], ACT.Copy).then_inc(S["e_hi"], 1)

            def x_hi(E, b):
                act.wait_ge(S["xt_ps"], E * 2 + b + 1)
                act.activation(xgh[:, 4 * b:4 * b + 4, :], bank[b][:, :].rearrange("p (c s) -> p c s", s=P), ACT.Copy).then_inc(S["xe_h"], 1)

            def hi_of(c, i, n):
                unit = n // 2
                half_hi(c * (6 * NE) + i * 24 + n, n % HS, n % 2,
                        (c * (3 * NE // RS) + i * (12 // RS) + unit // RS + 1) * 16, unit % RS)

            def start_pass(c):
                for n in range(6):
                    hi_of(c, 0, n)
                x_hi(c * NE, 0)
                x_hi(c * NE, 1)

            def four(c, i, last=False):
                for q in range(4):
                    E = c * NE + i * 4 + q
                    ahead = not (last and q == 3)
                    n = 6 * (q + 1)
                    if ahead:
                        hi_of(c, i, n)
                        hi_of(c, i, n + 1)
                    act.wait_ge(S["e_used"], c * (6 * NE) + i * 24 + 6 * q + HS + 2)
                    act.activation(act_g[:, :], bank[2][:, 0:FE], ACT.Silu).then_inc(S["silu"], 1)
                    if ahead:
                        hi_of(c, i, n + 2)
                        hi_of(c, i, n + 3)
                        x_hi(E + 1, 0)
                    act.wait_ge(S["ht_ps"], E + 1)
                    act.activation(hidh[:, :, :], bank[4][:, 0:FE].rearrange("p (m s) -> p m s", s=P), ACT.Copy).then_inc(S["ht_h"], 1)
                    if ahead:
                        x_hi(E + 1, 1)
                        hi_of(c, i, n + 4)
                        hi_of(c, i, n + 5)
                    s = q % 2
                    act.wait_ge(S["ye_free"], E + 1)
                    act.wait_ge(S["e_used"], c * (6 * NE) + i * 24 + 6 * q + HS + 6)
                    for b in range(2):
                        act.activation(ye[:, s, b * T:(b + 1) * T], bank[5 + b][:, :], ACT.Copy).then_inc(S["y_out"], 1)

            act.sem_inc(S["y_out"], 2)
            start_pass(0)
            with act.Fori(0, LOOPS - 1) as i:
                four(0, i)
            four(0, LOOPS - 1, last=True)
            most = act.value_load(flag[0:1, 0:1], min_val=0, max_val=T)
            with act.If(most > P):
                with act.Fori(1, NT) as c:
                    start_pass(c)
                    with act.Fori(0, LOOPS - 1) as i:
                        four(c, i)
                    four(c, LOOPS - 1, last=True)
            for t in range(NT):
                b = xn2[:, 2 * (t % 2), :]
                act.wait_ge(S["comb"], t + 1)
                act.activation(b, x2[:, t, :], ACT.Square, accum_out=stat[:, 0, t:t + 1]).then_inc(S["sq3"], 1)
                act.wait_ge(S["sq3"], t + 1)
                act.activation(stat[:, 1, t:t + 1], stat[:, 0, t:t + 1], ACT.Sqrt, bias=eps[:, 0:1], scale=1.0 / D).then_inc(S["root3"], 1)

        @block.vector
        def _(dve):
            st = Steps(dve, S["dve_step"])

            def stt(out_, a, s, b, o0, o1):
                return dve.scalar_tensor_tensor(out=out_, in0=a, scalar=s, in1=b, op0=o0, op1=o1)

            def lo(dst, src, hi):
                return dve.tensor_tensor(dst, src, hi.bitcast(F32), ALU.subtract)

            def head_lo(name, g, h):
                j, r = head_rows(h)
                dve.wait_ge(S[f"{name}_hi"], h + 1)
                lo(yl[r:r + HD, g, j, :], bank[4 + h % 2][r:r + HD, :], yh[r:r + HD, g, j, :]).then_inc(S[f"{name}_split"], 1)

            def residual(cg):
                if cg == 0:
                    dve.wait_ge(S["x2_in"], 16 * NT)
                for b in range(2):
                    dve.wait_ge(S["out_ps"], 2 * cg + b + 1)
                    cols = slice(cg * UC, (cg + 1) * UC)
                    dve.tensor_tensor(x2[:, 2 * b:2 * b + 2, cols], x2[:, 2 * b:2 * b + 2, cols],
                                      bank[2 * (cg % 2) + b][:, :].rearrange("p (t n) -> p t n", t=2), ALU.add).then_inc(S["x2_ready"], 1)

            dve.wait_ge(S["root"], 1)
            st.link(dve.reciprocal(stat[:, 2, :], stat[:, 1, :]))
            dve.wait_ge(S["g_in"], 16)
            for t in range(NT):
                stt(xt[:, t, :], xt[:, t, :], stat[:, 2, t:t + 1], gmix[:, :], ALU.mult, ALU.mult).then_inc(S["xn_ready"], 1)
            for c in range(KC):
                dve.wait_ge(S["xt_hi"], c + 1)
                lo(xl[:, c, :], bank[c % 4][:, :], xh[:, c, :]).then_inc(S["xt_ready"], 1)
            dve.wait_ge(S["tabs_psum"], 1)
            st.mark(dve.tensor_copy(ch[:, :, :], bank[7][:, 0:BJ * NROW].rearrange("p (j n) -> p j n", j=BJ)))
            dve.tensor_copy(bg[:, :], bank[7][:, P:P + NB * KC]).then_inc(S["tabs_ready"], 1)
            st.done()

            def split_lo(u, n):
                s = u % 2
                dve.wait_ge(S["hi_ready"], u + 1)
                lo(wl[:, s, 0:n], raw[:, s, 0:n], wh[:, s, 0:n]).then_inc(S["split_ready"], 1)

            taps = iter([(i, j) for i in range(CF_W) for j in range(BJ)])

            def conv_taps(count):
                for _ in range(count):
                    i, j = next(taps, (None, None))
                    if i is None:
                        return
                    win = cu[:, j, i:i + T]
                    if i == 0:
                        dwb = CA_W + CF_W
                        st.mark(dve.tensor_scalar(sg[:, j, :], win, ch[:, j, CA_W:CA_W + 1], ch[:, j, dwb:dwb + 1], ALU.mult, ALU.add))
                    else:
                        st.done(st.n - 1)
                        st.mark(stt(sg[:, j, :], win, ch[:, j, CA_W + i:CA_W + i + 1], sg[:, j, :], ALU.mult, ALU.add))

            for u in range(2):
                split_lo(u, KC * PROJ[u][2])
            for u, (name, _, cols) in enumerate(PROJ):
                pair = [bank[4 + 2 * (u % 2) + j] for j in range(2)]
                if name == "ug":
                    evacuated(dve, "u")
                    evacuated(dve, "ug")
                    for j in range(BJ):
                        st.mark(dve.tensor_tensor(cu[:, j, CF_W - 1:], cu[:, j, CF_W - 1:], sg[:, j, :], ALU.mult))
                    st.done()
                if name == "ac":
                    evacuated(dve, "ax")
                    dve.wait_ge(S["unit_used"], u + 1)
                    for j in range(BJ):
                        dve.tensor_tensor(ca[:, j, CA_W - 1:], axb[:, j, :], pair[j][:, :], ALU.mult).then_inc(proj_free[u % 2], 1)
                if name == "ab":
                    evacuated(dve, "ac")
                    evacuated(dve, "ab")
                    for j in range(BJ):
                        st.link(dve.tensor_scalar(axb[:, j, :], ca[:, j, 0:T], ch[:, j, 0:1], None, ALU.mult))
                        for i in range(1, CA_W):
                            st.link(stt(axb[:, j, :], ca[:, j, i:i + T], ch[:, j, i:i + 1], axb[:, j, :], ALU.mult, ALU.add))
                        st.link(dve.tensor_tensor(axb[:, j, :], axb[:, j, :], ab[:, j, :], ALU.mult))
                        st.link(dve.tensor_copy(yh[:, 0, j, :], axb[:, j, :]))
                        st.mark(lo(yl[:, 0, j, :], axb[:, j, :], yh[:, 0, j, :]))
                if name == "fv":
                    dve.wait_ge(S["unit_used"], u + 1)
                    dve.wait_ge(S["ff_abs"], 16)
                    dve.wait_ge(proj_free[u % 2], 2 * (u // 2) + NT)
                    for t in range(NT):
                        st.mark(dve.tensor_tensor(ff[:, 0, t, :], bank[4 + t][:, BW:BW + NH], bf[:, :], ALU.add))
                    st.done()
                    stt(ff[:, 1, :, :], ff[:, 0, :, :], -1.0, ff[:, 0, :, :], ALU.mult, ALU.max).then_inc(S["ff_ln"], 1)
                if u + 2 < NP:
                    split_lo(u + 2, KC * PROJ[u + 2][2])
                if u >= 1:
                    conv_taps(10)
            conv_taps(2 * CF_W)
            st.done()
            dve.sem_inc(S["ln_in"], 1)
            dve.wait_ge(S["ln_mean"], 1)
            for j in range(BJ):
                dve.tensor_tensor(sg[:, j, :], sg[:, j, :], bank[0][:, :], ALU.subtract).then_inc(S["ln_cent"], 1)
            dve.wait_ge(S["ln_root"], 1)
            st.link(dve.reciprocal(ab[:, 1, :], ab[:, 0, :]))
            for j in range(BJ):
                dve.tensor_tensor(sg[:, j, :], sg[:, j, :], ab[:, 1, :], ALU.mult).then_inc(S["ln_norm"], 1)
            for j in range(BJ):
                dve.wait_ge(S["ln_act"], j + 1)
                st.link(dve.tensor_copy(yh[:, 3, j, :], axb[:, j, :]))
                st.mark(lo(yl[:, 3, j, :], axb[:, j, :], yh[:, 3, j, :]))
            dve.wait_ge(S["act_step"], 2)
            stt(ff[:, 3, :, :], ff[:, 0, :, :], 0.0, ff[:, 2, :, :], ALU.min, ALU.subtract).then_inc(S["ff_ready"], 1)
            for n in range(STEPS):
                h, kt, q0 = stick_step(n)
                dve.wait_ge(S["sp_ln"], n + 1)
                if kt == NT - 1 and h >= 2:
                    dve.wait_ge(S["acc_done"], (h - 1) * NT)
                stt(sp[:, h % 2, kt, q0:], bank[n % 4][:, q0:], 0.0, tmp[:, n % 2, q0:], ALU.max, ALU.add).then_inc(S["sp_max"], 1)
                if kt == NT - 1 and h >= 2:
                    head_lo("o", 1, h - 2)
            for h in range(NH - 2, NH):
                head_lo("o", 1, h)
            dve.wait_ge(S["ff_ready"], 1)
            dve.wait_ge(S["wv_done"], STEPS)
            for h in range(NH):
                if h >= 2:
                    dve.wait_ge(S["dc_psum"], h - 1)
                dve.tensor_copy(fbc[:, h % 2, :, :], ff[:, 3, :, h:h + 1].to_broadcast([P, NT, P])).then_inc(S["fbc_ready"], 1)
            dve.wait_ge(S["dq_psum"], 1)
            st.link(dve.tensor_copy(dq[:, :, :], bank[5][:, 0:NT * NH].rearrange("p (t h) -> p t h", h=NH)))
            dve.sem_inc(S["dq_out"], 1)
            dve.wait_ge(S["dc_out"], NH)
            for n in range(STEPS + 1):
                if n < STEPS:
                    h, qt, m = fox_step(n)
                    sm = small[:, n % 2, :]
                    dve.wait_ge(S["l_psum"], n + 1)
                    if n >= 2:
                        dve.wait_ge(S["pt_psum"], n - 1)
                    st.link(dve.tensor_tensor_reduce(out=lg[:, n % 2, 0:m], in0=bank[n % 4][:, 0:m], in1=dcum[:, h, 0:m], scale=1.0,
                                                     scalar=-3e38, op0=ALU.subtract, op1=ALU.max, accum_out=sm[:, 0:1]))
                    dve.sem_inc(S["l_max"], 1)
                    st.link(dve.tensor_tensor(sm[:, 1:2], sm[:, 0:1], dq[:, qt, h:h + 1], ALU.add))
                    dve.tensor_tensor(sm[:, 2:3], dq[:, qt, h:h + 1], sm[:, 1:2], ALU.subtract).then_inc(S["l_bias"], 1)
                if n >= 1:
                    h, qt, m = fox_step(n - 1)
                    sm = small[:, (n - 1) % 2, :]
                    dve.wait_ge(S["l_exp"], n)
                    st.link(dve.reciprocal(sm[:, 4:5], sm[:, 3:4]))
                    dve.tensor_scalar(lg[:, (n - 1) % 2, 0:m], lg[:, (n - 1) % 2, 0:m], sm[:, 4:5], None, ALU.mult).then_inc(S["l_norm"], 1)
                if n >= 4 and n % NT == 2:
                    head_lo("fo", 2, n // NT - 1)
            head_lo("fo", 2, NH - 1)

            def gate_lo(g, cg):
                s = (GATE0 + cg) % 2
                dve.wait_ge(S["hi_ready"], g * CG + GATE0 + cg + 1)
                lo(wl[:, s, :], raw[:, s, :], wh[:, s, :]).then_inc(S["split_ready"], 1)

            def gate_sum(g, cg):
                for m in range(2):
                    d = g * KC + (2 * cg + m)
                    dve.wait_ge(S["gate_mul"], d + 1)
                    dve.wait_ge(S["br_ps"], d + (BR0 + 1))
                    dve.tensor_tensor(gp[:, m, :], gs[:, m, :], bank[2 + m][:, :], ALU.mult).then_inc(S["gate_free"], 1)
                    dve.wait_ge(S["gate_free"], d + 3)
                    dve.tensor_tensor(hsum[:, 2 * cg + m, :], hsum[:, 2 * cg + m, :], gp[:, m, :], ALU.add).then_inc(S["h_add"], 1)

            dve.wait_ge(S["h_zero"], 1)
            dve.sem_inc(S["gate_free"], 2)
            with dve.Fori(0, NB) as g:
                for cg in range(CG):
                    gate_lo(g, cg)
                    if cg >= 1:
                        gate_sum(g, cg - 1)
                gate_sum(g, CG - 1)
            for c in range(0, KC, 2):
                dve.wait_ge(S["h_hi"], c // 2 + 1)
                lo(xl[:, c:c + 2, :], hsum[:, c:c + 2, :], xh[:, c:c + 2, :]).then_inc(S["h_split"], 1)
            dve.sem_inc(S["e_split"], HS)
            for cg in range(CG):
                split_lo(OUT0 + cg, KC * UC)
                if cg >= 1:
                    residual(cg - 1)
            residual(CG - 1)
            dve.wait_ge(S["root2"], 1)
            st.link(dve.reciprocal(stat[:, 2, :], stat[:, 1, :]))
            dve.wait_ge(S["g_in"], 48)
            for t in range(NT):
                stt(xn2[:, t, :], x2[:, t, :], stat[:, 2, t:t + 1], gffn[:, :], ALU.mult, ALU.mult).then_inc(S["xn2_ready"], 1)
            for c in range(1, KC, 2):
                dve.wait_ge(S["xt2_ps"], c + 1)
                dve.tensor_copy(xt2[:, c, :], bank[4 + c % 4][:, :]).then_inc(S["xt2_b"], 1)
            dve.wait_ge(S["lg_ps"], 1)
            st.link(dve.tensor_copy(rl[:, :, :], bank[0][:, 0:NT * (NG + NE)].rearrange("p (t n) -> p t n", t=NT)))

            def first_max(src, n, top, eq, score, best, hot):
                st.link(dve.reduce_max(top, src, AX.X))
                st.link(dve.tensor_tensor(eq, src, top.unsqueeze(2).to_broadcast([P, NT, n]), ALU.is_equal))
                st.link(dve.tensor_tensor(score, eq, from_last[:, 0:n].unsqueeze(1).to_broadcast([P, NT, n]), ALU.mult))
                st.link(dve.reduce_max(best, score, AX.X))
                st.link(dve.tensor_tensor(hot, score, best.unsqueeze(2).to_broadcast([P, NT, n]), ALU.is_equal))

            gl, el = rl[:, :, 0:NG], rl[:, :, NG:]
            first_max(gl, NG, rs[:, 0, :], rg[:, 0, :, :], rg[:, 1, :, :], rs[:, 1, :], rg[:, 4, :, :])
            dve.tensor_tensor(rg[:, 2, :, :], gl, rs[:, 0, :].unsqueeze(2).to_broadcast([P, NT, NG]), ALU.subtract).then_inc(S["lg_d"], 1)
            st.link(dve.tensor_scalar(rg[:, 5, :, :], rg[:, 4, :, :], -1.0, -FAR, ALU.add, ALU.mult))
            for t in range(NT):
                st.mark(dve.tensor_tensor(re[:, 0, t, :].rearrange("p (g e) -> p g e", g=NG), el[:, t, :].rearrange("p (g e) -> p g e", g=NG),
                                          rg[:, 5, t, :].unsqueeze(2).to_broadcast([P, NG, EG]), ALU.add))
            st.done()
            first_max(re[:, 0, :, :], NE, rs[:, 2, :], re[:, 1, :, :], re[:, 2, :, :], rs[:, 1, :], ro[:, 0, :, :])
            st.link(stt(re[:, 3, :, :], ro[:, 0, :, :], 2 * FAR, re[:, 0, :, :], ALU.mult, ALU.add))
            first_max(re[:, 3, :, :], NE, rs[:, 3, :], re[:, 1, :, :], re[:, 2, :, :], rs[:, 1, :], ro[:, 1, :, :])
            dve.tensor_tensor(rs[:, 4, :], rs[:, 3, :], rs[:, 2, :], ALU.subtract).then_inc(S["lg_e"], 1)
            dve.tensor_tensor(rmask[:, :, :], ro[:, 0, :, :], ro[:, 1, :, :], ALU.add).then_inc(S["m_ready"], 1)
            dve.wait_ge(S["lg_act"], 1)
            st.link(dve.reduce_sum(rs[:, 6, :], rg[:, 3, :, :], AX.X))
            st.link(dve.reciprocal(rs[:, 7, :], rs[:, 6, :]))
            dve.wait_ge(S["lg_act"], 2)
            st.link(dve.tensor_scalar(rs[:, 8, :], rs[:, 5, :], 1.0, None, ALU.add))
            st.link(dve.reciprocal(rs[:, 9, :], rs[:, 8, :]))
            st.link(dve.tensor_tensor(cw[:, 0, :], rs[:, 9, :], rs[:, 7, :], ALU.mult))
            st.link(dve.tensor_tensor(cw[:, 1, :], cw[:, 0, :], rs[:, 5, :], ALU.mult))
            dve.wait_ge(S["rank_ps"], 1)
            st.link(stt(re[:, 0, :, :], bank[1][:, 0:NT * NE].rearrange("p (t e) -> p t e", e=NE), float(NE),
                        expert_i[:, :].unsqueeze(1).to_broadcast([P, NT, NE]), ALU.mult, ALU.add))
            for j in range(2):
                st.link(dve.tensor_tensor(re[:, 1 + j, :, :], re[:, 0, :, :], ro[:, j, :, :], ALU.mult))
                st.link(dve.reduce_sum(rposf[:, :, j:j + 1], re[:, 1 + j, :, :], AX.X))
            st.link(dve.reduce_max(rs[:, 10, 0:1], bank[1][:, NT * NE:(NT + 1) * NE], AX.X))
            st.link(dve.tensor_copy(flag[:, :], rs[:, 10, 0:1]))
            dve.tensor_copy(pos[:, :, :], rposf[:, :, :]).then_inc(S["pos_ready"], 1)
            dve.wait_ge(S["tab_r"], 16)
            dve.tensor_scalar(toks[:, :, :], slots[:, :, :], 1, None, ALU.arith_shift_right).then_inc(S["idx_ready"], 1)

            def lo_of(c, i, n):
                h = c * (6 * NE) + i * 24 + n
                unit = n // 2
                dve.wait_ge(S["e_hi"], h + 1)
                lo(ewl[:, n % HS, :], eraw[:, unit % RS, (n % 2) * HU:(n % 2 + 1) * HU], ewh[:, n % HS, :]).then_inc(S["e_split"], 1)

            def x_lo(E, b):
                dve.wait_ge(S["xe_h"], E * 2 + b + 1)
                lo(xgl[:, 4 * b:4 * b + 4, :], bank[b][:, :].rearrange("p (c s) -> p c s", s=P), xgh[:, 4 * b:4 * b + 4, :]).then_inc(S["xe_l"], 1)

            def start_pass(c):
                for n in range(6):
                    lo_of(c, 0, n)
                x_lo(c * NE, 0)
                x_lo(c * NE, 1)

            def four(c, i, last=False):
                for q in range(4):
                    E = c * NE + i * 4 + q
                    ahead = not (last and q == 3)
                    n = 6 * (q + 1)
                    if ahead:
                        lo_of(c, i, n)
                        lo_of(c, i, n + 1)
                        lo_of(c, i, n + 2)
                        lo_of(c, i, n + 3)
                    dve.wait_ge(S["silu"], E + 1)
                    dve.wait_ge(S["e_used"], c * (6 * NE) + i * 24 + 6 * q + HS + 4)
                    dve.tensor_tensor(hid[:, :], act_g[:, :], bank[3][:, 0:FE], ALU.mult).then_inc(S["hid_r"], 1)
                    if ahead:
                        x_lo(E + 1, 0)
                    dve.wait_ge(S["ht_h"], E + 1)
                    lo(hidl[:, :, :], bank[4][:, 0:FE].rearrange("p (m s) -> p m s", s=P), hidh[:, :, :]).then_inc(S["ht_l"], 1)
                    if ahead:
                        x_lo(E + 1, 1)
                        lo_of(c, i, n + 4)
                        lo_of(c, i, n + 5)

            start_pass(0)
            with dve.Fori(0, LOOPS - 1) as i:
                four(0, i)
            four(0, LOOPS - 1, last=True)
            most = dve.value_load(flag[0:1, 0:1], min_val=0, max_val=T)
            with dve.If(most > P):
                with dve.Fori(1, NT) as c:
                    start_pass(c)
                    with dve.Fori(0, LOOPS - 1) as i:
                        four(c, i)
                    four(c, LOOPS - 1, last=True)
            for t in range(NT):
                y0, y1 = xn2[:, 2 * (t % 2), :], xn2[:, 2 * (t % 2) + 1, :]
                dve.wait_ge(y_in[t % 2], 16 * (t // 2 + 1))
                st.link(stt(x2[:, t, :], y0, cw[:, 0, t:t + 1], x2[:, t, :], ALU.mult, ALU.add))
                stt(x2[:, t, :], y1, cw[:, 1, t:t + 1], x2[:, t, :], ALU.mult, ALU.add).then_inc(S["comb"], 1)
                dve.wait_ge(S["root3"], t + 1)
                st.link(dve.reciprocal(stat[:, 2, t:t + 1], stat[:, 1, t:t + 1]))
                dve.wait_ge(S["g_in"], 48)
                stt(y0, x2[:, t, :], stat[:, 2, t:t + 1], gfin[:, :], ALU.mult, ALU.mult).then_inc(S["fin"], 1)

        @block.tensor
        def _(pe):
            def passes(dst, pairs, start=True, stop=True):
                seq = []
                for lh, ll, rh, rlo in pairs:
                    seq += [(lh, rh), (lh, rlo), (ll, rh)]
                for n, (a, b) in enumerate(seq):
                    last = nc.tensor.matmul(dst, a, b, start=start and n == 0, stop=stop and n == len(seq) - 1)
                return last

            pe.wait_ge(S["consts"], 1)
            for c in range(KC):
                if c >= 4:
                    pe.wait_ge(S["xt_ready"], c - 3)
                for t in range(NT):
                    if c == 0:
                        pe.wait_ge(S["xn_ready"], t + 1)
                    last = nc.tensor.transpose(bank[c % 4][:, t * P:(t + 1) * P],
                                               xt[:, t, :].rearrange("p (n c) -> p c n", c=KC)[:, c, :], ident[:, :])
                last.then_inc(S["xt_psum"], 1)
            pe.wait_ge(S["small_in"], N_SMALL)
            for j in range(BJ):
                nc.tensor.transpose(bank[7][:, j * NROW:(j + 1) * NROW], rows[0:NROW, j * P:(j + 1) * P], ident[0:NROW, 0:NROW])
            nc.tensor.transpose(bank[7][:, P:P + NB * KC], gb_rows[0:NB * KC, :], ident[0:NB * KC, 0:NB * KC]).then_inc(S["tabs_psum"], 1)
            pe.wait_ge(S["tabs_ready"], 1)

            for u, (name, _, cols) in enumerate(PROJ):
                s = u % 2
                pe.wait_ge(S["split_ready"], u + 1)
                if u == 0:
                    pe.wait_ge(S["xt_ready"], KC)
                if u >= 2:
                    pe.wait_ge(proj_free[s], 2 * (u // 2))
                if name == "fv":
                    pe.wait_ge(proj_free[1 - s], 2 * ((u - 1) // 2 + 1))
                wv = [w[:, s, 0:KC * cols].rearrange("p (c n) -> p c n", c=KC) for w in (wh, wl)]
                if name in ("sv", "fv"):
                    for t in range(NT):
                        tok = slice(t * P, (t + 1) * P)
                        dst = bank[4 + 2 * s + t // 2][:, (t % 2) * UC:(t % 2) * UC + cols] if name == "sv" else bank[4 + t][:, 0:cols]
                        last = passes(dst, [(xh[:, c, tok], xl[:, c, tok], wv[0][:, c, :], wv[1][:, c, :]) for c in range(KC)])
                else:
                    for j in range(BJ):
                        f = slice(j * P, (j + 1) * P)
                        last = passes(bank[4 + 2 * s + j][:, :], [(wv[0][:, c, f], wv[1][:, c, f], xh[:, c, :], xl[:, c, :]) for c in range(KC)])
                last.then_inc(S["unit_used"], 1)
            pe.wait_ge(S["ln_in"], 1)
            for j in range(BJ):
                last = nc.tensor.matmul(bank[0][:, :], avg[:, :], sg[:, j, :], start=j == 0, stop=j == BJ - 1)
            last.then_inc(S["ln_mean"], 1)
            for j in range(BJ):
                pe.wait_ge(S["ln_sq"], j + 1)
                last = nc.tensor.matmul(bank[1][:, :], avg[:, :], axb[:, j, :], start=j == 0, stop=j == BJ - 1)
            last.then_inc(S["ln_var"], 1)
            pe.wait_ge(S["ln_root"], 1)
            for name in ("sq", "sk", "sv", "fq", "fk", "fv"):
                evacuated(pe, name)
            for n in range(STEPS + 3):
                if n < STEPS:
                    h, kt, q0 = stick_step(n)
                    j, r = head_rows(h)
                    if n >= 4:
                        pe.wait_ge(S["w_exp"], n - 3)
                    nc.tensor.matmul(bank[n % 4][:, q0:], k_s[r:r + HD, j, kt * P:(kt + 1) * P], q_s[r:r + HD, j, q0:],
                                     start=True, stop=True).then_inc(S["z_psum"], 1)
                if 2 <= n < STEPS + 2:
                    m = n - 2
                    h, kt, q0 = stick_step(m)
                    pe.wait_ge(S["sp_mask"], m + 1)
                    last = nc.tensor.matmul(bank[m % 4][:, q0:], neg_tri[:, :], sp[:, h % 2, kt, q0:], start=False, stop=True, skip_group_check=True)
                    for k2 in range(kt + 1, NT):
                        last = nc.tensor.matmul(bank[m % 4][:, k2 * P:], neg_one[:, :], sp[:, h % 2, k2, k2 * P:], start=False, stop=True, skip_group_check=True)
                    last.then_inc(S["acc_done"], 1)
                if n >= 3:
                    m = n - 3
                    h, kt, q0 = stick_step(m)
                    j, r = head_rows(h)
                    pe.wait_ge(S["w_mask"], m + 1)
                    if kt == NT - 1 and h >= 2:
                        pe.wait_ge(S["o_split"], h - 1)
                    last = nc.tensor.matmul(bank[4 + h % 2][:, q0:], sv[:, kt, j * P:(j + 1) * P], wts[:, m % 2, q0:],
                                            start=kt == NT - 1, stop=kt == 0, skip_group_check=True)
                    last.then_inc(S["wv_done"], 1)
            for h in range(NH):
                pe.wait_ge(S["fbc_ready"], h + 1)
                if h >= 2:
                    pe.wait_ge(S["dc_out"], h - 1)
                for t in range(NT):
                    last = nc.tensor.matmul(bank[6 + h % 2][:, t * P:], fbc[:, h % 2, t, :], causal[:, 0:T - t * P], start=t == 0, stop=t == NT - 1)
                last.then_inc(S["dc_psum"], 1)
            pe.wait_ge(S["o_split"], NH)
            for t in range(NT):
                for t2 in range(t + 1):
                    last = nc.tensor.matmul(bank[5][:, t * NH:(t + 1) * NH], causal[:, 0:P] if t2 == t else causal[:, P:2 * P],
                                            ff[:, 3, t2, :], start=t2 == 0, stop=t2 == t)
            last.then_inc(S["dq_psum"], 1)
            pe.wait_ge(S["dq_out"], 1)
            pe.wait_ge(S["dc_out"], NH)
            for n in range(STEPS + 2):
                if n < STEPS:
                    h, qt, m = fox_step(n)
                    j, r = head_rows(h)
                    if n >= 4:
                        pe.wait_ge(S["l_max"], n - 3)
                    nc.tensor.matmul(bank[n % 4][:, 0:m], q_f[r:r + HD, j, qt * P:(qt + 1) * P], k_f[r:r + HD, j, 0:m], start=True, stop=True)
                    nc.tensor.matmul(bank[n % 4][:, m - P:m], identb[:, :], maskb[:, :], start=False, stop=True,
                                     skip_group_check=True).then_inc(S["l_psum"], 1)
                if 1 <= n < STEPS + 1:
                    h, qt, m = fox_step(n - 1)
                    pe.wait_ge(S["l_norm"], n)
                    if n >= 3:
                        pe.wait_ge(S["pt_out"], n - 2)
                    for kt in range(qt + 1):
                        last = nc.tensor.transpose(bank[6 + (n - 1) % 2][:, kt * P:(kt + 1) * P], lg[:, (n - 1) % 2, kt * P:(kt + 1) * P], ident[:, :])
                    last.then_inc(S["pt_psum"], 1)
                if n >= 2 and (n - 2) % NT == NT - 1:
                    h = (n - 2) // NT
                    j, r = head_rows(h)
                    pe.wait_ge(S["pt_out"], n - 1)
                    if h >= 2:
                        pe.wait_ge(S["fo_split"], h - 1)
                    for kt in range(NT):
                        last = nc.tensor.matmul(bank[4 + h % 2][:, kt * P:], fv[:, kt, j * P:(j + 1) * P], pt[:, kt, kt * P:],
                                                start=kt == 0, stop=kt == NT - 1)
                    last.then_inc(S["fo_psum"], 1)
            pe.wait_ge(S["fo_split"], NH)
            pe.wait_ge(S["o_split"], NH)

            yh_f = yh[:, :, :, :].rearrange("p g j t -> p (g j t)")
            yl_f = yl[:, :, :, :].rearrange("p g j t -> p (g j t)")
            pe.sem_inc(S["br_ps"], BR0)
            with pe.Fori(0, NB) as g:
                for cg in range(CG):
                    s = (GATE0 + cg) % 2
                    pe.wait_ge(S["split_ready"], g * CG + GATE0 + cg + 1)
                    gate_w = [w[:, s, 0:KC * UC].rearrange("p (c n) -> p c n", c=KC) for w in (wh, wl)]
                    br_w = [w[:, s, KC * UC:UNIT].rearrange("p (c n) -> p c n", c=BJ) for w in (wh, wl)]
                    for m in range(2):
                        d = g * KC + (2 * cg + m)
                        f = slice(m * P, (m + 1) * P)
                        pe.wait_ge(S["gate_free"], d + 1)
                        passes(bank[m][:, :], [(gate_w[0][:, c, f], gate_w[1][:, c, f], xh[:, c, :], xl[:, c, :])
                                               for c in range(KC)]).then_inc(S["gate_ps"], 1)
                        last = passes(bank[2 + m][:, :], [(br_w[0][:, j, f], br_w[1][:, j, f],
                                                           yh_f[:, bass.ds(g * (BJ * T) + j * T, T)],
                                                           yl_f[:, bass.ds(g * (BJ * T) + j * T, T)]) for j in range(BJ)])
                        last.then_inc(S["br_ps"], 1)

            pe.wait_ge(S["h_split"], KC // 2)
            for cg in range(CG):
                u = OUT0 + cg
                s = u % 2
                pe.wait_ge(S["split_ready"], u + 1)
                if cg >= 2:
                    pe.wait_ge(S["x2_ready"], 2 * (cg - 1))
                wv = [w[:, s, 0:KC * UC].rearrange("p (c n) -> p c n", c=KC) for w in (wh, wl)]
                for t in range(NT):
                    tok = slice(t * P, (t + 1) * P)
                    last = passes(bank[2 * (cg % 2) + t // 2][:, (t % 2) * UC:(t % 2 + 1) * UC],
                                  [(xh[:, c, tok], xl[:, c, tok], wv[0][:, c, :], wv[1][:, c, :]) for c in range(KC)])
                    if t % 2:
                        last.then_inc(S["out_ps"], 1)
            pe.sem_inc(S["e_used"], HS)

            for c in range(KC):
                if c >= 4:
                    pe.wait_ge(S["xt2_a"], (c - 4) // 2 + 1)
                    if c > 4:
                        pe.wait_ge(S["xt2_b"], (c - 3) // 2)
                for t in range(NT):
                    if c == 0:
                        pe.wait_ge(S["xn2_ready"], t + 1)
                    last = nc.tensor.transpose(bank[4 + c % 4][:, t * P:(t + 1) * P],
                                               xn2[:, t, :].rearrange("p (n c) -> p c n", c=KC)[:, c, :], ident[:, :])
                last.then_inc(S["xt2_ps"], 1)
            pe.wait_ge(S["wr_in"], 32)
            pe.wait_ge(S["xt2_a"], KC // 2)
            pe.wait_ge(S["xt2_b"], KC // 2)
            pe.wait_ge(S["x2_ready"], 2 * CG)
            NR = NG + NE
            for t in range(NT):
                for c in range(KC):
                    last = nc.tensor.matmul(bank[0][:, t * NR:(t + 1) * NR], xt2[:, c, t * P:(t + 1) * P], wr[:, c, :], start=c == 0, stop=c == KC - 1)
            last.then_inc(S["lg_ps"], 1)
            pe.wait_ge(S["m_ready"], 1)
            for t in range(NT):
                for t2 in range(t + 1):
                    nc.tensor.matmul(bank[1][:, t * NE:(t + 1) * NE], strictb[:, :] if t2 == t else oneb[:, :], rmask[:, t2, :], start=t2 == 0, stop=t2 == t)
            for t in range(NT):
                last = nc.tensor.matmul(bank[1][:, NT * NE:(NT + 1) * NE], oneb[:, :], rmask[:, t, :], start=t == 0, stop=t == NT - 1)
            last.then_inc(S["rank_ps"], 1)
            pe.wait_ge(S["idx_ready"], 1)

            def x_transposes(q, gathered, b):
                if b == 0:
                    pe.wait_ge(g_full[q % 2], gathered)
                for c in range(4 * b, 4 * b + 4):
                    last = nc.tensor.transpose(bank[b][:, (c % 4) * P:(c % 4 + 1) * P],
                                               xg[:, q % 2, :].rearrange("p (n c) -> p c n", c=KC)[:, c, :], ident[:, :])
                last.then_inc(S["xt_ps"], 1)

            def start_pass(c):
                for b in range(2):
                    x_transposes(0, (c * (NE // 2) + 1) * 16, b)

            def used(ins):
                ins.then_inc(S["e_used"], 1)

            def four(c, i, last=False):
                for q in range(4):
                    E = c * NE + i * 4 + q
                    h0 = c * (6 * NE) + i * 24 + 6 * q + HS
                    pe.wait_ge(S["xe_l"], E * 2 + 2)
                    for m, dst in ((0, bank[2]), (1, bank[3])):
                        for half in range(2):
                            n = 6 * q + 2 * m + half
                            pe.wait_ge(S["e_split"], h0 + 2 * m + half + 1)
                            wv = [w[:, n % HS, :].rearrange("p (c f) -> p c f", f=FE) for w in (ewh, ewl)]
                            ins = passes(dst[:, 0:FE], [(xgh[:, 4 * half + k, :], xgl[:, 4 * half + k, :], wv[0][:, k, :], wv[1][:, k, :])
                                                        for k in range(4)], start=half == 0, stop=half == 1)
                            used(ins)
                    ahead = not (last and q == 3)
                    nxt = (c * (NE // 2) + i * 2 + (q + 1) // 2 + 1) * 16
                    if ahead:
                        x_transposes(q + 1, nxt, 0)
                    pe.wait_ge(S["hid_r"], E + 1)
                    for m in range(FE // P):
                        ins = nc.tensor.transpose(bank[4][:, m * P:(m + 1) * P], hid[:, :].rearrange("p (n m) -> p m n", m=FE // P)[:, m, :], ident[:, :])
                    ins.then_inc(S["ht_ps"], 1)
                    if ahead:
                        x_transposes(q + 1, nxt, 1)
                    pe.wait_ge(S["ht_l"], E + 1)
                    pe.wait_ge(S["y_out"], E * 2 + 2)
                    for m in range(FE // P):
                        n = 6 * q + 4 + m
                        pe.wait_ge(S["e_split"], h0 + 4 + m + 1)
                        for b in range(2):
                            ins = passes(bank[5 + b][:, :], [(hidh[:, m, :], hidl[:, m, :], ewh[:, n % HS, b * T:(b + 1) * T],
                                                              ewl[:, n % HS, b * T:(b + 1) * T])], start=m == 0, stop=m == FE // P - 1)
                        used(ins)

            start_pass(0)
            with pe.Fori(0, LOOPS - 1) as i:
                four(0, i)
            four(0, LOOPS - 1, last=True)
            most = pe.value_load(flag[0:1, 0:1], min_val=0, max_val=T)
            with pe.If(most > P):
                with pe.Fori(1, NT) as c:
                    start_pass(c)
                    with pe.Fori(0, LOOPS - 1) as i:
                        four(c, i)
                    four(c, LOOPS - 1, last=True)


_INS = ["x", "mix_norm_g", "w_in", "b_forget", "conv_a_w", "conf_dw_w", "conf_dw_b", "conf_ln_g", "conf_ln_b",
        "w_branch", "w_gate", "b_gate", "w_out", "ffn_norm_g", "w_router_group", "w_router_expert",
        "w_expert_gate", "w_expert_up", "w_expert_down", "final_norm_g"]


def kernel(**inputs):
    import concourse.bacc as _bacc
    from concourse.bass_utils import run_bass_kernel_spmd as _run

    nc = _bacc.Bacc("TRN2", target_bir_lowering=False, num_devices=1)
    arrays, args = {}, []
    for name in _INS:
        a = np.ascontiguousarray(inputs[name])
        arrays[f"in_{name}"] = a
        args.append(nc.dram_tensor(f"in_{name}", a.shape, mybir.dt.from_np(a.dtype), kind="ExternalInput").ap())
    shape = inputs["x"].shape
    args.append(nc.dram_tensor("out_0", shape, F32, kind="ExternalOutput").ap())
    hybrid_trunk(nc, *args)
    r = _run(nc, [arrays], core_ids=[0])
    return r.results[0]["out_0"]
```

```python
from contextlib import ExitStack

import numpy as np

import concourse.bass as bass
from concourse import mybir
from concourse.alu_op_type import AluOpType as ALU

ACT = mybir.ActivationFunctionType
AX = mybir.AxisListType
F32 = mybir.dt.float32
F32R = mybir.dt.float32r
BF16 = mybir.dt.bfloat16
I32 = mybir.dt.int32


class Steps:

    def __init__(self, eng, sem):
        self.eng, self.sem, self.n = eng, sem, 0

    def mark(self, ins):
        ins.then_inc(self.sem, 1)
        self.n += 1
        return self.n

    def done(self, n=None):
        self.eng.wait_ge(self.sem, self.n if n is None else n)

    def link(self, ins):
        self.mark(ins)
        self.done()


def hybrid_trunk(nc, x, mix_norm_g, w_in, b_forget, conv_a_w, conf_dw_w, conf_dw_b, conf_ln_g,
                 conf_ln_b, w_branch, w_gate, b_gate, w_out, ffn_norm_g, w_router_group,
                 w_router_expert, w_expert_gate, w_expert_up, w_expert_down, final_norm_g, out):
    P = 128
    T, D = x.shape[1], x.shape[2]
    NT = T // P
    KC = D // P
    NB = w_branch.shape[1]
    BW = w_branch.shape[2]
    BJ = BW // P
    NH = b_forget.shape[1]
    HD = BW // NH
    NE = w_expert_gate.shape[1]
    NG = w_router_group.shape[2]
    EG = NE // NG
    FE = w_expert_gate.shape[3]
    CA_W, CF_W = conv_a_w.shape[1], conf_dw_w.shape[1]
    EPS = 1e-6
    SCALE = HD ** -0.5
    MASKED = -float(2 ** 100)
    FAR = -1e30

    COL_AX, COL_AB, COL_AC = 0, BW, 2 * BW
    COL_SQ, COL_SK, COL_SV = 3 * BW, 4 * BW, 5 * BW
    COL_FQ, COL_FK, COL_FV = 6 * BW, 7 * BW, 8 * BW
    COL_U = 9 * BW + NH
    COL_UG = COL_U + BW
    UC = 256
    PROJ = [("u", COL_U, UC), ("ug", COL_UG, UC), ("ax", COL_AX, UC), ("ac", COL_AC, UC),
            ("ab", COL_AB, UC), ("fv", COL_FV, UC + NH), ("sv", COL_SV, UC), ("sq", COL_SQ, UC),
            ("sk", COL_SK, UC), ("fq", COL_FQ, UC), ("fk", COL_FK, UC)]
    NP = len(PROJ)
    CG = D // UC
    GATE0 = NP
    OUT0 = NP + NB * CG
    NMIX = OUT0 + CG
    UNIT = KC * UC + BJ * UC

    x_v = x[0].rearrange("(t p) d -> t p d", p=P)
    out_v = out[0].rearrange("(t p) d -> t p d", p=P)
    w_in_v = w_in[0].rearrange("(p c) n -> p c n", c=KC)
    w_gate_v = w_gate[0].rearrange("g (p c) n -> g p c n", c=KC)
    w_branch_v = w_branch[0].rearrange("g (j p) n -> g p j n", p=P)
    w_out_v = w_out[0].rearrange("(c p) n -> p c n", p=P)
    eg_v = w_expert_gate[0].rearrange("e (p c) f -> e p (c f)", c=KC)
    eu_v = w_expert_up[0].rearrange("e (p c) f -> e p (c f)", c=KC)
    ed_v = w_expert_down[0].rearrange("e (p m) n -> e p (m n)", m=FE // P)
    xn_dram = nc.dram_tensor("xn_dram", (T, D), F32, kind="Internal").ap()
    y_dram = nc.dram_tensor("y_dram", (2 * T, D), F32, kind="Internal").ap()
    slot_dram = nc.dram_tensor("slot_dram", (NE * T, 1), I32, kind="Internal").ap()

    main = ExitStack()
    with main:
        def region():
            return ExitStack()

        def sb(ctx, name, shape, dt=F32):
            return ctx.enter_context(nc.sbuf_tensor(name, [P] + list(shape), dt))

        def sem(name):
            return main.enter_context(nc.semaphore(name))

        ident = sb(main, "ident", [P])
        identb = sb(main, "identb", [P], BF16)
        causal = sb(main, "causal", [T])
        neg_tri = sb(main, "neg_tri", [P])
        neg_one = sb(main, "neg_one", [P])
        avg = sb(main, "avg", [P])
        maskb = sb(main, "maskb", [P], BF16)
        strictb = sb(main, "strictb", [P], BF16)
        oneb = sb(main, "oneb", [P], BF16)
        eps = sb(main, "eps", [1])
        stat = sb(main, "stat", [3, NT])
        NROW = CA_W + CF_W + 3
        ch = sb(main, "ch", [BJ, NROW])
        bg = sb(main, "bg", [NB * KC])
        bf = sb(main, "bf", [NH])
        expert_i = sb(main, "expert_i", [NE])
        from_last = sb(main, "from_last", [NE])
        val = sb(main, "val", [NT, 2], I32)
        pos = sb(main, "pos", [NT, 2], I32)
        cw = sb(main, "cw", [2, NT])
        slots = sb(main, "slots", [NT, NE], I32)
        toks = sb(main, "toks", [NT, NE], I32)
        flag = sb(main, "flag", [1], I32)
        gather_i = sb(main, "gather_i", [4, 1], I32)
        scatter_i = sb(main, "scatter_i", [2, 1], I32)

        bg_neg = sb(main, "bg_neg", [NB * KC])
        ff = sb(main, "ff", [4, NT, NH])
        dq = sb(main, "dq", [NT, NH])
        small = sb(main, "small", [2, 5])
        mix = region()
        first = region()
        gmix = sb(first, "gmix", [D])
        junk = sb(first, "junk", [D])
        first.close()
        sv = sb(mix, "sv", [NT, BW])
        fv = sb(mix, "fv", [NT, BW])
        conv = region()
        cu = sb(conv, "cu", [BJ, CF_W - 1 + T])
        ca = sb(conv, "ca", [BJ, CA_W - 1 + T])
        ab = sb(conv, "ab", [BJ, T])
        sg = sb(conv, "sg", [BJ, T])
        axb = sb(conv, "axb", [BJ, T])
        rows = sb(conv, "rows", [BW])
        gb_rows = sb(conv, "gb_rows", [P])
        conv.close()
        dcum = sb(mix, "dcum", [NH, T])
        sp = sb(mix, "sp", [NT, T])
        wts = sb(mix, "wts", [T])
        tmp = sb(mix, "tmp", [T])
        lg = sb(mix, "lg", [T])
        pt = sb(mix, "pt", [NT, P])
        gated = region()
        fbc = sb(gated, "fbc", [NH, NT, P])
        gated.close()
        gs = sb(mix, "gs", [2, T])
        gp = sb(mix, "gp", [2, T])
        a1 = region()
        xt = sb(a1, "xt", [NT, D])
        a1.close()
        q_s = sb(mix, "q_s", [BJ, T])
        k_s = sb(mix, "k_s", [BJ, T])
        q_f = sb(mix, "q_f", [BJ, T])
        k_f = sb(mix, "k_f", [BJ, T])
        hsum = sb(mix, "hsum", [KC, T])
        xh = sb(mix, "xh", [KC, T], F32R)
        xl = sb(mix, "xl", [KC, T], F32R)
        raw = sb(mix, "raw", [2, UNIT])
        wh = sb(mix, "wh", [2, UNIT], F32R)
        wl = sb(mix, "wl", [2, UNIT], F32R)
        yh = sb(mix, "yh", [NB, BJ, T], F32R)
        yl = sb(mix, "yl", [NB, BJ, T], F32R)
        mix.close()

        moe = region()
        x2 = sb(moe, "x2", [NT, D])
        RS = 6
        HS = 8
        HU = KC * FE // 2
        eraw = sb(moe, "eraw", [RS, 2 * HU])
        gffn = sb(moe, "gffn", [D])
        xn2 = sb(moe, "xn2", [NT, D])
        routing = region()
        xt2 = sb(routing, "xt2", [KC, T])
        routing.close()
        XG = 4
        xg = sb(moe, "xg", [XG, D])
        wr = sb(moe, "wr", [KC, NG + NE])
        rl = sb(moe, "rl", [NT, NG + NE])
        rg = sb(moe, "rg", [6, NT, NG])
        re = sb(moe, "re", [4, NT, NE])
        ro = sb(moe, "ro", [2, NT, NE])
        rs = sb(moe, "rs", [14, NT])
        rposf = sb(moe, "rposf", [NT, 2])
        rmask = sb(moe, "rmask", [NT, NE], BF16)
        gfin = sb(moe, "gfin", [D])
        ewh = sb(moe, "ewh", [HS, HU], F32R)
        ewl = sb(moe, "ewl", [HS, HU], F32R)
        xgh = sb(moe, "xgh", [KC, P], F32R)
        xgl = sb(moe, "xgl", [KC, P], F32R)
        act_g = sb(moe, "act_g", [FE])
        hid = sb(moe, "hid", [FE])
        hidh = sb(moe, "hidh", [FE // P, P], F32R)
        hidl = sb(moe, "hidl", [FE // P, P], F32R)
        ye = sb(moe, "ye", [2, D])
        moe.close()
        yt = eraw[:, :, :].rearrange("p s n -> p (s n)")[:, 0:2 * NT * D].rearrange("p (t j n) -> p t j n", t=NT, j=2)
        fill = slots

        bank = [main.enter_context(nc.psum_tensor(f"bank{i}", [P, T], F32)) for i in range(8)]

        S = {name: sem(name) for name in (
            "pool_step act_step dve_step consts small_in tabs_ready x0 x1 x2s x3 sq_done root xn_ready "
            "xt_psum xt_hi xt_ready raw0 raw1 br0 br1 hi_ready split_ready unit_used "
            "tabs_psum free_p0 free_p1 "
            "ln_in ln_mean ln_cent ln_sq ln_var ln_root ln_norm ln_act y_ready bf_in ff_sum ff_abs ff_ln ff_ready "
            "fbc_ready dc_psum dc_out dq_psum dq_out "
            "z_psum sp_min sp_ln sp_max sp_mask acc_done w_exp w_mask o_hi o_split wv_done "
            "l_psum l_max l_bias l_exp l_norm pt_psum pt_out fo_psum fo_hi fo_split "
            "hi_part xg_ps xg_neg xg_min xg_ln xg_max xg_exp xb_ps xg_free gate_ps br_ps gate_free gate_mul h_add h_hi h_split out_ps x2_in x2_ready "
            "g_in wr_in sq2 root2 xn2_ready xn_out xt2_ps xt2_a xt2_b lg_ps lg_act lg_d lg_e m_ready rank_ps "
            "pos_ready tab_init tab_w tab_r idx_ready turns gather_col scatter_col gf0 gf1 gf2 gf3 xt_ps xe_h xe_l silu hid_r "
            "ht_ps ht_h ht_l y_out ye_free sc0 sc1 er0 er1 er2 er3 er4 er5 e_hi e_split e_used "
            "yp0 yp1 yp2 yp3 comb sq3 root3 fin out_done").split()}
        x_in = [S["x0"], S["x1"], S["x2s"], S["x3"]]
        raw_full, br_full = [S["raw0"], S["raw1"]], [S["br0"], S["br1"]]
        proj_free = [S["free_p0"], S["free_p1"]]
        eraw_full = [S[f"er{n}"] for n in range(RS)]
        g_full, scattered = [S[f"gf{n}"] for n in range(XG)], [S["sc0"], S["sc1"]]
        y_in = [S[f"yp{n}"] for n in range(NT)]
        N_SMALL = 16 * 6

        UNIT_OF = {name: n for n, (name, _, _) in enumerate(PROJ)}

        def evacuated(eng, name):
            n = UNIT_OF[name]
            eng.wait_ge(proj_free[n % 2], 2 * (n // 2 + 1))

        STEPS = NH * NT
        NX = 2 * CG
        LOOP0 = GATE0 + NX - CG
        CAP = 40.0

        def x_unit(k):
            return (0, NB - 1)[k // CG], k % CG

        def stick_step(n):
            h, kt = n // NT, NT - 1 - n % NT
            return h, kt, kt * P

        def fox_step(n):
            return n // NT, n % NT, (n % NT + 1) * P

        def x_tile(n):
            g, cg = x_unit(n // 2)
            return g, 2 * cg + n % 2

        def head_rows(h):
            per = P // HD
            return h // per, (h % per) * HD

        BR0 = 4
        LOOPS = NE // 4
        SC = 2 * RS
        HPE = 6
        UPE = 3
        block = main.enter_context(nc.Block())

        @block.sync
        def _(sp_e):
            for t in range(NT):
                sp_e.dma_start(xt[:, t, :], x_v[t]).then_inc(x_in[t], 16)
                if t == 0:
                    sp_e.dma_start(gmix[:, :], mix_norm_g.to_broadcast([P, D])).then_inc(S["g_in"], 16)
            r = 0
            for src, n in ((conv_a_w[0], CA_W), (conf_dw_w[0], CF_W), (conf_dw_b, 1), (conf_ln_g, 1), (conf_ln_b, 1)):
                sp_e.dma_start(rows[r:r + n, :], src).then_inc(S["small_in"], 16)
                r += n
            sp_e.dma_start(gb_rows[0:NB * KC, :], b_gate[0].rearrange("g (c p) -> (g c) p", p=P)).then_inc(S["small_in"], 16)
            sp_e.dma_start(bf[:, :], b_forget.to_broadcast([P, NH])).then_inc(S["bf_in"], 16)

            def load_unit(u, src_main, src_branch=None, cols=UC):
                s = u % 2
                if u >= 2:
                    sp_e.wait_ge(S["split_ready"], u - 1)
                sp_e.dma_start(raw[:, s, 0:KC * cols].rearrange("p (c n) -> p c n", c=KC), src_main).then_inc(raw_full[s], 16)

            for u, (_, col, cols) in enumerate(PROJ):
                load_unit(u, w_in_v[:, :, col:col + cols], cols=cols)
            sp_e.wait_ge(S["consts"], 1)
            sp_e.dma_start(slot_dram.rearrange("(p a) o -> p (a o)", p=P), fill[:, :, :].rearrange("p t e -> p (t e)")).then_inc(S["tab_init"], 16)
            for k in range(NX):
                g, cg = x_unit(k)
                s = (GATE0 + k) % 2
                load_unit(GATE0 + k, w_gate_v[g, :, :, cg * UC:(cg + 1) * UC])
                sp_e.dma_start(raw[:, s, KC * UC:UNIT].rearrange("p (j n) -> p j n", j=BJ),
                               w_branch_v[g, :, :, cg * UC:(cg + 1) * UC]).then_inc(br_full[s], 16)
            with sp_e.Fori(1, NB - 1) as g:
                for cg in range(CG):
                    s = (GATE0 + cg) % 2
                    sp_e.wait_ge(S["split_ready"], g * CG + LOOP0 + cg - 1)
                    sp_e.dma_start(raw[:, s, 0:KC * UC].rearrange("p (c n) -> p c n", c=KC),
                                   w_gate_v[bass.ds(g, 1), :, :, cg * UC:(cg + 1) * UC].rearrange("o p c n -> (o p) c n")).then_inc(raw_full[s], 16)
                    sp_e.dma_start(raw[:, s, KC * UC:UNIT].rearrange("p (j n) -> p j n", j=BJ),
                                   w_branch_v[bass.ds(g, 1), :, :, cg * UC:(cg + 1) * UC].rearrange("o p j n -> (o p) j n")).then_inc(br_full[s], 16)
            for t in range(NT):
                sp_e.dma_start(x2[:, t, :], x_v[t]).then_inc(S["x2_in"], 16)
            for cg in range(CG):
                load_unit(OUT0 + cg, w_out_v[:, :, cg * UC:(cg + 1) * UC])
            sp_e.wait_ge(S["h_split"], KC // 2)
            sp_e.dma_start(gffn[:, :], ffn_norm_g.to_broadcast([P, D])).then_inc(S["g_in"], 16)

            def load_expert(w, k, e, slot):
                sp_e.wait_ge(S["e_split"], 2 * w + 2)
                src = (eg_v, eu_v, ed_v)[k]
                view = src[bass.ds(e, 1)].rearrange("o p n -> (o p) n") if not isinstance(e, int) else src[e]
                sp_e.dma_start(eraw[:, slot, :], view).then_inc(eraw_full[slot], 16)

            def load_step(c, i, q, k):
                w = 2 + UPE * q + k
                load_expert(c * (UPE * NE) + i * (4 * UPE) + w, k, i * 4 + q + (k < 2), w % RS)

            def load_last(c):
                q = 3
                w = 2 + UPE * q
                load_expert(c * (UPE * NE) + (LOOPS - 1) * (4 * UPE) + w, 2, NE - 1, w % RS)

            def load_four(c, i, skip=0, last=False):
                for n in range(skip, 4 * UPE):
                    if not (last and n >= 3 * UPE):
                        load_step(c, i, n // UPE, n % UPE)
                if last:
                    load_last(c)

            for k in range(2):
                load_expert(k, k, 0, k)
            AHEAD = RS
            for n in range(AHEAD - 2):
                load_step(0, 0, n // UPE, n % UPE)
            sp_e.wait_ge(S["out_ps"], 2 * CG)
            sp_e.dma_start(wr[:, :, 0:NG], w_router_group[0].rearrange("(p c) n -> p c n", c=KC)).then_inc(S["wr_in"], 16)
            sp_e.dma_start(wr[:, :, NG:], w_router_expert[0].rearrange("(p c) g n -> p c (g n)", c=KC)).then_inc(S["wr_in"], 16)
            sp_e.dma_start(gfin[:, :], final_norm_g.rearrange("(o d) -> o d", o=1).to_broadcast([P, D])).then_inc(S["g_in"], 16)
            for t in range(NT):
                sp_e.wait_ge(S["xn2_ready"], t + 1)
                sp_e.dma_start(xn_dram[t * P:(t + 1) * P, :], xn2[:, t, :]).then_inc(S["xn_out"], 16)
            sp_e.wait_ge(S["tab_w"], 16 * 2 * NT)
            sp_e.dma_start(slots[:, :, :], slot_dram.rearrange("(t p e) o -> p t (e o)", p=P, e=NE)).then_inc(S["tab_r"], 16)

            load_four(0, 0, AHEAD - 2)
            with sp_e.Fori(1, LOOPS - 1) as i:
                load_four(0, i)
            load_four(0, LOOPS - 1, last=True)
            most = sp_e.value_load(flag[0:1, 0:1], min_val=0, max_val=T)
            sp_e.wait_ge(S["idx_ready"], 1)
            with sp_e.If(most > P):
                with sp_e.Fori(1, NT) as c:
                    for k in range(2):
                        load_expert(c * (UPE * NE) + k, k, 0, k)
                    with sp_e.Fori(0, LOOPS - 1) as i:
                        load_four(c, i)
                    load_four(c, LOOPS - 1, last=True)
                for s in range(2):
                    sp_e.wait_ge(scattered[s], 16 * NE // 2 * NT)
            for s in range(2):
                sp_e.wait_ge(scattered[s], 16 * NE // 2)
            y_v = y_dram.rearrange("(t p j) d -> t p j d", p=P, j=2)
            for t in range(NT):
                sp_e.dma_start(yt[:, t, :, :], y_v[t]).then_inc(y_in[t], 16)
            for t in range(NT):
                sp_e.wait_ge(S["fin"], t + 1)
                sp_e.dma_start(out_v[t], yt[:, t, 0, :]).then_inc(S["out_done"], 16)
            sp_e.wait_ge(S["out_done"], 16 * NT)

        @block.gpsimd
        def _(pool):
            st = Steps(pool, S["pool_step"])

            def select(t, cols, op, fill_v, base, step, mult, view=None):
                ap = t[:, 0:cols] if view is None else view
                return pool.affine_select(out=ap, in_=ap, compare_op=op, fill=fill_v, base=base,
                                          pattern=[[step, cols]], channel_multiplier=mult)

            for t, v in ((ident, 0.0), (causal, 1.0), (neg_tri, -1.0), (neg_one, -1.0), (avg, 1.0 / BW),
                         (maskb, 0.0), (strictb, 1.0), (oneb, 1.0), (eps, EPS)):
                st.mark(pool.memset(t[:], v))
            st.mark(pool.memset(cu[:, :, 0:CF_W - 1], 0.0))
            st.mark(pool.memset(ca[:, :, 0:CA_W - 1], 0.0))
            st.mark(pool.memset(fill[:, :, :], 8 * T))
            st.mark(pool.iota(expert_i[:, :], pattern=[[1, NE]], base=0, channel_multiplier=0, allow_small_or_imprecise_dtypes=True))
            st.mark(pool.iota(from_last[:, :], pattern=[[-1, NE]], base=NE, channel_multiplier=0, allow_small_or_imprecise_dtypes=True))
            st.mark(pool.iota(val[:, :, :], pattern=[[2 * P, NT], [1, 2]], base=0, channel_multiplier=2))
            st.done()
            st.mark(select(ident, P, ALU.not_equal, 1.0, 0, -1, 1))
            st.mark(select(causal, T, ALU.is_ge, 0.0, 0, 1, -1))
            st.mark(select(neg_tri, P, ALU.is_ge, 0.0, 0, -1, 1))
            st.mark(select(maskb, P, ALU.is_ge, MASKED, 0, -1, 1))
            st.mark(select(strictb, P, ALU.is_gt, 0.0, 0, 1, -1))
            st.done()
            st.link(pool.tensor_copy(identb[:, :], ident[:, :]))
            pool.sem_inc(S["consts"], 1)

            for n in range(STEPS):
                h, kt, q0 = stick_step(n)
                pool.wait_ge(S["sp_max"], n + 1)
                select(None, P, ALU.is_gt, 0.0, 0, 1, -1, view=sp[:, kt, q0:q0 + P]).then_inc(S["sp_mask"], 1)
                pool.wait_ge(S["w_exp"], n + 1)
                select(None, P, ALU.is_gt, 0.0, 0, 1, -1, view=wts[:, q0:q0 + P]).then_inc(S["w_mask"], 1)
            pool.wait_ge(S["lg_ps"], 1)
            pool.memset(xg[:, :, :], 0.0).then_inc(S["pool_step"], 1)
            st.n += 1
            pool.wait_ge(S["tab_init"], 16)
            pool.wait_ge(S["pos_ready"], 1)
            for t in range(NT):
                for j in range(2):
                    pool.indirect_dma_start(out=slot_dram[:, :], out_offset=bass.IndirectOffsetOnAxis(ap=pos[:, t, j:j + 1], axis=0),
                                            in_=val[:, t, j:j + 1], in_offset=None, bounds_check=NE * T - 1,
                                            oob_is_err=False).then_inc(S["tab_w"], 16)
            pool.wait_ge(S["xn_out"], 16 * NT)
            pool.wait_ge(S["idx_ready"], 1)
            st.done()
            pool.sem_inc(S["ye_free"], 2)
            last_token = pool.to_reg(T - 1)
            last_row = pool.to_reg(2 * T - 1)

            def turn():
                pool.sem_inc(S["turns"], 1)

            def gather(E, q):
                s = q % XG
                pool.tensor_copy(gather_i[:, s, :], toks_f[:, bass.ds(E, 1)]).then_inc(S["gather_col"], 1)
                pool.wait_ge(S["gather_col"], E + 1)
                turn()
                pool.indirect_dma_start(out=xg[:, s, :], out_offset=None, in_=xn_dram[:, :],
                                        in_offset=bass.IndirectOffsetOnAxis(ap=gather_i[:, s, :], axis=0),
                                        bounds_check=last_token, oob_is_err=False).then_inc(g_full[s], 16)

            def scatter(E, q):
                s = q % 2
                pool.wait_ge(S["y_out"], E * 2 + 4)
                pool.wait_ge(S["consts"], 1)
                pool.tensor_copy(scatter_i[:, s, :], slots_f[:, bass.ds(E, 1)]).then_inc(S["scatter_col"], 1)
                pool.wait_ge(S["scatter_col"], E + 1)
                turn()
                pool.indirect_dma_start(out=y_dram[:, :], out_offset=bass.IndirectOffsetOnAxis(ap=scatter_i[:, s, :], axis=0),
                                        in_=ye[:, s, :], in_offset=None, bounds_check=last_row,
                                        oob_is_err=False).then_inc(scattered[s], 16)

            toks_f = toks[:, :, :].rearrange("p t e -> p (t e)")
            slots_f = slots[:, :, :].rearrange("p t e -> p (t e)")

            def start_pass(c):
                for q in range(3):
                    if not isinstance(c, int):
                        pool.wait_ge(S["xt_ps"], c * (2 * NE))
                    gather(c * NE + q, q)

            def four(c, i, last=False):
                for q in range(4):
                    E = c * NE + i * 4 + q
                    if not (last and q >= 1):
                        pool.wait_ge(S["xt_ps"], E * 2 + 2)
                        gather(E + 3, q + 3)
                    scatter(E, q)
                    pool.wait_ge(scattered[q % 2], (c * (NE // 2) + i * 2 + q // 2 + 1) * 16)
                    pool.sem_inc(S["ye_free"], 1)

            start_pass(0)
            with pool.Fori(0, LOOPS - 1) as i:
                four(0, i)
            four(0, LOOPS - 1, last=True)
            most = pool.value_load(flag[0:1, 0:1], min_val=0, max_val=T)
            with pool.If(most > P):
                with pool.Fori(1, NT) as c:
                    start_pass(c)
                    with pool.Fori(0, LOOPS - 1) as i:
                        four(c, i)
                    four(c, LOOPS - 1, last=True)

        @block.scalar
        def _(act):
            st = Steps(act, S["act_step"])
            act.wait_ge(S["consts"], 1)
            for t in range(NT):
                act.wait_ge(x_in[t], 16)
                if t:
                    act.wait_ge(S["sq_done"], t)
                act.activation(junk[:, :], xt[:, t, :], ACT.Square, accum_out=stat[:, 0, t:t + 1]).then_inc(S["sq_done"], 1)
            act.wait_ge(S["sq_done"], NT)
            act.activation(stat[:, 1, :], stat[:, 0, :], ACT.Sqrt, bias=eps[:, 0:1], scale=1.0 / D).then_inc(S["root"], 1)
            for c in range(KC):
                act.wait_ge(S["xt_psum"], c + 1)
                act.activation(xh[:, c, :], bank[c % 4][:, :], ACT.Copy).then_inc(S["xt_hi"], 1)

            def split_hi(u, n):
                s = u % 2
                act.wait_ge(raw_full[s], 16 * (u // 2 + 1))
                if u >= OUT0 + 2:
                    act.wait_ge(S["out_ps"], 2 * (u - OUT0 - 1))
                elif 2 <= u < NP:
                    act.wait_ge(S["unit_used"], u - 1)
                act.activation(wh[:, s, 0:n], raw[:, s, 0:n], ACT.Copy).then_inc(S["hi_ready"], 1)

            HALF = UNIT // 2

            def x_hi_part(k, part):
                s = (GATE0 + k) % 2
                if part == 0:
                    act.wait_ge(raw_full[s], 16 * ((GATE0 + k) // 2 + 1))
                    act.wait_ge(br_full[s], 16 * (k // 2 + 1))
                    if k < 2:
                        act.wait_ge(S["unit_used"], GATE0 + k - 1)
                    else:
                        act.wait_ge(S["xb_ps"], 2 * (k - 1))
                part_of = slice(part * HALF, (part + 1) * HALF)
                act.activation(wh[:, s, part_of], raw[:, s, part_of], ACT.Copy).then_inc(S["hi_ready" if part else "hi_part"], 1)

            for u in range(2):
                split_hi(u, KC * PROJ[u][2])
            for u, (name, _, cols) in enumerate(PROJ):
                pair = [bank[4 + 2 * (u % 2) + j] for j in range(2)]
                free = proj_free[u % 2]
                act.wait_ge(S["unit_used"], u + 1)
                if name in ("u", "ax", "ab", "sk", "fk"):
                    dst = {"u": cu[:, :, CF_W - 1:], "ax": axb, "ab": ab, "sk": k_s, "fk": k_f}[name]
                    for j in range(BJ):
                        act.activation(dst[:, j, :], pair[j][:, :], ACT.Copy).then_inc(free, 1)
                elif name == "ug":
                    for j in range(BJ):
                        act.activation(sg[:, j, :], pair[j][:, :], ACT.Sigmoid).then_inc(free, 1)
                elif name in ("sq", "fq"):
                    for j in range(BJ):
                        act.activation({"sq": q_s, "fq": q_f}[name][:, j, :], pair[j][:, :], ACT.Copy, scale=SCALE).then_inc(free, 1)
                elif name == "sv":
                    for j in range(2):
                        act.activation(sv[:, 2 * j:2 * j + 2, :], pair[j][:, :].rearrange("p (t n) -> p t n", t=2), ACT.Copy).then_inc(free, 1)
                elif name == "fv":
                    for t in range(NT):
                        ins = act.activation(fv[:, t, :], bank[4 + t][:, 0:BW], ACT.Copy)
                        if t % 2:
                            ins.then_inc(free, 1)
                if u + 2 < NP:
                    split_hi(u + 2, KC * PROJ[u + 2][2])
                else:
                    for part in range(2):
                        x_hi_part(u + 2 - NP, part)
                if name == "sk":
                    act.wait_ge(S["ff_abs"], 1)
                    act.activation(ff[:, 2, :, :], ff[:, 1, :, :], ACT.Exp, scale=-1.0).then_inc(S["ff_ln"], 1)
                    act.wait_ge(S["ff_ln"], 1)
                    act.activation(ff[:, 2, :, :], ff[:, 2, :, :], ACT.Ln, bias=1.0).then_inc(S["ff_ln"], 1)
                if name == "fq":
                    act.wait_ge(S["ln_in"], 1)
                    for h in range(NH - 1):
                        act.wait_ge(S["dc_psum"], h + 1)
                        act.activation(dcum[:, h, :], bank[1 + h][:, :], ACT.Copy).then_inc(S["dc_out"], 1)
                    for j in range(BJ):
                        act.wait_ge(S["ln_cent"], j + 1)
                        act.activation(axb[:, j, :], sg[:, j, :], ACT.Square).then_inc(S["ln_sq"], 1)
            act.wait_ge(S["dc_psum"], NH)
            act.activation(dcum[:, NH - 1, :], bank[1][:, :], ACT.Copy).then_inc(S["dc_out"], 1)
            act.preload_act_table_set("natural_log_exp_and_others")
            act.wait_ge(S["ln_var"], 1)
            st.link(act.activation(ab[:, 0, :], bank[0][:, :], ACT.Ln, bias=eps[:, 0:1]))
            act.activation(ab[:, 1, :], ab[:, 0, :], ACT.Exp, scale=-0.5).then_inc(S["ln_root"], 1)
            lng, lnb = CA_W + CF_W + 1, CA_W + CF_W + 2
            for j in range(BJ):
                act.wait_ge(S["ln_norm"], j + 1)
                act.activation(axb[:, j, :], sg[:, j, :], ACT.Silu, bias=ch[:, j, lnb:lnb + 1], scale=ch[:, j, lng:lng + 1]).then_inc(S["ln_act"], 1)
            act.preload_act_table_set("natural_log_exp_and_others")
            for n in range(STEPS + 1):
                if n < STEPS:
                    h, kt, q0 = stick_step(n)
                    b = tmp[:, q0:]
                    g, d = x_tile(n)
                    act.wait_ge(S["xg_ps"], n + 1)
                    if n >= 2:
                        act.wait_ge(S["xg_free"], n - 1)
                    act.activation(gs[:, n % 2, :], bank[6 + n % 2][:, :], ACT.Identity, scale=-1.0,
                                   bias=bg_neg[:, g * KC + d:g * KC + d + 1]).then_inc(S["xg_neg"], 1)
                    act.wait_ge(S["sp_min"], n + 1)
                    st.link(act.activation(b, b, ACT.Exp))
                    act.activation(b, b, ACT.Ln, bias=1.0).then_inc(S["sp_ln"], 1)
                    h, qt, m = fox_step(n)
                    act.wait_ge(S["l_bias"], n + 1)
                    act.activation(lg[:, 0:m], lg[:, 0:m], ACT.Exp, bias=small[:, n % 2, 2:3],
                                   accum_out=small[:, n % 2, 3:4]).then_inc(S["l_exp"], 1)
                    b = gp[:, n % 2, :]
                    act.wait_ge(S["xg_min"], n + 1)
                    st.link(act.activation(b, b, ACT.Exp))
                    act.activation(b, b, ACT.Ln, bias=1.0).then_inc(S["xg_ln"], 1)
                    k, part = (n + 3) // 2, (n + 1) % 2
                    if n >= 1 and k < NX:
                        x_hi_part(k, part)
                    act.wait_ge(S["xg_max"], n + 1)
                    act.activation(gs[:, n % 2, :], gp[:, n % 2, :], ACT.Exp, scale=-1.0).then_inc(S["xg_exp"], 1)
                if n and n % NT == 0:
                    h = n // NT - 1
                    j, r = head_rows(h)
                    act.wait_ge(S["wv_done"], n)
                    act.activation(yh[r:r + HD, 1, j, :], bank[3][r:r + HD, :], ACT.Copy).then_inc(S["o_hi"], 1)
                    act.wait_ge(S["fo_psum"], n)
                    act.activation(yh[r:r + HD, 2, j, :], bank[4][r:r + HD, :], ACT.Copy).then_inc(S["fo_hi"], 1)
                if n < STEPS:
                    h, kt, q0 = stick_step(n)
                    act.wait_ge(S["acc_done"], n + 1)
                    if n >= 1:
                        act.wait_ge(S["wv_done"], n)
                    act.activation(wts[:, q0:], bank[0][:, q0:], ACT.Exp).then_inc(S["w_exp"], 1)
                    h, qt, m = fox_step(n)
                    act.wait_ge(S["pt_psum"], n + 1)
                    if n >= 1:
                        act.wait_ge(S["fo_psum"], n)
                    act.activation(pt[:, 0:qt + 1, :], bank[2][:, 0:m].rearrange("p (k q) -> p k q", q=P),
                                   ACT.Copy).then_inc(S["pt_out"], 1)

            def gate_sigmoid(g, cg):
                for m in range(2):
                    d = g * KC + (2 * cg + m)
                    act.wait_ge(S["gate_ps"], d + (1 - KC))
                    act.wait_ge(S["gate_free"], d + (1 - KC))
                    act.activation(gs[:, m, :], bank[m][:, :], ACT.Sigmoid,
                                   bias=bg[:, bass.ds(d, 1)]).then_inc(S["gate_mul"], 1)

            def gate_hi(g, cg):
                s = (GATE0 + cg) % 2
                act.wait_ge(raw_full[s], (g * (CG // 2) + (LOOP0 + cg) // 2 + 1) * 16)
                act.wait_ge(br_full[s], (g * (CG // 2) + (NX - CG + cg) // 2 + 1) * 16)
                act.wait_ge(S["br_ps"], g * (2 * CG) + (2 * cg + BR0 - 2 - KC))
                act.activation(wh[:, s, :], raw[:, s, :], ACT.Copy).then_inc(S["hi_ready"], 1)

            act.wait_ge(S["xb_ps"], STEPS)
            act.wait_ge(S["xg_free"], STEPS)
            with act.Fori(1, NB - 1) as g:
                for cg in range(CG):
                    gate_hi(g, cg)
                    if cg >= 1:
                        gate_sigmoid(g, cg - 1)
                gate_sigmoid(g, CG - 1)

            act.wait_ge(S["br_ps"], BR0 + 2 * KC)
            for c in range(0, KC, 2):
                act.wait_ge(S["h_add"], 2 * KC)
                act.activation(xh[:, c:c + 2, :], hsum[:, c:c + 2, :], ACT.Copy).then_inc(S["h_hi"], 1)
            for cg in range(CG):
                split_hi(OUT0 + cg, KC * UC)
            act.wait_ge(S["x2_ready"], 2 * CG)
            for t in range(NT):
                act.activation(xn2[:, t, :], x2[:, t, :], ACT.Square, accum_out=stat[:, 0, t:t + 1]).then_inc(S["sq2"], 1)
            act.wait_ge(S["sq2"], NT)
            act.activation(stat[:, 1, :], stat[:, 0, :], ACT.Sqrt, bias=eps[:, 0:1], scale=1.0 / D).then_inc(S["root2"], 1)
            for c in range(0, KC, 2):
                act.wait_ge(S["xt2_ps"], c + 1)
                act.activation(xt2[:, c, :], bank[4 + c % 4][:, :], ACT.Copy).then_inc(S["xt2_a"], 1)
            act.wait_ge(S["lg_d"], 1)
            act.activation(rg[:, 3, :, :], rg[:, 2, :, :], ACT.Exp).then_inc(S["lg_act"], 1)
            act.wait_ge(S["lg_e"], 1)
            act.activation(rs[:, 5, :], rs[:, 4, :], ACT.Exp).then_inc(S["lg_act"], 1)


            def half_hi(c, i, n):
                unit = n // 2
                act.wait_ge(eraw_full[unit % RS], (c * (UPE * NE // RS) + i * (4 * UPE // RS) + unit // RS + 1) * 16)
                act.wait_ge(S["e_used"], c * (HPE * NE) + i * (4 * HPE) + n + 1)
                act.activation(ewh[:, n % HS, :], eraw[:, unit % RS, n % 2 * HU:(n % 2 + 1) * HU], ACT.Copy).then_inc(S["e_hi"], 1)

            def x_hi(c, i, q):
                E = c * NE + i * 4 + q
                for b in range(2):
                    act.wait_ge(S["xt_ps"], E * 2 + b + 1)
                    if q:
                        done = HPE * (q - 2) + 8 if q > 1 else 4
                        act.wait_ge(S["e_used"], c * (HPE * NE) + i * (4 * HPE) + (done + HS))
                    act.activation(xgh[:, 4 * b:4 * b + 4, :], bank[b][:, :].rearrange("p (c s) -> p c s", s=P), ACT.Copy).then_inc(S["xe_h"], 1)

            def start_pass(c):
                for n in range(4):
                    half_hi(c, 0, n)
                x_hi(c, 0, 0)
                for n in range(4, 8):
                    half_hi(c, 0, n)
                x_hi(c, 0, 1)
                for n in range(8, 10):
                    half_hi(c, 0, n)

            def four(c, i, last=False):
                for q in range(4):
                    E = c * NE + i * 4 + q
                    n = 4 + HPE * (q + 1)
                    halves = range(n, n + (HPE if not last or q < 2 else 2 if q == 2 else 0))
                    act.wait_ge(S["e_used"], c * (HPE * NE) + i * (4 * HPE) + (HPE * q + 4 + HS))
                    act.activation(act_g[:, :], bank[2 + q % 2][:, 0:FE], ACT.Silu).then_inc(S["silu"], 1)
                    for k in halves[0:2]:
                        half_hi(c, i, k)
                    act.wait_ge(S["ht_ps"], E + 1)
                    act.activation(hidh[:, :, :], bank[4][:, 0:FE].rearrange("p (m s) -> p m s", s=P), ACT.Copy).then_inc(S["ht_h"], 1)
                    for k in halves[2:4]:
                        half_hi(c, i, k)
                    if not (last and q >= 2):
                        x_hi(c, i, q + 2)
                    for k in halves[4:6]:
                        half_hi(c, i, k)
                    s = q % 2
                    act.wait_ge(S["ye_free"], E + 1)
                    done = HPE * (q + 1) + 4 if not (last and q == 3) else HPE * (q + 1)
                    act.wait_ge(S["e_used"], c * (HPE * NE) + i * (4 * HPE) + (done + HS))
                    for b in range(2):
                        act.activation(ye[:, s, b * T:(b + 1) * T], bank[5 + b][:, :], ACT.Copy).then_inc(S["y_out"], 1)

            act.sem_inc(S["y_out"], 2)
            start_pass(0)
            with act.Fori(0, LOOPS - 1) as i:
                four(0, i)
            four(0, LOOPS - 1, last=True)
            most = act.value_load(flag[0:1, 0:1], min_val=0, max_val=T)
            with act.If(most > P):
                with act.Fori(1, NT) as c:
                    start_pass(c)
                    with act.Fori(0, LOOPS - 1) as i:
                        four(c, i)
                    four(c, LOOPS - 1, last=True)
            for t in range(NT):
                act.wait_ge(S["comb"], t + 1)
                act.activation(yt[:, t, 0, :], x2[:, t, :], ACT.Square, accum_out=stat[:, 0, t:t + 1]).then_inc(S["sq3"], 1)
                act.wait_ge(S["sq3"], t + 1)
                act.activation(stat[:, 1, t:t + 1], stat[:, 0, t:t + 1], ACT.Sqrt, bias=eps[:, 0:1], scale=1.0 / D).then_inc(S["root3"], 1)

        @block.vector
        def _(dve):
            st = Steps(dve, S["dve_step"])

            def stt(out_, a, s, b, o0, o1):
                return dve.scalar_tensor_tensor(out=out_, in0=a, scalar=s, in1=b, op0=o0, op1=o1)

            def lo(dst, src, hi):
                return dve.tensor_tensor(dst, src, hi.bitcast(F32), ALU.subtract)

            def head_lo(name, g, h):
                j, r = head_rows(h)
                dve.wait_ge(S[f"{name}_hi"], h + 1)
                lo(yl[r:r + HD, g, j, :], bank[2 + g][r:r + HD, :], yh[r:r + HD, g, j, :]).then_inc(S[f"{name}_split"], 1)

            def residual(cg):
                if cg == 0:
                    dve.wait_ge(S["x2_in"], 16 * NT)
                for b in range(2):
                    dve.wait_ge(S["out_ps"], 2 * cg + b + 1)
                    cols = slice(cg * UC, (cg + 1) * UC)
                    dve.tensor_tensor(x2[:, 2 * b:2 * b + 2, cols], x2[:, 2 * b:2 * b + 2, cols],
                                      bank[2 * (cg % 2) + b][:, :].rearrange("p (t n) -> p t n", t=2), ALU.add).then_inc(S["x2_ready"], 1)

            dve.wait_ge(S["root"], 1)
            st.link(dve.reciprocal(stat[:, 2, :], stat[:, 1, :]))
            dve.wait_ge(S["g_in"], 16)
            for t in range(NT):
                stt(xt[:, t, :], xt[:, t, :], stat[:, 2, t:t + 1], gmix[:, :], ALU.mult, ALU.mult).then_inc(S["xn_ready"], 1)
            for c in range(KC):
                dve.wait_ge(S["xt_hi"], c + 1)
                lo(xl[:, c, :], bank[c % 4][:, :], xh[:, c, :]).then_inc(S["xt_ready"], 1)
            dve.wait_ge(S["tabs_psum"], 1)
            st.mark(dve.tensor_copy(ch[:, :, :], bank[7][:, 0:BJ * NROW].rearrange("p (j n) -> p j n", j=BJ)))
            st.mark(dve.tensor_scalar(bg_neg[:, :], bank[7][:, P:P + NB * KC], -1.0, None, ALU.mult))
            dve.tensor_copy(bg[:, :], bank[7][:, P:P + NB * KC]).then_inc(S["tabs_ready"], 1)
            st.done()

            def split_lo(u, n):
                s = u % 2
                dve.wait_ge(S["hi_ready"], u + 1)
                lo(wl[:, s, 0:n], raw[:, s, 0:n], wh[:, s, 0:n]).then_inc(S["split_ready"], 1)

            HALF = UNIT // 2

            def x_lo_part(k, part):
                s = (GATE0 + k) % 2
                dve.wait_ge(S["hi_ready" if part else "hi_part"], (GATE0 if part else 0) + k + 1)
                part_of = slice(part * HALF, (part + 1) * HALF)
                ins = lo(wl[:, s, part_of], raw[:, s, part_of], wh[:, s, part_of])
                if part:
                    ins.then_inc(S["split_ready"], 1)

            taps = iter([(i, j) for i in range(CF_W) for j in range(BJ)])

            def conv_taps(count):
                for _ in range(count):
                    i, j = next(taps, (None, None))
                    if i is None:
                        return
                    win = cu[:, j, i:i + T]
                    if i == 0:
                        dwb = CA_W + CF_W
                        st.mark(dve.tensor_scalar(sg[:, j, :], win, ch[:, j, CA_W:CA_W + 1], ch[:, j, dwb:dwb + 1], ALU.mult, ALU.add))
                    else:
                        st.done(st.n - 1)
                        st.mark(stt(sg[:, j, :], win, ch[:, j, CA_W + i:CA_W + i + 1], sg[:, j, :], ALU.mult, ALU.add))

            for u in range(2):
                split_lo(u, KC * PROJ[u][2])
            for u, (name, _, cols) in enumerate(PROJ):
                pair = [bank[4 + 2 * (u % 2) + j] for j in range(2)]
                if name == "ug":
                    evacuated(dve, "u")
                    evacuated(dve, "ug")
                    for j in range(BJ):
                        st.mark(dve.tensor_tensor(cu[:, j, CF_W - 1:], cu[:, j, CF_W - 1:], sg[:, j, :], ALU.mult))
                    st.done()
                if name == "ac":
                    evacuated(dve, "ax")
                    dve.wait_ge(S["unit_used"], u + 1)
                    for j in range(BJ):
                        dve.tensor_tensor(ca[:, j, CA_W - 1:], axb[:, j, :], pair[j][:, :], ALU.mult).then_inc(proj_free[u % 2], 1)
                if name == "ab":
                    evacuated(dve, "ac")
                    evacuated(dve, "ab")
                    for j in range(BJ):
                        st.link(dve.tensor_scalar(axb[:, j, :], ca[:, j, 0:T], ch[:, j, 0:1], None, ALU.mult))
                        for i in range(1, CA_W):
                            st.link(stt(axb[:, j, :], ca[:, j, i:i + T], ch[:, j, i:i + 1], axb[:, j, :], ALU.mult, ALU.add))
                        st.link(dve.tensor_tensor(axb[:, j, :], axb[:, j, :], ab[:, j, :], ALU.mult))
                        st.link(dve.tensor_copy(yh[:, 0, j, :], axb[:, j, :]))
                        st.mark(lo(yl[:, 0, j, :], axb[:, j, :], yh[:, 0, j, :]))
                if name == "fv":
                    dve.wait_ge(S["unit_used"], u + 1)
                    dve.wait_ge(S["bf_in"], 16)
                    dve.wait_ge(proj_free[u % 2], 2 * (u // 2 + 1))
                    for t in range(NT):
                        st.mark(dve.tensor_tensor(ff[:, 0, t, :], bank[4 + t][:, BW:BW + NH], bf[:, :], ALU.add))
                    st.done()
                    stt(ff[:, 1, :, :], ff[:, 0, :, :], -1.0, ff[:, 0, :, :], ALU.mult, ALU.max).then_inc(S["ff_abs"], 1)
                if u + 2 < NP:
                    split_lo(u + 2, KC * PROJ[u + 2][2])
                else:
                    for part in range(2):
                        x_lo_part(u + 2 - NP, part)
                if u >= 1:
                    conv_taps(10)
                if name == "sk":
                    dve.wait_ge(S["ff_ln"], 2)
                    st.link(stt(ff[:, 3, :, :], ff[:, 0, :, :], 0.0, ff[:, 2, :, :], ALU.min, ALU.subtract))
                    for h in range(NH):
                        dve.tensor_copy(fbc[:, h, :, :], ff[:, 3, :, h:h + 1].to_broadcast([P, NT, P])).then_inc(S["fbc_ready"], 1)
                    conv_taps(2 * CF_W)
                    st.done()
                    dve.sem_inc(S["ln_in"], 1)
                if name == "fq":
                    dve.wait_ge(S["ln_mean"], 1)
                    for j in range(BJ):
                        dve.tensor_tensor(sg[:, j, :], sg[:, j, :], bank[0][:, :], ALU.subtract).then_inc(S["ln_cent"], 1)
            dve.wait_ge(S["dq_psum"], 1)
            st.link(dve.tensor_copy(dq[:, :, :], bank[2][:, 0:NT * NH].rearrange("p (t h) -> p t h", h=NH)))
            dve.sem_inc(S["dq_out"], 1)
            dve.wait_ge(S["ln_root"], 1)
            for j in range(BJ):
                dve.tensor_tensor(sg[:, j, :], sg[:, j, :], ab[:, 1, :], ALU.mult).then_inc(S["ln_norm"], 1)
            for j in range(BJ):
                dve.wait_ge(S["ln_act"], j + 1)
                st.link(dve.tensor_copy(yh[:, 3, j, :], axb[:, j, :]))
                st.mark(lo(yl[:, 3, j, :], axb[:, j, :], yh[:, 3, j, :]))
            st.done()
            dve.sem_inc(S["y_ready"], 1)
            dve.wait_ge(S["dc_out"], NH)
            for n in range(STEPS + 1):
                if n < STEPS:
                    h, kt, q0 = stick_step(n)
                    dve.wait_ge(S["z_psum"], n + 1)
                    dve.tensor_scalar(tmp[:, q0:], bank[0][:, q0:], CAP, None, ALU.min).then_inc(S["sp_min"], 1)
                    h, qt, m = fox_step(n)
                    sm = small[:, n % 2, :]
                    dve.wait_ge(S["l_psum"], n + 1)
                    if n >= 1:
                        dve.wait_ge(S["pt_psum"], n)
                    st.link(dve.tensor_tensor_reduce(out=lg[:, 0:m], in0=bank[1][:, 0:m], in1=dcum[:, h, 0:m], scale=1.0,
                                                     scalar=-3e38, op0=ALU.subtract, op1=ALU.max, accum_out=sm[:, 0:1]))
                    dve.sem_inc(S["l_max"], 1)
                    st.link(dve.tensor_tensor(sm[:, 1:2], sm[:, 0:1], dq[:, qt, h:h + 1], ALU.add))
                    dve.tensor_tensor(sm[:, 2:3], dq[:, qt, h:h + 1], sm[:, 1:2], ALU.subtract).then_inc(S["l_bias"], 1)
                    g, d = x_tile(n)
                    b, c = gp[:, n % 2, :], gs[:, n % 2, :]
                    dve.wait_ge(S["xg_neg"], n + 1)
                    dve.tensor_scalar(b, c, CAP, None, ALU.min).then_inc(S["xg_min"], 1)
                    h, kt, q0 = stick_step(n)
                    dve.wait_ge(S["sp_ln"], n + 1)
                    if kt == NT - 1 and h:
                        dve.wait_ge(S["acc_done"], h * NT)
                    stt(sp[:, kt, q0:], bank[0][:, q0:], 0.0, tmp[:, q0:], ALU.add, ALU.max).then_inc(S["sp_max"], 1)
                    dve.wait_ge(S["l_exp"], n + 1)
                    st.link(dve.reciprocal(sm[:, 4:5], sm[:, 3:4]))
                    dve.tensor_scalar(lg[:, 0:m], lg[:, 0:m], sm[:, 4:5], None, ALU.mult).then_inc(S["l_norm"], 1)
                    dve.wait_ge(S["xg_ln"], n + 1)
                    dve.tensor_tensor(b, b, c, ALU.max).then_inc(S["xg_max"], 1)
                    k, part = (n + 3) // 2, (n + 1) % 2
                    if n >= 1 and k < NX:
                        x_lo_part(k, part)
                    dve.wait_ge(S["xg_exp"], n + 1)
                    dve.wait_ge(S["xb_ps"], n + 1)
                    if g == 0:
                        dve.tensor_tensor(hsum[:, d, :], c, bank[5][:, :], ALU.mult).then_inc(S["xg_free"], 1)
                    else:
                        dve.tensor_tensor(b, c, bank[5][:, :], ALU.mult).then_inc(S["xg_free"], 1)
                        dve.wait_ge(S["xg_free"], n + 1)
                        dve.tensor_tensor(hsum[:, d, :], hsum[:, d, :], b, ALU.add)
                if n and n % NT == 0:
                    head_lo("o", 1, n // NT - 1)
                    head_lo("fo", 2, n // NT - 1)

            def gate_lo(g, cg):
                s = (GATE0 + cg) % 2
                dve.wait_ge(S["hi_ready"], g * CG + LOOP0 + cg + 1)
                lo(wl[:, s, :], raw[:, s, :], wh[:, s, :]).then_inc(S["split_ready"], 1)

            def gate_sum(g, cg):
                for m in range(2):
                    d = g * KC + (2 * cg + m)
                    dve.wait_ge(S["gate_mul"], d + (1 - KC))
                    dve.wait_ge(S["br_ps"], d + (BR0 + 1 - KC))
                    dve.tensor_tensor(gp[:, m, :], gs[:, m, :], bank[2 + m][:, :], ALU.mult).then_inc(S["gate_free"], 1)
                    dve.wait_ge(S["gate_free"], d + (3 - KC))
                    dve.tensor_tensor(hsum[:, 2 * cg + m, :], hsum[:, 2 * cg + m, :], gp[:, m, :], ALU.add).then_inc(S["h_add"], 1)

            dve.sem_inc(S["gate_free"], 2)
            with dve.Fori(1, NB - 1) as g:
                for cg in range(CG):
                    gate_lo(g, cg)
                    if cg >= 1:
                        gate_sum(g, cg - 1)
                gate_sum(g, CG - 1)
            for c in range(0, KC, 2):
                dve.wait_ge(S["h_hi"], c // 2 + 1)
                lo(xl[:, c:c + 2, :], hsum[:, c:c + 2, :], xh[:, c:c + 2, :]).then_inc(S["h_split"], 1)
            dve.sem_inc(S["e_split"], SC)
            for cg in range(CG):
                split_lo(OUT0 + cg, KC * UC)
                if cg >= 1:
                    residual(cg - 1)
            residual(CG - 1)
            dve.wait_ge(S["root2"], 1)
            st.link(dve.reciprocal(stat[:, 2, :], stat[:, 1, :]))
            dve.wait_ge(S["g_in"], 48)
            for t in range(NT):
                stt(xn2[:, t, :], x2[:, t, :], stat[:, 2, t:t + 1], gffn[:, :], ALU.mult, ALU.mult).then_inc(S["xn2_ready"], 1)
            for c in range(1, KC, 2):
                dve.wait_ge(S["xt2_ps"], c + 1)
                dve.tensor_copy(xt2[:, c, :], bank[4 + c % 4][:, :]).then_inc(S["xt2_b"], 1)
            dve.wait_ge(S["lg_ps"], 1)
            st.link(dve.tensor_copy(rl[:, :, :], bank[0][:, 0:NT * (NG + NE)].rearrange("p (t n) -> p t n", t=NT)))

            def first_max(src, n, top, eq, score, best, hot):
                st.link(dve.reduce_max(top, src, AX.X))
                st.link(dve.tensor_tensor(eq, src, top.unsqueeze(2).to_broadcast([P, NT, n]), ALU.is_equal))
                st.link(dve.tensor_tensor(score, eq, from_last[:, 0:n].unsqueeze(1).to_broadcast([P, NT, n]), ALU.mult))
                st.link(dve.reduce_max(best, score, AX.X))
                st.link(dve.tensor_tensor(hot, score, best.unsqueeze(2).to_broadcast([P, NT, n]), ALU.is_equal))

            gl, el = rl[:, :, 0:NG], rl[:, :, NG:]
            first_max(gl, NG, rs[:, 0, :], rg[:, 0, :, :], rg[:, 1, :, :], rs[:, 1, :], rg[:, 4, :, :])
            dve.tensor_tensor(rg[:, 2, :, :], gl, rs[:, 0, :].unsqueeze(2).to_broadcast([P, NT, NG]), ALU.subtract).then_inc(S["lg_d"], 1)
            st.link(dve.tensor_scalar(rg[:, 5, :, :], rg[:, 4, :, :], -1.0, -FAR, ALU.add, ALU.mult))
            for t in range(NT):
                st.mark(dve.tensor_tensor(re[:, 0, t, :].rearrange("p (g e) -> p g e", g=NG), el[:, t, :].rearrange("p (g e) -> p g e", g=NG),
                                          rg[:, 5, t, :].unsqueeze(2).to_broadcast([P, NG, EG]), ALU.add))
            st.done()
            first_max(re[:, 0, :, :], NE, rs[:, 2, :], re[:, 1, :, :], re[:, 2, :, :], rs[:, 1, :], ro[:, 0, :, :])
            st.link(stt(re[:, 3, :, :], ro[:, 0, :, :], 2 * FAR, re[:, 0, :, :], ALU.mult, ALU.add))
            first_max(re[:, 3, :, :], NE, rs[:, 3, :], re[:, 1, :, :], re[:, 2, :, :], rs[:, 1, :], ro[:, 1, :, :])
            dve.tensor_tensor(rs[:, 4, :], rs[:, 3, :], rs[:, 2, :], ALU.subtract).then_inc(S["lg_e"], 1)
            dve.tensor_tensor(rmask[:, :, :], ro[:, 0, :, :], ro[:, 1, :, :], ALU.add).then_inc(S["m_ready"], 1)
            dve.wait_ge(S["lg_act"], 1)
            st.link(dve.reduce_sum(rs[:, 6, :], rg[:, 3, :, :], AX.X))
            st.link(dve.reciprocal(rs[:, 7, :], rs[:, 6, :]))
            dve.wait_ge(S["lg_act"], 2)
            st.link(dve.tensor_scalar(rs[:, 8, :], rs[:, 5, :], 1.0, None, ALU.add))
            st.link(dve.reciprocal(rs[:, 9, :], rs[:, 8, :]))
            st.link(dve.tensor_tensor(cw[:, 0, :], rs[:, 9, :], rs[:, 7, :], ALU.mult))
            st.link(dve.tensor_tensor(cw[:, 1, :], cw[:, 0, :], rs[:, 5, :], ALU.mult))
            dve.wait_ge(S["rank_ps"], 1)
            st.link(stt(re[:, 0, :, :], bank[1][:, 0:NT * NE].rearrange("p (t e) -> p t e", e=NE), float(NE),
                        expert_i[:, :].unsqueeze(1).to_broadcast([P, NT, NE]), ALU.mult, ALU.add))
            for j in range(2):
                st.link(dve.tensor_tensor(re[:, 1 + j, :, :], re[:, 0, :, :], ro[:, j, :, :], ALU.mult))
                st.link(dve.reduce_sum(rposf[:, :, j:j + 1], re[:, 1 + j, :, :], AX.X))
            st.link(dve.reduce_max(rs[:, 10, 0:1], bank[1][:, NT * NE:(NT + 1) * NE], AX.X))
            st.link(dve.tensor_copy(flag[:, :], rs[:, 10, 0:1]))
            dve.tensor_copy(pos[:, :, :], rposf[:, :, :]).then_inc(S["pos_ready"], 1)
            dve.wait_ge(S["tab_r"], 16)
            dve.tensor_scalar(toks[:, :, :], slots[:, :, :], 1, None, ALU.arith_shift_right).then_inc(S["idx_ready"], 1)

            def half_lo(c, i, n):
                unit = n // 2
                dve.wait_ge(S["e_hi"], c * (HPE * NE) + i * (4 * HPE) + n + 1)
                lo(ewl[:, n % HS, :], eraw[:, unit % RS, (n % 2) * HU:(n % 2 + 1) * HU], ewh[:, n % HS, :]).then_inc(S["e_split"], 1)

            def x_lo(E):
                for b in range(2):
                    dve.wait_ge(S["xe_h"], E * 2 + b + 1)
                    lo(xgl[:, 4 * b:4 * b + 4, :], bank[b][:, :].rearrange("p (c s) -> p c s", s=P), xgh[:, 4 * b:4 * b + 4, :]).then_inc(S["xe_l"], 1)

            def start_pass(c):
                for n in range(4):
                    half_lo(c, 0, n)
                x_lo(c * NE)
                for n in range(4, 8):
                    half_lo(c, 0, n)
                x_lo(c * NE + 1)
                for n in range(8, 10):
                    half_lo(c, 0, n)

            def four(c, i, last=False):
                for q in range(4):
                    E = c * NE + i * 4 + q
                    n = 4 + HPE * (q + 1)
                    halves = range(n, n + (HPE if not last or q < 2 else 2 if q == 2 else 0))
                    dve.wait_ge(S["silu"], E + 1)
                    dve.tensor_tensor(hid[:, :], act_g[:, :], bank[2 + q % 2][:, FE:2 * FE], ALU.mult).then_inc(S["hid_r"], 1)
                    for k in halves[0:2]:
                        half_lo(c, i, k)
                    dve.wait_ge(S["ht_h"], E + 1)
                    lo(hidl[:, :, :], bank[4][:, 0:FE].rearrange("p (m s) -> p m s", s=P), hidh[:, :, :]).then_inc(S["ht_l"], 1)
                    for k in halves[2:4]:
                        half_lo(c, i, k)
                    if not (last and q >= 2):
                        x_lo(E + 2)
                    for k in halves[4:6]:
                        half_lo(c, i, k)

            start_pass(0)
            with dve.Fori(0, LOOPS - 1) as i:
                four(0, i)
            four(0, LOOPS - 1, last=True)
            most = dve.value_load(flag[0:1, 0:1], min_val=0, max_val=T)
            with dve.If(most > P):
                with dve.Fori(1, NT) as c:
                    start_pass(c)
                    with dve.Fori(0, LOOPS - 1) as i:
                        four(c, i)
                    four(c, LOOPS - 1, last=True)
            dve.wait_ge(S["g_in"], 48)
            for t in range(NT + 1):
                if t < NT:
                    dve.wait_ge(y_in[t], 16)
                    st.link(stt(x2[:, t, :], yt[:, t, 0, :], cw[:, 0, t:t + 1], x2[:, t, :], ALU.mult, ALU.add))
                    stt(x2[:, t, :], yt[:, t, 1, :], cw[:, 1, t:t + 1], x2[:, t, :], ALU.mult, ALU.add).then_inc(S["comb"], 1)
                if t >= 1:
                    u = t - 1
                    dve.wait_ge(S["root3"], t)
                    st.link(dve.reciprocal(stat[:, 2, u:u + 1], stat[:, 1, u:u + 1]))
                    stt(yt[:, u, 0, :], x2[:, u, :], stat[:, 2, u:u + 1], gfin[:, :], ALU.mult, ALU.mult).then_inc(S["fin"], 1)

        @block.tensor
        def _(pe):
            def passes(dst, pairs, start=True, stop=True):
                seq = []
                for lh, ll, rh, rlo in pairs:
                    seq += [(lh, rh), (lh, rlo), (ll, rh)]
                for n, (a, b) in enumerate(seq):
                    last = nc.tensor.matmul(dst, a, b, start=start and n == 0, stop=stop and n == len(seq) - 1)
                return last

            pe.wait_ge(S["consts"], 1)
            for c in range(KC):
                if c >= 4:
                    pe.wait_ge(S["xt_ready"], c - 3)
                for t in range(NT):
                    if c == 0:
                        pe.wait_ge(S["xn_ready"], t + 1)
                    last = nc.tensor.transpose(bank[c % 4][:, t * P:(t + 1) * P],
                                               xt[:, t, :].rearrange("p (n c) -> p c n", c=KC)[:, c, :], ident[:, :])
                last.then_inc(S["xt_psum"], 1)
            pe.wait_ge(S["small_in"], N_SMALL)
            for j in range(BJ):
                nc.tensor.transpose(bank[7][:, j * NROW:(j + 1) * NROW], rows[0:NROW, j * P:(j + 1) * P], ident[0:NROW, 0:NROW])
            nc.tensor.transpose(bank[7][:, P:P + NB * KC], gb_rows[0:NB * KC, :], ident[0:NB * KC, 0:NB * KC]).then_inc(S["tabs_psum"], 1)
            pe.wait_ge(S["tabs_ready"], 1)

            def cumulative(h, dst):
                for t in range(NT):
                    last = nc.tensor.matmul(dst[:, t * P:], fbc[:, h, t, :], causal[:, 0:T - t * P], start=t == 0, stop=t == NT - 1)
                last.then_inc(S["dc_psum"], 1)

            for u, (name, _, cols) in enumerate(PROJ):
                s = u % 2
                pe.wait_ge(S["split_ready"], u + 1)
                if u == 0:
                    pe.wait_ge(S["xt_ready"], KC)
                if u >= 2:
                    pe.wait_ge(proj_free[s], 2 * (u // 2))
                if name in ("fv", "sv"):
                    pe.wait_ge(proj_free[1 - s], 2 * ((u - 1) // 2 + 1))
                if name == "sv":
                    pe.wait_ge(S["ff_abs"], 1)
                wv = [w[:, s, 0:KC * cols].rearrange("p (c n) -> p c n", c=KC) for w in (wh, wl)]
                if name in ("sv", "fv"):
                    for t in range(NT):
                        tok = slice(t * P, (t + 1) * P)
                        dst = bank[4 + 2 * s + t // 2][:, (t % 2) * UC:(t % 2) * UC + cols] if name == "sv" else bank[4 + t][:, 0:cols]
                        last = passes(dst, [(xh[:, c, tok], xl[:, c, tok], wv[0][:, c, :], wv[1][:, c, :]) for c in range(KC)])
                else:
                    for j in range(BJ):
                        f = slice(j * P, (j + 1) * P)
                        last = passes(bank[4 + 2 * s + j][:, :], [(wv[0][:, c, f], wv[1][:, c, f], xh[:, c, :], xl[:, c, :]) for c in range(KC)])
                last.then_inc(S["unit_used"], 1)
                if name == "fq":
                    pe.wait_ge(S["ln_in"], 1)
                    for j in range(BJ):
                        last = nc.tensor.matmul(bank[0][:, :], avg[:, :], sg[:, j, :], start=j == 0, stop=j == BJ - 1)
                    last.then_inc(S["ln_mean"], 1)
                    pe.wait_ge(S["fbc_ready"], NH)
                    for h in range(NH - 1):
                        cumulative(h, bank[1 + h])
            pe.wait_ge(S["dc_out"], 1)
            cumulative(NH - 1, bank[1])
            pe.wait_ge(S["dc_out"], 2)
            for t in range(NT):
                for t2 in range(t + 1):
                    last = nc.tensor.matmul(bank[2][:, t * NH:(t + 1) * NH], causal[:, 0:P] if t2 == t else causal[:, P:2 * P],
                                            ff[:, 3, t2, :], start=t2 == 0, stop=t2 == t)
            last.then_inc(S["dq_psum"], 1)
            pe.wait_ge(S["ln_sq"], BJ)
            for j in range(BJ):
                last = nc.tensor.matmul(bank[0][:, :], avg[:, :], axb[:, j, :], start=j == 0, stop=j == BJ - 1)
            last.then_inc(S["ln_var"], 1)
            for name in ("sq", "sk", "sv", "fq", "fk", "fv"):
                evacuated(pe, name)
            def x_products():
                for n in range(STEPS):
                    g, d = x_tile(n)
                    s = (GATE0 + n // 2) % 2
                    f = slice(n % 2 * P, (n % 2 + 1) * P)
                    gate_w = [w[:, s, 0:KC * UC].rearrange("p (c n) -> p c n", c=KC) for w in (wh, wl)]
                    br_w = [w[:, s, KC * UC:UNIT].rearrange("p (c n) -> p c n", c=BJ) for w in (wh, wl)]
                    pe.wait_ge(S["split_ready"], GATE0 + n // 2 + 1)
                    if n >= 2:
                        pe.wait_ge(S["xg_neg"], n - 1)
                    for c in range(KC):
                        for q, (a, b) in enumerate(((gate_w[0], xh), (gate_w[0], xl), (gate_w[1], xh))):
                            last = nc.tensor.matmul(bank[6 + n % 2][:, :], a[:, c, f], b[:, c, :], start=c == 0 and q == 0, stop=c == KC - 1 and q == 2)
                            if c == KC - 1 and q == 2:
                                last.then_inc(S["xg_ps"], 1)
                            yield
                    if n:
                        pe.wait_ge(S["xg_free"], n)
                    if n == KC:
                        pe.wait_ge(S["y_ready"], 1)
                    for j in range(BJ):
                        for q, (a, b) in enumerate(((br_w[0], yh), (br_w[0], yl), (br_w[1], yh))):
                            last = nc.tensor.matmul(bank[5][:, :], a[:, j, f], b[:, g, j, :], start=j == 0 and q == 0, stop=j == BJ - 1 and q == 2)
                            if j == BJ - 1 and q == 2:
                                last.then_inc(S["xb_ps"], 1)
                            yield

            products = x_products()
            PER_TILE = 3 * (KC + BJ)

            def gates(count):
                for _ in range(count):
                    next(products, None)

            gates(PER_TILE)
            pe.wait_ge(S["dc_out"], NH)
            pe.wait_ge(S["dq_out"], 1)
            pe.wait_ge(S["ln_root"], 1)
            for n in range(STEPS + 1):
                if n < STEPS:
                    h, kt, q0 = stick_step(n)
                    j, r = head_rows(h)
                    if n >= 1:
                        pe.wait_ge(S["w_exp"], n)
                    nc.tensor.matmul(bank[0][:, q0:], k_s[r:r + HD, j, kt * P:(kt + 1) * P], q_s[r:r + HD, j, q0:],
                                     start=True, stop=True).then_inc(S["z_psum"], 1)
                    h, qt, m = fox_step(n)
                    if n >= 1:
                        pe.wait_ge(S["l_max"], n)
                    nc.tensor.matmul(bank[1][:, 0:m], q_f[r:r + HD, j, qt * P:(qt + 1) * P], k_f[r:r + HD, j, 0:m], start=True, stop=True)
                    nc.tensor.matmul(bank[1][:, m - P:m], identb[:, :], maskb[:, :], start=False, stop=True,
                                     skip_group_check=True).then_inc(S["l_psum"], 1)
                    gates(PER_TILE // 3)
                if n >= 1:
                    h, kt, q0 = stick_step(n - 1)
                    j, r = head_rows(h)
                    pe.wait_ge(S["w_mask"], n)
                    if kt == NT - 1 and h:
                        pe.wait_ge(S["o_split"], h)
                    nc.tensor.matmul(bank[3][:, q0:], sv[:, kt, j * P:(j + 1) * P], wts[:, q0:],
                                     start=kt == NT - 1, stop=kt == 0, skip_group_check=True).then_inc(S["wv_done"], 1)
                    h, qt, m = fox_step(n - 1)
                    pe.wait_ge(S["pt_out"], n)
                    if qt == 0 and h:
                        pe.wait_ge(S["fo_split"], h)
                    for kt in range(qt + 1):
                        last = nc.tensor.matmul(bank[4][:, qt * P:(qt + 1) * P], fv[:, kt, j * P:(j + 1) * P], pt[:, kt, :],
                                                start=kt == 0, stop=kt == qt)
                    last.then_inc(S["fo_psum"], 1)
                if n < STEPS:
                    gates(PER_TILE // 3)
                    h, kt, q0 = stick_step(n)
                    pe.wait_ge(S["sp_mask"], n + 1)
                    last = nc.tensor.matmul(bank[0][:, q0:], neg_tri[:, :], sp[:, kt, q0:], start=False, stop=True, skip_group_check=True)
                    for k2 in range(kt + 1, NT):
                        last = nc.tensor.matmul(bank[0][:, k2 * P:], neg_one[:, :], sp[:, k2, k2 * P:], start=False, stop=True, skip_group_check=True)
                    last.then_inc(S["acc_done"], 1)
                    h, qt, m = fox_step(n)
                    pe.wait_ge(S["l_norm"], n + 1)
                    for kt in range(qt + 1):
                        last = nc.tensor.transpose(bank[2][:, kt * P:(kt + 1) * P], lg[:, kt * P:(kt + 1) * P], ident[:, :])
                    last.then_inc(S["pt_psum"], 1)
                    gates(PER_TILE // 3)
            pe.wait_ge(S["xg_free"], STEPS)
            pe.wait_ge(S["fo_split"], NH)
            pe.wait_ge(S["o_split"], NH)

            yh_f = yh[:, :, :, :].rearrange("p g j t -> p (g j t)")
            yl_f = yl[:, :, :, :].rearrange("p g j t -> p (g j t)")
            pe.sem_inc(S["br_ps"], BR0)
            with pe.Fori(1, NB - 1) as g:
                for cg in range(CG):
                    s = (GATE0 + cg) % 2
                    pe.wait_ge(S["split_ready"], g * CG + LOOP0 + cg + 1)
                    gate_w = [w[:, s, 0:KC * UC].rearrange("p (c n) -> p c n", c=KC) for w in (wh, wl)]
                    br_w = [w[:, s, KC * UC:UNIT].rearrange("p (c n) -> p c n", c=BJ) for w in (wh, wl)]
                    for m in range(2):
                        d = g * KC + (2 * cg + m)
                        f = slice(m * P, (m + 1) * P)
                        pe.wait_ge(S["gate_free"], d + (1 - KC))
                        passes(bank[m][:, :], [(gate_w[0][:, c, f], gate_w[1][:, c, f], xh[:, c, :], xl[:, c, :])
                                               for c in range(KC)]).then_inc(S["gate_ps"], 1)
                        last = passes(bank[2 + m][:, :], [(br_w[0][:, j, f], br_w[1][:, j, f],
                                                           yh_f[:, bass.ds(g * (BJ * T) + j * T, T)],
                                                           yl_f[:, bass.ds(g * (BJ * T) + j * T, T)]) for j in range(BJ)])
                        last.then_inc(S["br_ps"], 1)

            pe.wait_ge(S["h_split"], KC // 2)
            for cg in range(CG):
                u = OUT0 + cg
                s = u % 2
                pe.wait_ge(S["split_ready"], u + 1)
                if cg >= 2:
                    pe.wait_ge(S["x2_ready"], 2 * (cg - 1))
                wv = [w[:, s, 0:KC * UC].rearrange("p (c n) -> p c n", c=KC) for w in (wh, wl)]
                for t in range(NT):
                    tok = slice(t * P, (t + 1) * P)
                    last = passes(bank[2 * (cg % 2) + t // 2][:, (t % 2) * UC:(t % 2 + 1) * UC],
                                  [(xh[:, c, tok], xl[:, c, tok], wv[0][:, c, :], wv[1][:, c, :]) for c in range(KC)])
                    if t % 2:
                        last.then_inc(S["out_ps"], 1)
            pe.sem_inc(S["e_used"], HS)

            for c in range(KC):
                if c >= 4:
                    pe.wait_ge(S["xt2_a"], (c - 4) // 2 + 1)
                    if c > 4:
                        pe.wait_ge(S["xt2_b"], (c - 3) // 2)
                for t in range(NT):
                    if c == 0:
                        pe.wait_ge(S["xn2_ready"], t + 1)
                    last = nc.tensor.transpose(bank[4 + c % 4][:, t * P:(t + 1) * P],
                                               xn2[:, t, :].rearrange("p (n c) -> p c n", c=KC)[:, c, :], ident[:, :])
                last.then_inc(S["xt2_ps"], 1)
            pe.wait_ge(S["wr_in"], 32)
            pe.wait_ge(S["xt2_a"], KC // 2)
            pe.wait_ge(S["xt2_b"], KC // 2)
            pe.wait_ge(S["x2_ready"], 2 * CG)
            NR = NG + NE
            for t in range(NT):
                for c in range(KC):
                    last = nc.tensor.matmul(bank[0][:, t * NR:(t + 1) * NR], xt2[:, c, t * P:(t + 1) * P], wr[:, c, :], start=c == 0, stop=c == KC - 1)
            last.then_inc(S["lg_ps"], 1)
            pe.wait_ge(S["m_ready"], 1)
            for t in range(NT):
                for t2 in range(t + 1):
                    nc.tensor.matmul(bank[1][:, t * NE:(t + 1) * NE], strictb[:, :] if t2 == t else oneb[:, :], rmask[:, t2, :], start=t2 == 0, stop=t2 == t)
            for t in range(NT):
                last = nc.tensor.matmul(bank[1][:, NT * NE:(NT + 1) * NE], oneb[:, :], rmask[:, t, :], start=t == 0, stop=t == NT - 1)
            last.then_inc(S["rank_ps"], 1)
            pe.wait_ge(S["idx_ready"], 1)

            def x_transposes(c, i, q):
                pe.wait_ge(g_full[q % XG], (c * (NE // XG) + i * (4 // XG) + q // XG + 1) * 16)
                for k in range(KC):
                    last = nc.tensor.transpose(bank[k // 4][:, (k % 4) * P:(k % 4 + 1) * P],
                                               xg[:, q % XG, :].rearrange("p (n c) -> p c n", c=KC)[:, k, :], ident[:, :])
                    if k % 4 == 3:
                        last.then_inc(S["xt_ps"], 1)

            def product(c, i, n, q, col):
                for half in range(2):
                    pe.wait_ge(S["e_split"], c * (HPE * NE) + i * (4 * HPE) + (n + half + SC + 1))
                    wv = [w[:, (n + half) % HS, :].rearrange("p (c f) -> p c f", f=FE) for w in (ewh, ewl)]
                    passes(bank[2 + q % 2][:, col:col + FE],
                           [(xgh[:, 4 * half + k, :], xgl[:, 4 * half + k, :], wv[0][:, k, :], wv[1][:, k, :]) for k in range(4)],
                           start=half == 0, stop=half == 1).then_inc(S["e_used"], 1)

            def start_pass(c):
                x_transposes(c, 0, 0)
                pe.wait_ge(S["xe_l"], c * (2 * NE) + 2)
                if not isinstance(c, int):
                    pe.wait_ge(S["hid_r"], c * NE)
                product(c, 0, 0, 0, 0)
                product(c, 0, 2, 0, FE)
                x_transposes(c, 0, 1)

            def four(c, i, last=False):
                for q in range(4):
                    E = c * NE + i * 4 + q
                    n = 4 + HPE * q
                    ahead = not (last and q == 3)
                    if ahead:
                        pe.wait_ge(S["xe_l"], E * 2 + 4)
                        product(c, i, n, q + 1, 0)
                    pe.wait_ge(S["hid_r"], E + 1)
                    for m in range(FE // P):
                        ins = nc.tensor.transpose(bank[4][:, m * P:(m + 1) * P], hid[:, :].rearrange("p (n m) -> p m n", m=FE // P)[:, m, :], ident[:, :])
                    ins.then_inc(S["ht_ps"], 1)
                    if ahead:
                        product(c, i, n + 2, q + 1, FE)
                    if not (last and q >= 2):
                        x_transposes(c, i, q + 2)
                    pe.wait_ge(S["ht_l"], E + 1)
                    pe.wait_ge(S["y_out"], E * 2 + 2)
                    d = n + 4 if ahead else n
                    for m in range(FE // P):
                        pe.wait_ge(S["e_split"], c * (HPE * NE) + i * (4 * HPE) + (d + m + SC + 1))
                        for b in range(2):
                            ins = passes(bank[5 + b][:, :], [(hidh[:, m, :], hidl[:, m, :], ewh[:, (d + m) % HS, b * T:(b + 1) * T],
                                                              ewl[:, (d + m) % HS, b * T:(b + 1) * T])], start=m == 0, stop=m == FE // P - 1)
                        ins.then_inc(S["e_used"], 1)

            start_pass(0)
            with pe.Fori(0, LOOPS - 1) as i:
                four(0, i)
            four(0, LOOPS - 1, last=True)
            most = pe.value_load(flag[0:1, 0:1], min_val=0, max_val=T)
            with pe.If(most > P):
                with pe.Fori(1, NT) as c:
                    start_pass(c)
                    with pe.Fori(0, LOOPS - 1) as i:
                        four(c, i)
                    four(c, LOOPS - 1, last=True)


_INS = ["x", "mix_norm_g", "w_in", "b_forget", "conv_a_w", "conf_dw_w", "conf_dw_b", "conf_ln_g", "conf_ln_b",
        "w_branch", "w_gate", "b_gate", "w_out", "ffn_norm_g", "w_router_group", "w_router_expert",
        "w_expert_gate", "w_expert_up", "w_expert_down", "final_norm_g"]


def kernel(**inputs):
    import concourse.bacc as _bacc
    from concourse.bass_utils import run_bass_kernel_spmd as _run

    nc = _bacc.Bacc("TRN2", target_bir_lowering=False, num_devices=1)
    arrays, args = {}, []
    for name in _INS:
        a = np.ascontiguousarray(inputs[name])
        arrays[f"in_{name}"] = a
        args.append(nc.dram_tensor(f"in_{name}", a.shape, mybir.dt.from_np(a.dtype), kind="ExternalInput").ap())
    shape = inputs["x"].shape
    args.append(nc.dram_tensor("out_0", shape, F32, kind="ExternalOutput").ap())
    hybrid_trunk(nc, *args)
    r = _run(nc, [arrays], core_ids=[0])
    return r.results[0]["out_0"]
```

```python
from contextlib import ExitStack

import numpy as np

import concourse.bass as bass
from concourse import mybir
from concourse.alu_op_type import AluOpType as ALU

ACT = mybir.ActivationFunctionType
AX = mybir.AxisListType
F32 = mybir.dt.float32
F32R = mybir.dt.float32r
BF16 = mybir.dt.bfloat16
I32 = mybir.dt.int32


class Steps:

    def __init__(self, eng, sem):
        self.eng, self.sem, self.n = eng, sem, 0

    def mark(self, ins):
        ins.then_inc(self.sem, 1)
        self.n += 1
        return self.n

    def done(self, n=None):
        self.eng.wait_ge(self.sem, self.n if n is None else n)

    def link(self, ins):
        self.mark(ins)
        self.done()


def hybrid_trunk(nc, x, mix_norm_g, w_in, b_forget, conv_a_w, conf_dw_w, conf_dw_b, conf_ln_g,
                 conf_ln_b, w_branch, w_gate, b_gate, w_out, ffn_norm_g, w_router_group,
                 w_router_expert, w_expert_gate, w_expert_up, w_expert_down, final_norm_g, out):
    P = 128
    T, D = x.shape[1], x.shape[2]
    NT = T // P
    KC = D // P
    NB = w_branch.shape[1]
    BW = w_branch.shape[2]
    BJ = BW // P
    NH = b_forget.shape[1]
    HD = BW // NH
    NE = w_expert_gate.shape[1]
    NG = w_router_group.shape[2]
    EG = NE // NG
    FE = w_expert_gate.shape[3]
    CA_W, CF_W = conv_a_w.shape[1], conf_dw_w.shape[1]
    EPS = 1e-6
    SCALE = HD ** -0.5
    MASKED = -float(2 ** 100)
    FAR = -1e30

    COL_AX, COL_AB, COL_AC = 0, BW, 2 * BW
    COL_SQ, COL_SK, COL_SV = 3 * BW, 4 * BW, 5 * BW
    COL_FQ, COL_FK, COL_FV = 6 * BW, 7 * BW, 8 * BW
    COL_U = 9 * BW + NH
    COL_UG = COL_U + BW
    UC = 256
    PROJ = [("u", COL_U, UC), ("ug", COL_UG, UC), ("ax", COL_AX, UC), ("ac", COL_AC, UC),
            ("ab", COL_AB, UC), ("fv", COL_FV, UC + NH), ("sv", COL_SV, UC), ("sq", COL_SQ, UC),
            ("sk", COL_SK, UC), ("fq", COL_FQ, UC), ("fk", COL_FK, UC)]
    NP = len(PROJ)
    CG = D // UC
    GATE0 = NP
    OUT0 = NP + NB * CG
    NMIX = OUT0 + CG
    UNIT = KC * UC + BJ * UC

    x_v = x[0].rearrange("(t p) d -> t p d", p=P)
    out_v = out[0].rearrange("(t p) d -> t p d", p=P)
    w_in_v = w_in[0].rearrange("(p c) n -> p c n", c=KC)
    w_gate_v = w_gate[0].rearrange("g (p c) n -> g p c n", c=KC)
    w_branch_v = w_branch[0].rearrange("g (j p) n -> g p j n", p=P)
    w_out_v = w_out[0].rearrange("(c p) n -> p c n", p=P)
    eg_v = w_expert_gate[0].rearrange("e (p c) f -> e p (c f)", c=KC)
    eu_v = w_expert_up[0].rearrange("e (p c) f -> e p (c f)", c=KC)
    ed_v = w_expert_down[0].rearrange("e (p m) n -> e p (m n)", m=FE // P)
    xn_dram = nc.dram_tensor("xn_dram", (T, D), F32, kind="Internal").ap()
    y_dram = nc.dram_tensor("y_dram", (2 * T, D), F32, kind="Internal").ap()

    main = ExitStack()
    with main:
        def region():
            return ExitStack()

        def sb(ctx, name, shape, dt=F32):
            return ctx.enter_context(nc.sbuf_tensor(name, [P] + list(shape), dt))

        def sem(name):
            return main.enter_context(nc.semaphore(name))

        ident = sb(main, "ident", [P])
        identb = sb(main, "identb", [P], BF16)
        causal = sb(main, "causal", [T])
        neg_tri = sb(main, "neg_tri", [P])
        neg_one = sb(main, "neg_one", [P])
        avg = sb(main, "avg", [P])
        maskb = sb(main, "maskb", [P], BF16)
        strictb = sb(main, "strictb", [P], BF16)
        oneb = sb(main, "oneb", [P], BF16)
        eps = sb(main, "eps", [1])
        stat = sb(main, "stat", [3, NT])
        gmix = sb(main, "gmix", [KC])
        NROW = CA_W + CF_W + 3
        ch = sb(main, "ch", [BJ, NROW])
        bg = sb(main, "bg", [NB * KC])
        bf = sb(main, "bf", [NH])
        from_last = sb(main, "from_last", [NE])
        UNUSED = 2 * T
        row_no = sb(main, "row_no", [NT, 2])
        slot_no = sb(main, "slot_no", [P])
        wr = sb(main, "wr", [KC, NG + NE])
        gffn_t = sb(main, "gffn_t", [KC])
        sq_part = sb(main, "sq_part", [NT, CG])
        sq_junk = sb(main, "sq_junk", [NT, UC], BF16)
        cw = sb(main, "cw", [2, NT])
        slots = sb(main, "slots", [NE], I32)
        toks = sb(main, "toks", [NE], I32)
        flag = sb(main, "flag", [1], I32)
        gather_i = sb(main, "gather_i", [4, 1], I32)
        scatter_i = sb(main, "scatter_i", [2, 1], I32)

        bg_neg = sb(main, "bg_neg", [NB * KC])
        ff = sb(main, "ff", [4, NT, NH])
        dq = sb(main, "dq", [NT, NH])
        small = sb(main, "small", [2, 5])
        mix = region()
        yh = sb(mix, "yh", [NB, BJ, T], F32R)
        yl = sb(mix, "yl", [NB, BJ, T], F32R)
        first = region()
        junk = sb(first, "junk", [D])
        first.close()
        sv = sb(mix, "sv", [NT, BW])
        fv = sb(mix, "fv", [NT, BW])
        conv = region()
        cu = sb(conv, "cu", [BJ, CF_W - 1 + T])
        ca = sb(conv, "ca", [BJ, CA_W - 1 + T])
        ab = sb(conv, "ab", [BJ, T])
        sg = sb(conv, "sg", [BJ, T])
        axb = sb(conv, "axb", [BJ, T])
        rows = sb(conv, "rows", [BW])
        gb_rows = sb(conv, "gb_rows", [P])
        conv.close()
        dcum = sb(mix, "dcum", [NH, T])
        sp = sb(mix, "sp", [NT, T])
        wts = sb(mix, "wts", [T])
        tmp = sb(mix, "tmp", [T])
        lg = sb(mix, "lg", [T])
        pt = sb(mix, "pt", [NT, P])
        gated = region()
        fbc = sb(gated, "fbc", [NH, NT, P])
        gated.close()
        gs = sb(mix, "gs", [2, T])
        gp = sb(mix, "gp", [2, T])
        a1 = region()
        xt = sb(a1, "xt", [NT, D])
        a1.close()
        q_s = sb(mix, "q_s", [BJ, T])
        k_s = sb(mix, "k_s", [BJ, T])
        q_f = sb(mix, "q_f", [BJ, T])
        k_f = sb(mix, "k_f", [BJ, T])
        hsum = sb(mix, "hsum", [KC, T])
        xh = sb(mix, "xh", [KC, T], F32R)
        xl = sb(mix, "xl", [KC, T], F32R)
        raw = sb(mix, "raw", [2, UNIT])
        wh = sb(mix, "wh", [2, UNIT], F32R)
        wl = sb(mix, "wl", [2, UNIT], F32R)
        mix.close()

        moe = region()
        HU = KC * FE // 2
        HS = 8
        ewh = [sb(moe, f"ewh{n}", [HU], F32R) for n in range(HS // 2)]
        ewl = [sb(moe, f"ewl{n}", [HU], F32R) for n in range(HS // 2)]
        x2 = sb(moe, "x2", [NT, D])
        RS = 6
        routing = region()
        xt2 = sb(routing, "xt2", [KC, T])
        routing.close()
        XG = 4
        xg = sb(moe, "xg", [XG, D])
        eraw = sb(moe, "eraw", [RS, 2 * HU])
        gffn = sb(moe, "gffn", [D])
        xn2 = sb(moe, "xn2", [NT, D])
        rl = sb(moe, "rl", [NT, NG + NE])
        rg = sb(moe, "rg", [6, NT, NG])
        re = sb(moe, "re", [4, NT, NE])
        ro = sb(moe, "ro", [2, NT, NE])
        rv = sb(moe, "rv", [NT, 2, NE], F32R)
        rs = sb(moe, "rs", [14, NT])
        rank = sb(moe, "rank", [NT, 2])
        rmask = sb(moe, "rmask", [NT, NE], BF16)
        gfin = sb(moe, "gfin", [D])
        ewh += [sb(moe, f"ewh{n}", [HU], F32R) for n in range(HS // 2, HS)]
        ewl += [sb(moe, f"ewl{n}", [HU], F32R) for n in range(HS // 2, HS)]
        hot_in = region()
        hot = sb(hot_in, "hot", [NT, 2, P], F32R)
        hot_in.close()
        xgh = sb(moe, "xgh", [KC, P], F32R)
        xgl = sb(moe, "xgl", [KC, P], F32R)
        act_g = sb(moe, "act_g", [FE])
        hid = sb(moe, "hid", [FE])
        hidh = sb(moe, "hidh", [FE // P, P], F32R)
        hidl = sb(moe, "hidl", [FE // P, P], F32R)
        ye = sb(moe, "ye", [2, D])
        moe.close()
        yt = eraw[:, :, :].rearrange("p s n -> p (s n)")[:, 0:2 * NT * D].rearrange("p (t j n) -> p t j n", t=NT, j=2)

        bank = [main.enter_context(nc.psum_tensor(f"bank{i}", [P, T], F32)) for i in range(8)]

        S = {name: sem(name) for name in (
            "pool_step act_step dve_step consts small_in tabs_ready x0 x1 x2s x3 sq_done root xn_ready "
            "xt_psum xt_hi xt_ready raw0 raw1 br0 br1 hi_ready split_ready unit_used "
            "tabs_psum free_p0 free_p1 "
            "ln_in ln_mean ln_cent ln_sq ln_var ln_root ln_norm ln_act y_ready bf_in ff_sum ff_abs ff_ln ff_ready "
            "fbc_ready dc_psum dc_out dq_psum dq_out "
            "z_psum sp_min sp_ln sp_max sp_mask acc_done w_exp w_mask o_hi o_split wv_done "
            "l_psum l_max l_bias l_exp l_norm pt_psum pt_out fo_psum fo_hi fo_split "
            "hi_part xg_ps xg_neg xg_min xg_ln xg_max xg_exp xb_ps xg_free gate_ps br_ps gate_free gate_mul h_add h_hi h_split out_ps x2_in x2_ready "
            "g_in wr_in sq2 root2 xn2_ready xn_out xt2_ps xt2_a xt2_b lg_ps sq2_sum recip2 gffn_in gfin_in wr_ready slots_in flag_ready lg_act lg_d lg_e m_ready rank_ps "
            "hot_ready slot_ps idx_ready xn2_scaled rank_ready turns gather_col scatter_col gf0 gf1 gf2 gf3 xt_ps xe_h xe_l silu hid_r "
            "ht_ps ht_h ht_l y_out ye_free sc0 sc1 er0 er1 er2 er3 er4 er5 e_hi e_split e_used "
            "yp0 yp1 yp2 yp3 yq0 yq1 yq2 yq3 fin_scaled recip3 fin_last comb sq3 root3 fin out_done").split()}
        x_in = [S["x0"], S["x1"], S["x2s"], S["x3"]]
        raw_full, br_full = [S["raw0"], S["raw1"]], [S["br0"], S["br1"]]
        proj_free = [S["free_p0"], S["free_p1"]]
        eraw_full = [S[f"er{n}"] for n in range(RS)]
        g_full, scattered = [S[f"gf{n}"] for n in range(XG)], [S["sc0"], S["sc1"]]
        y_in = [[S[f"y{k}{n}"] for k in "pq"] for n in range(NT)]
        N_SMALL = 16 * 7

        UNIT_OF = {name: n for n, (name, _, _) in enumerate(PROJ)}

        def evacuated(eng, name):
            n = UNIT_OF[name]
            eng.wait_ge(proj_free[n % 2], 2 * (n // 2 + 1))

        STEPS = NH * NT
        NX = 2 * CG
        LOOP0 = GATE0 + NX - CG
        CAP = 40.0

        def x_unit(k):
            return (0, NB - 1)[k // CG], k % CG

        def stick_step(n):
            h, kt = n // NT, NT - 1 - n % NT
            return h, kt, kt * P

        def fox_step(n):
            return n // NT, n % NT, (n % NT + 1) * P

        def x_tile(n):
            g, cg = x_unit(n // 2)
            return g, 2 * cg + n % 2

        def head_rows(h):
            per = P // HD
            return h // per, (h % per) * HD

        BR0 = 4
        LOOPS = NE // 4
        SC = 2 * RS
        HPE = 6
        UPE = 3
        POOL_TILES = NT // 2
        EARLY = HS // 2
        block = main.enter_context(nc.Block())

        @block.sync
        def _(sp_e):
            for t in range(NT):
                sp_e.dma_start(xt[:, t, :], x_v[t]).then_inc(x_in[t], 16)
            sp_e.dma_start(gmix[:, :], mix_norm_g[0].rearrange("(p c) -> p c", c=KC)).then_inc(S["g_in"], 16)
            r = 0
            for src, n in ((conv_a_w[0], CA_W), (conf_dw_w[0], CF_W), (conf_dw_b, 1), (conf_ln_g, 1), (conf_ln_b, 1)):
                sp_e.dma_start(rows[r:r + n, :], src).then_inc(S["small_in"], 16)
                r += n
            sp_e.dma_start(gb_rows[0:NB * KC, :], b_gate[0].rearrange("g (c p) -> (g c) p", p=P)).then_inc(S["small_in"], 16)
            sp_e.dma_start(gb_rows[NB * KC:(NB + 1) * KC, :], ffn_norm_g[0].rearrange("(c p) -> c p", p=P)).then_inc(S["small_in"], 16)
            sp_e.dma_start(bf[:, :], b_forget.to_broadcast([P, NH])).then_inc(S["bf_in"], 16)

            def load_unit(u, src_main, src_branch=None, cols=UC):
                s = u % 2
                if u >= 2:
                    sp_e.wait_ge(S["split_ready"], u - 1)
                sp_e.dma_start(raw[:, s, 0:KC * cols].rearrange("p (c n) -> p c n", c=KC), src_main).then_inc(raw_full[s], 16)

            for u, (_, col, cols) in enumerate(PROJ):
                load_unit(u, w_in_v[:, :, col:col + cols], cols=cols)
            sp_e.dma_start(wr[:, :, 0:NG], w_router_group[0].rearrange("(c p) n -> p c n", p=P)).then_inc(S["wr_in"], 16)
            sp_e.dma_start(wr[:, :, NG:], w_router_expert[0].rearrange("(c p) g n -> p c (g n)", p=P)).then_inc(S["wr_in"], 16)
            for k in range(NX):
                g, cg = x_unit(k)
                s = (GATE0 + k) % 2
                load_unit(GATE0 + k, w_gate_v[g, :, :, cg * UC:(cg + 1) * UC])
                sp_e.dma_start(raw[:, s, KC * UC:UNIT].rearrange("p (j n) -> p j n", j=BJ),
                               w_branch_v[g, :, :, cg * UC:(cg + 1) * UC]).then_inc(br_full[s], 16)
            with sp_e.Fori(1, NB - 1) as g:
                for cg in range(CG):
                    s = (GATE0 + cg) % 2
                    sp_e.wait_ge(S["split_ready"], g * CG + LOOP0 + cg - 1)
                    sp_e.dma_start(raw[:, s, 0:KC * UC].rearrange("p (c n) -> p c n", c=KC),
                                   w_gate_v[bass.ds(g, 1), :, :, cg * UC:(cg + 1) * UC].rearrange("o p c n -> (o p) c n")).then_inc(raw_full[s], 16)
                    sp_e.dma_start(raw[:, s, KC * UC:UNIT].rearrange("p (j n) -> p j n", j=BJ),
                                   w_branch_v[bass.ds(g, 1), :, :, cg * UC:(cg + 1) * UC].rearrange("o p j n -> (o p) j n")).then_inc(br_full[s], 16)
            for t in range(NT):
                sp_e.dma_start(x2[:, t, :], x_v[t]).then_inc(S["x2_in"], 16)
            s = OUT0 % 2
            sp_e.wait_ge(S["split_ready"], OUT0 - 1)
            halves = (raw_full[s], br_full[s])
            for n in range(2):
                c = slice(n * KC // 2, (n + 1) * KC // 2)
                sp_e.dma_start(raw[:, s, n * KC // 2 * UC:(n + 1) * KC // 2 * UC].rearrange("p (c n) -> p c n", c=KC // 2),
                               w_out_v[:, c, 0:UC]).then_inc(halves[n], 16)
            for cg in range(1, CG):
                load_unit(OUT0 + cg, w_out_v[:, :, cg * UC:(cg + 1) * UC])
            sp_e.wait_ge(S["h_split"], KC)

            def load_expert(w, k, e, slot):
                sp_e.wait_ge(S["e_split"], 2 * w + 2)
                src = (eg_v, eu_v, ed_v)[k]
                view = src[bass.ds(e, 1)].rearrange("o p n -> (o p) n") if not isinstance(e, int) else src[e]
                sp_e.dma_start(eraw[:, slot, :], view).then_inc(eraw_full[slot], 16)

            def load_step(c, i, q, k):
                w = 2 + UPE * q + k
                load_expert(c * (UPE * NE) + i * (4 * UPE) + w, k, i * 4 + q + (k < 2), w % RS)

            def load_last(c):
                q = 3
                w = 2 + UPE * q
                load_expert(c * (UPE * NE) + (LOOPS - 1) * (4 * UPE) + w, 2, NE - 1, w % RS)

            def load_four(c, i, skip=0, last=False):
                for n in range(skip, 4 * UPE):
                    if not (last and n >= 3 * UPE):
                        load_step(c, i, n // UPE, n % UPE)
                if last:
                    load_last(c)

            for k in range(2):
                load_expert(k, k, 0, k)
            AHEAD = RS - 1
            for n in range(AHEAD - 2):
                load_step(0, 0, n // UPE, n % UPE)
            for n in range(AHEAD - 1, AHEAD + 1):
                load_step(0, 0, n // UPE, n % UPE)
            sp_e.wait_ge(S["out_ps"], 2 * CG)
            sp_e.dma_start(gffn[:, :], ffn_norm_g.to_broadcast([P, D])).then_inc(S["gffn_in"], 16)
            load_step(0, 0, (AHEAD - 2) // UPE, (AHEAD - 2) % UPE)
            sp_e.dma_start(gfin[:, :], final_norm_g.rearrange("(o d) -> o d", o=1).to_broadcast([P, D])).then_inc(S["gfin_in"], 16)
            for t in range(NT):
                sp_e.wait_ge(S["xn2_ready"], t + 1)
                sp_e.dma_start(xn_dram[t * P:(t + 1) * P, :], xn2[:, t, :]).then_inc(S["xn_out"], 16)
            load_four(0, 0, AHEAD + 1)
            with sp_e.Fori(1, LOOPS - 1) as i:
                load_four(0, i)
            load_four(0, LOOPS - 1, last=True)
            sp_e.wait_ge(S["flag_ready"], 1)
            most = sp_e.value_load(flag[0:1, 0:1], min_val=0, max_val=T)
            with sp_e.If(most > P):
                with sp_e.Fori(1, NT) as c:
                    for k in range(2):
                        load_expert(c * (UPE * NE) + k, k, 0, k)
                    with sp_e.Fori(0, LOOPS - 1) as i:
                        load_four(c, i)
                    load_four(c, LOOPS - 1, last=True)
                for s in range(2):
                    sp_e.wait_ge(scattered[s], 16 * NE // 2 * NT)
            for s in range(2):
                sp_e.wait_ge(scattered[s], 16 * NE // 2)
            y_v = y_dram.rearrange("(t p j) d -> t p j d", p=P, j=2)
            for t in range(NT):
                for j in range(2):
                    sp_e.dma_start(yt[:, t, j, :], y_v[t, :, j, :]).then_inc(y_in[t][j], 16)
            for t in range(NT):
                if t < POOL_TILES:
                    sp_e.wait_ge(S["fin"], t + 1)
                else:
                    sp_e.wait_ge(S["fin_last"], t + 1 - POOL_TILES)
                sp_e.dma_start(out_v[t], yt[:, t, 0, :]).then_inc(S["out_done"], 16)
            sp_e.wait_ge(S["out_done"], 16 * NT)

        @block.gpsimd
        def _(pool):
            st = Steps(pool, S["pool_step"])

            def select(t, cols, op, fill_v, base, step, mult, view=None):
                ap = t[:, 0:cols] if view is None else view
                return pool.affine_select(out=ap, in_=ap, compare_op=op, fill=fill_v, base=base,
                                          pattern=[[step, cols]], channel_multiplier=mult)

            for t, v in ((ident, 0.0), (causal, 1.0), (neg_tri, -1.0), (neg_one, -1.0), (avg, 1.0 / BW),
                         (maskb, 0.0), (strictb, 1.0), (oneb, 1.0), (eps, EPS)):
                st.mark(pool.memset(t[:], v))
            st.mark(pool.memset(cu[:, :, 0:CF_W - 1], 0.0))
            st.mark(pool.memset(ca[:, :, 0:CA_W - 1], 0.0))
            st.mark(pool.iota(slot_no[:, :], pattern=[[1, P]], base=0, channel_multiplier=0, allow_small_or_imprecise_dtypes=True))
            st.mark(pool.iota(from_last[:, :], pattern=[[-1, NE]], base=NE, channel_multiplier=0, allow_small_or_imprecise_dtypes=True))
            st.mark(pool.iota(row_no[:, :, :], pattern=[[2 * P, NT], [1, 2]], base=-UNUSED, channel_multiplier=2,
                              allow_small_or_imprecise_dtypes=True))
            st.done()
            st.mark(select(ident, P, ALU.not_equal, 1.0, 0, -1, 1))
            st.mark(select(causal, T, ALU.is_ge, 0.0, 0, 1, -1))
            st.mark(select(neg_tri, P, ALU.is_ge, 0.0, 0, -1, 1))
            st.mark(select(maskb, P, ALU.is_ge, MASKED, 0, -1, 1))
            st.mark(select(strictb, P, ALU.is_gt, 0.0, 0, 1, -1))
            st.done()
            st.link(pool.tensor_copy(identb[:, :], ident[:, :]))
            pool.sem_inc(S["consts"], 1)

            for n in range(STEPS):
                h, kt, q0 = stick_step(n)
                pool.wait_ge(S["sp_max"], n + 1)
                select(None, P, ALU.is_gt, 0.0, 0, 1, -1, view=sp[:, kt, q0:q0 + P]).then_inc(S["sp_mask"], 1)
                pool.wait_ge(S["w_exp"], n + 1)
                select(None, P, ALU.is_gt, 0.0, 0, 1, -1, view=wts[:, q0:q0 + P]).then_inc(S["w_mask"], 1)
            pool.wait_ge(S["gffn_in"], 16)
            for t in range(NT):
                pool.wait_ge(S["xn2_scaled"], t + 1)
                pool.tensor_tensor(xn2[:, t, :], xn2[:, t, :], gffn[:, :], ALU.mult).then_inc(S["xn2_ready"], 1)
            pool.wait_ge(S["lg_ps"], 1)
            st.mark(pool.memset(xg[:, :, :], 0.0))
            pool.wait_ge(S["xn_out"], 16 * NT)
            st.done()
            pool.sem_inc(S["ye_free"], 2)
            last_token = pool.to_reg(T - 1)
            last_row = pool.to_reg(2 * T - 1)

            def turn():
                pool.sem_inc(S["turns"], 1)

            def gather(E, e, q):
                s = q % XG
                pool.tensor_copy(gather_i[:, s, :], toks[:, bass.ds(e, 1)]).then_inc(S["gather_col"], 1)
                pool.wait_ge(S["gather_col"], E + 1)
                turn()
                pool.indirect_dma_start(out=xg[:, s, :], out_offset=None, in_=xn_dram[:, :],
                                        in_offset=bass.IndirectOffsetOnAxis(ap=gather_i[:, s, :], axis=0),
                                        bounds_check=last_token, oob_is_err=False).then_inc(g_full[s], 16)

            def scatter(E, e, q):
                s = q % 2
                pool.wait_ge(S["y_out"], E * 2 + 4)
                turn()
                pool.tensor_copy(scatter_i[:, s, :], slots[:, bass.ds(e, 1)]).then_inc(S["scatter_col"], 1)
                pool.wait_ge(S["scatter_col"], E + 1)
                turn()
                pool.indirect_dma_start(out=y_dram[:, :], out_offset=bass.IndirectOffsetOnAxis(ap=scatter_i[:, s, :], axis=0),
                                        in_=ye[:, s, :], in_offset=None, bounds_check=last_row,
                                        oob_is_err=False).then_inc(scattered[s], 16)

            def start_pass(c):
                pool.wait_ge(S["idx_ready"], c + 1)
                turn()
                for q in range(XG):
                    gather(c * NE + q, q, q)

            def four(c, i, last=False):
                for q in range(4):
                    E = c * NE + i * 4 + q
                    if not last:
                        pool.wait_ge(S["xt_ps"], E * 2 + 2)
                        gather(E + XG, i * 4 + q + XG, q)
                    scatter(E, i * 4 + q, q)
                    pool.wait_ge(scattered[q % 2], (c * (NE // 2) + i * 2 + q // 2 + 1) * 16)
                    pool.sem_inc(S["ye_free"], 1)

            start_pass(0)
            with pool.Fori(0, LOOPS - 1) as i:
                four(0, i)
            four(0, LOOPS - 1, last=True)
            pool.wait_ge(S["flag_ready"], 1)
            most = pool.value_load(flag[0:1, 0:1], min_val=0, max_val=T)
            with pool.If(most > P):
                with pool.Fori(1, NT) as c:
                    start_pass(c)
                    with pool.Fori(0, LOOPS - 1) as i:
                        four(c, i)
                    four(c, LOOPS - 1, last=True)

            for t in range(POOL_TILES):
                pool.wait_ge(S["fin_scaled"], t + 1)
                if t == 0:
                    pool.wait_ge(S["gfin_in"], 16)
                pool.tensor_tensor(yt[:, t, 0, :], yt[:, t, 0, :], gfin[:, :], ALU.mult).then_inc(S["fin"], 1)

        @block.scalar
        def _(act):
            st = Steps(act, S["act_step"])
            def split_hi(u, n):
                s = u % 2
                act.wait_ge(raw_full[s], 16 * (u // 2 + 1))
                if u >= OUT0 + 2:
                    act.wait_ge(S["out_ps"], 2 * (u - OUT0 - 1))
                elif 2 <= u < NP:
                    act.wait_ge(S["unit_used"], u - 1)
                act.activation(wh[:, s, 0:n], raw[:, s, 0:n], ACT.Copy).then_inc(S["hi_ready"], 1)

            act.preload_act_table(ACT.Sqrt)
            for t in range(NT):
                act.wait_ge(x_in[t], 16)
                act.activation(junk[:, :], xt[:, t, :], ACT.Square, accum_out=stat[:, 0, t:t + 1]).then_inc(S["sq_done"], 1)
                act.wait_ge(S["sq_done"], t + 1)
                if t == 0:
                    act.wait_ge(S["consts"], 1)
                act.activation(stat[:, 1, t:t + 1], stat[:, 0, t:t + 1], ACT.Sqrt, bias=eps[:, 0:1], scale=1.0 / D).then_inc(S["root"], 1)
            act.wait_ge(S["g_in"], 16)
            for c in range(KC):
                act.wait_ge(S["xt_psum"], c + 1)
                act.activation(xh[:, c, :], bank[(c + 4) % 8][:, :], ACT.Copy, scale=gmix[:, c:c + 1]).then_inc(S["xt_hi"], 1)
                if c == 3:
                    split_hi(0, KC * PROJ[0][2])

            HALF = UNIT // 2

            def x_hi_part(k, part):
                s = (GATE0 + k) % 2
                if part == 0:
                    act.wait_ge(raw_full[s], 16 * ((GATE0 + k) // 2 + 1))
                    act.wait_ge(br_full[s], 16 * (k // 2 + 1))
                    if k < 2:
                        act.wait_ge(S["unit_used"], GATE0 + k - 1)
                    else:
                        act.wait_ge(S["xb_ps"], 2 * (k - 1))
                part_of = slice(part * HALF, (part + 1) * HALF)
                act.activation(wh[:, s, part_of], raw[:, s, part_of], ACT.Copy).then_inc(S["hi_ready" if part else "hi_part"], 1)

            split_hi(1, KC * PROJ[1][2])
            for u, (name, _, cols) in enumerate(PROJ):
                pair = [bank[4 + 2 * (u % 2) + j] for j in range(2)]
                free = proj_free[u % 2]
                act.wait_ge(S["unit_used"], u + 1)
                if name in ("u", "ax", "ab", "sk", "fk"):
                    dst = {"u": cu[:, :, CF_W - 1:], "ax": axb, "ab": ab, "sk": k_s, "fk": k_f}[name]
                    for j in range(BJ):
                        act.activation(dst[:, j, :], pair[j][:, :], ACT.Copy).then_inc(free, 1)
                elif name == "ug":
                    for j in range(BJ):
                        act.activation(sg[:, j, :], pair[j][:, :], ACT.Sigmoid).then_inc(free, 1)
                elif name in ("sq", "fq"):
                    for j in range(BJ):
                        act.activation({"sq": q_s, "fq": q_f}[name][:, j, :], pair[j][:, :], ACT.Copy, scale=SCALE).then_inc(free, 1)
                elif name == "sv":
                    for j in range(2):
                        act.activation(sv[:, 2 * j:2 * j + 2, :], pair[j][:, :].rearrange("p (t n) -> p t n", t=2), ACT.Copy).then_inc(free, 1)
                elif name == "fv":
                    for t in range(NT):
                        ins = act.activation(fv[:, t, :], bank[4 + t][:, 0:BW], ACT.Copy)
                        if t % 2:
                            ins.then_inc(free, 1)
                if u + 2 < NP:
                    split_hi(u + 2, KC * PROJ[u + 2][2])
                else:
                    for part in range(2):
                        x_hi_part(u + 2 - NP, part)
                if name == "sk":
                    act.wait_ge(S["ff_abs"], 1)
                    act.activation(ff[:, 2, :, :], ff[:, 1, :, :], ACT.Exp, scale=-1.0).then_inc(S["ff_ln"], 1)
                    act.wait_ge(S["ff_ln"], 1)
                    act.activation(ff[:, 2, :, :], ff[:, 2, :, :], ACT.Ln, bias=1.0).then_inc(S["ff_ln"], 1)
                if name == "fq":
                    act.wait_ge(S["ln_in"], 1)
                    for h in range(NH - 1):
                        act.wait_ge(S["dc_psum"], h + 1)
                        act.activation(dcum[:, h, :], bank[1 + h][:, :], ACT.Copy).then_inc(S["dc_out"], 1)
                    for j in range(BJ):
                        act.wait_ge(S["ln_cent"], j + 1)
                        act.activation(axb[:, j, :], sg[:, j, :], ACT.Square).then_inc(S["ln_sq"], 1)
            act.wait_ge(S["dc_psum"], NH)
            act.activation(dcum[:, NH - 1, :], bank[1][:, :], ACT.Copy).then_inc(S["dc_out"], 1)
            act.preload_act_table_set("natural_log_exp_and_others")
            act.wait_ge(S["ln_var"], 1)
            st.link(act.activation(ab[:, 0, :], bank[0][:, :], ACT.Ln, bias=eps[:, 0:1]))
            act.activation(ab[:, 1, :], ab[:, 0, :], ACT.Exp, scale=-0.5).then_inc(S["ln_root"], 1)
            lng, lnb = CA_W + CF_W + 1, CA_W + CF_W + 2
            for j in range(BJ):
                act.wait_ge(S["ln_norm"], j + 1)
                act.activation(axb[:, j, :], sg[:, j, :], ACT.Silu, bias=ch[:, j, lnb:lnb + 1], scale=ch[:, j, lng:lng + 1]).then_inc(S["ln_act"], 1)
            act.preload_act_table_set("natural_log_exp_and_others")
            for n in range(STEPS + 1):
                if n < STEPS:
                    h, kt, q0 = stick_step(n)
                    b = tmp[:, q0:]
                    g, d = x_tile(n)
                    act.wait_ge(S["xg_ps"], n + 1)
                    if n >= 2:
                        act.wait_ge(S["xg_free"], n - 1)
                    act.activation(gs[:, n % 2, :], bank[6 + n % 2][:, :], ACT.Identity, scale=-1.0,
                                   bias=bg_neg[:, g * KC + d:g * KC + d + 1]).then_inc(S["xg_neg"], 1)
                    act.wait_ge(S["sp_min"], n + 1)
                    st.link(act.activation(b, b, ACT.Exp))
                    act.activation(b, b, ACT.Ln, bias=1.0).then_inc(S["sp_ln"], 1)
                    h, qt, m = fox_step(n)
                    act.wait_ge(S["l_bias"], n + 1)
                    act.activation(lg[:, 0:m], lg[:, 0:m], ACT.Exp, bias=small[:, n % 2, 2:3],
                                   accum_out=small[:, n % 2, 3:4]).then_inc(S["l_exp"], 1)
                    b = gp[:, n % 2, :]
                    act.wait_ge(S["xg_min"], n + 1)
                    st.link(act.activation(b, b, ACT.Exp))
                    act.activation(b, b, ACT.Ln, bias=1.0).then_inc(S["xg_ln"], 1)
                    k, part = (n + 3) // 2, (n + 1) % 2
                    if n >= 1 and k <= NX:
                        x_hi_part(k, part)
                    act.wait_ge(S["xg_max"], n + 1)
                    act.activation(gs[:, n % 2, :], gp[:, n % 2, :], ACT.Exp, scale=-1.0).then_inc(S["xg_exp"], 1)
                if n and n % NT == 0:
                    h = n // NT - 1
                    j, r = head_rows(h)
                    act.wait_ge(S["wv_done"], n)
                    act.activation(yh[r:r + HD, 1, j, :], bank[3][r:r + HD, :], ACT.Copy).then_inc(S["o_hi"], 1)
                    act.wait_ge(S["fo_psum"], n)
                    act.activation(yh[r:r + HD, 2, j, :], bank[4][r:r + HD, :], ACT.Copy).then_inc(S["fo_hi"], 1)
                if n < STEPS:
                    h, kt, q0 = stick_step(n)
                    act.wait_ge(S["acc_done"], n + 1)
                    if n >= 1:
                        act.wait_ge(S["wv_done"], n)
                    act.activation(wts[:, q0:], bank[0][:, q0:], ACT.Exp).then_inc(S["w_exp"], 1)
                    h, qt, m = fox_step(n)
                    act.wait_ge(S["pt_psum"], n + 1)
                    if n >= 1:
                        act.wait_ge(S["fo_psum"], n)
                    act.activation(pt[:, 0:qt + 1, :], bank[2][:, 0:m].rearrange("p (k q) -> p k q", q=P),
                                   ACT.Copy).then_inc(S["pt_out"], 1)

            def gate_sigmoid(g, cg):
                for m in range(2):
                    d = g * KC + (2 * cg + m)
                    act.wait_ge(S["gate_ps"], d + (1 - KC))
                    act.wait_ge(S["gate_free"], d + (1 - KC))
                    act.activation(gs[:, m, :], bank[m][:, :], ACT.Sigmoid,
                                   bias=bg[:, bass.ds(d, 1)]).then_inc(S["gate_mul"], 1)

            def gate_hi(g, cg):
                s = (GATE0 + cg) % 2
                act.wait_ge(raw_full[s], (g * (CG // 2) + (LOOP0 + cg) // 2 + 1) * 16)
                act.wait_ge(br_full[s], (g * (CG // 2) + (NX - CG + cg) // 2 + 1) * 16)
                act.wait_ge(S["br_ps"], g * (2 * CG) + (2 * cg + BR0 - 2 - KC))
                act.activation(wh[:, s, :], raw[:, s, :], ACT.Copy).then_inc(S["hi_ready"], 1)

            act.wait_ge(S["xb_ps"], STEPS)
            act.wait_ge(S["xg_free"], STEPS)
            with act.Fori(1, NB - 1) as g:
                for cg in range(CG):
                    gate_hi(g, cg + 1)
                    gate_sigmoid(g, cg)

            act.wait_ge(S["br_ps"], BR0 + 2 * KC)
            for c in range(KC):
                act.wait_ge(S["h_add"], 2 * KC - (KC - 1 - c))
                act.activation(xh[:, c, :], hsum[:, c, :], ACT.Copy).then_inc(S["h_hi"], 1)
            def squares(cg):
                act.wait_ge(S["x2_ready"], 2 * (cg + 1))
                if cg:
                    act.wait_ge(S["sq2"], NT * cg)
                for t in range(NT):
                    act.activation(sq_junk[:, t, :], x2[:, t, cg * UC:(cg + 1) * UC], ACT.Square,
                                   accum_out=sq_part[:, t, cg:cg + 1]).then_inc(S["sq2"], 1)

            def router_input(cg):
                c = 2 * cg
                act.wait_ge(S["xt2_ps"], c + 1)
                act.activation(xt2[:, c, :], bank[4][:, :], ACT.Copy).then_inc(S["xt2_a"], 1)

            def half_hi(c, i, n):
                unit = n // 2
                act.wait_ge(eraw_full[unit % RS], (c * (UPE * NE // RS) + i * (4 * UPE // RS) + unit // RS + 1) * 16)
                act.wait_ge(S["e_used"], c * (HPE * NE) + i * (4 * HPE) + n + 1)
                act.activation(ewh[n % HS][:, :], eraw[:, unit % RS, n % 2 * HU:(n % 2 + 1) * HU], ACT.Copy).then_inc(S["e_hi"], 1)

            act.preload_act_table(ACT.Sqrt)
            for cg in range(1, CG):
                split_hi(OUT0 + cg, KC * UC)
                squares(cg - 1)
                router_input(cg - 1)
                for n in range(2 * cg - 2, min(2 * cg, EARLY)):
                    half_hi(0, 0, n)
            squares(CG - 1)
            act.wait_ge(S["sq2_sum"], 1)
            act.activation(stat[:, 1, :], stat[:, 0, :], ACT.Sqrt, bias=eps[:, 0:1], scale=1.0 / D).then_inc(S["root2"], 1)
            router_input(CG - 1)
            half_hi(0, 0, EARLY)
            act.wait_ge(S["recip2"], 1)
            for t in range(NT):
                act.activation(xn2[:, t, :], x2[:, t, :], ACT.Copy, scale=stat[:, 2, t:t + 1]).then_inc(S["xn2_scaled"], 1)
            half_hi(0, 0, EARLY + 1)
            act.wait_ge(S["lg_d"], 1)
            act.activation(rg[:, 3, :, :], rg[:, 2, :, :], ACT.Exp).then_inc(S["lg_act"], 1)
            act.wait_ge(S["lg_e"], 1)
            act.activation(rs[:, 5, :], rs[:, 4, :], ACT.Exp).then_inc(S["lg_act"], 1)


            def x_hi(c, i, q):
                E = c * NE + i * 4 + q
                for b in range(2):
                    act.wait_ge(S["xt_ps"], E * 2 + b + 1)
                    if q:
                        done = HPE * (q - 2) + 8 if q > 1 else 4
                        act.wait_ge(S["e_used"], c * (HPE * NE) + i * (4 * HPE) + (done + HS))
                    act.activation(xgh[:, 4 * b:4 * b + 4, :], bank[b][:, :].rearrange("p (c s) -> p c s", s=P), ACT.Copy).then_inc(S["xe_h"], 1)

            def start_pass(c, done=0):
                for n in range(done, 4):
                    half_hi(c, 0, n)
                for n in range(max(done, 4), 8):
                    half_hi(c, 0, n)
                x_hi(c, 0, 0)
                x_hi(c, 0, 1)
                for n in range(8, 10):
                    half_hi(c, 0, n)

            def four(c, i, last=False):
                for q in range(4):
                    E = c * NE + i * 4 + q
                    n = 4 + HPE * (q + 1)
                    halves = range(n, n + (HPE if not last or q < 2 else 2 if q == 2 else 0))
                    act.wait_ge(S["e_used"], c * (HPE * NE) + i * (4 * HPE) + (HPE * q + 4 + HS))
                    act.activation(act_g[:, :], bank[2 + q % 2][:, 0:FE], ACT.Silu).then_inc(S["silu"], 1)
                    for k in halves[0:2]:
                        half_hi(c, i, k)
                    act.wait_ge(S["ht_ps"], E + 1)
                    act.activation(hidh[:, :, :], bank[4][:, 0:FE].rearrange("p (m s) -> p m s", s=P), ACT.Copy).then_inc(S["ht_h"], 1)
                    for k in halves[2:4]:
                        half_hi(c, i, k)
                    if not (last and q >= 2):
                        x_hi(c, i, q + 2)
                    for k in halves[4:6]:
                        half_hi(c, i, k)
                    s = q % 2
                    act.wait_ge(S["ye_free"], E + 1)
                    done = HPE * (q + 1) + 4 if not (last and q == 3) else HPE * (q + 1)
                    act.wait_ge(S["e_used"], c * (HPE * NE) + i * (4 * HPE) + (done + HS))
                    for b in range(2):
                        act.activation(ye[:, s, b * T:(b + 1) * T], bank[5 + b][:, :], ACT.Copy).then_inc(S["y_out"], 1)

            act.sem_inc(S["y_out"], 2)
            start_pass(0, EARLY + 2)
            with act.Fori(0, LOOPS - 1) as i:
                four(0, i)
            four(0, LOOPS - 1, last=True)
            act.wait_ge(S["flag_ready"], 1)
            most = act.value_load(flag[0:1, 0:1], min_val=0, max_val=T)
            with act.If(most > P):
                with act.Fori(1, NT) as c:
                    start_pass(c)
                    with act.Fori(0, LOOPS - 1) as i:
                        four(c, i)
                    four(c, LOOPS - 1, last=True)
            act.preload_act_table(ACT.Sqrt)
            for t in range(NT + 1):
                if t < NT:
                    act.wait_ge(S["comb"], t + 1)
                    act.activation(yt[:, t, 0, :], x2[:, t, :], ACT.Square, accum_out=stat[:, 0, t:t + 1]).then_inc(S["sq3"], 1)
                    act.wait_ge(S["sq3"], t + 1)
                    act.activation(stat[:, 1, t:t + 1], stat[:, 0, t:t + 1], ACT.Sqrt, bias=eps[:, 0:1], scale=1.0 / D).then_inc(S["root3"], 1)
                if 1 <= t <= POOL_TILES:
                    act.wait_ge(S["recip3"], t)
                    act.activation(yt[:, t - 1, 0, :], x2[:, t - 1, :], ACT.Copy, scale=stat[:, 2, t - 1:t]).then_inc(S["fin_scaled"], 1)

        @block.vector
        def _(dve):
            st = Steps(dve, S["dve_step"])

            def stt(out_, a, s, b, o0, o1):
                return dve.scalar_tensor_tensor(out=out_, in0=a, scalar=s, in1=b, op0=o0, op1=o1)

            def lo(dst, src, hi):
                return dve.tensor_tensor(dst, src, hi.bitcast(F32), ALU.subtract)

            def head_lo(name, g, h):
                j, r = head_rows(h)
                dve.wait_ge(S[f"{name}_hi"], h + 1)
                lo(yl[r:r + HD, g, j, :], bank[2 + g][r:r + HD, :], yh[r:r + HD, g, j, :]).then_inc(S[f"{name}_split"], 1)

            def residual(cg):
                if cg == 0:
                    dve.wait_ge(S["x2_in"], 16 * NT)
                for b in range(2):
                    dve.wait_ge(S["out_ps"], 2 * cg + b + 1)
                    cols = slice(cg * UC, (cg + 1) * UC)
                    dve.tensor_tensor(x2[:, 2 * b:2 * b + 2, cols], x2[:, 2 * b:2 * b + 2, cols],
                                      bank[2 * (cg % 2) + b][:, :].rearrange("p (t n) -> p t n", t=2), ALU.add).then_inc(S["x2_ready"], 1)

            def split_lo(u, n):
                s = u % 2
                dve.wait_ge(S["hi_ready"], u + 1)
                lo(wl[:, s, 0:n], raw[:, s, 0:n], wh[:, s, 0:n]).then_inc(S["split_ready"], 1)

            for t in range(NT):
                dve.wait_ge(S["root"], t + 1)
                st.link(dve.reciprocal(stat[:, 2, t:t + 1], stat[:, 1, t:t + 1]))
                dve.tensor_scalar(xt[:, t, :], xt[:, t, :], stat[:, 2, t:t + 1], None, ALU.mult).then_inc(S["xn_ready"], 1)
            for c in range(KC):
                dve.wait_ge(S["xt_hi"], c + 1)
                stt(xl[:, c, :], bank[(c + 4) % 8][:, :], gmix[:, c:c + 1], xh[:, c, :].bitcast(F32), ALU.mult, ALU.subtract).then_inc(S["xt_ready"], 1)
                if c == 3:
                    split_lo(0, KC * PROJ[0][2])
            HALF = UNIT // 2

            def x_lo_part(k, part):
                s = (GATE0 + k) % 2
                dve.wait_ge(S["hi_ready" if part else "hi_part"], (GATE0 if part else 0) + k + 1)
                part_of = slice(part * HALF, (part + 1) * HALF)
                ins = lo(wl[:, s, part_of], raw[:, s, part_of], wh[:, s, part_of])
                if part:
                    ins.then_inc(S["split_ready"], 1)

            taps = iter([(i, j) for i in range(CF_W) for j in range(BJ)])

            def conv_taps(count):
                for _ in range(count):
                    i, j = next(taps, (None, None))
                    if i is None:
                        return
                    win = cu[:, j, i:i + T]
                    if i == 0:
                        dwb = CA_W + CF_W
                        st.mark(dve.tensor_scalar(sg[:, j, :], win, ch[:, j, CA_W:CA_W + 1], ch[:, j, dwb:dwb + 1], ALU.mult, ALU.add))
                    else:
                        st.done(st.n - 1)
                        st.mark(stt(sg[:, j, :], win, ch[:, j, CA_W + i:CA_W + i + 1], sg[:, j, :], ALU.mult, ALU.add))

            split_lo(1, KC * PROJ[1][2])
            dve.wait_ge(S["tabs_psum"], 1)
            st.mark(dve.tensor_copy(ch[:, :, :], bank[0][:, 0:BJ * NROW].rearrange("p (j n) -> p j n", j=BJ)))
            st.mark(dve.tensor_copy(gffn_t[:, :], bank[0][:, P + NB * KC:P + (NB + 1) * KC]))
            st.mark(dve.tensor_scalar(bg_neg[:, :], bank[0][:, P:P + NB * KC], -1.0, None, ALU.mult))
            dve.tensor_copy(bg[:, :], bank[0][:, P:P + NB * KC]).then_inc(S["tabs_ready"], 1)
            st.done()

            for u, (name, _, cols) in enumerate(PROJ):
                pair = [bank[4 + 2 * (u % 2) + j] for j in range(2)]
                if name == "ug":
                    evacuated(dve, "u")
                    evacuated(dve, "ug")
                    for j in range(BJ):
                        st.mark(dve.tensor_tensor(cu[:, j, CF_W - 1:], cu[:, j, CF_W - 1:], sg[:, j, :], ALU.mult))
                    st.done()
                if name == "ac":
                    evacuated(dve, "ax")
                    dve.wait_ge(S["unit_used"], u + 1)
                    for j in range(BJ):
                        dve.tensor_tensor(ca[:, j, CA_W - 1:], axb[:, j, :], pair[j][:, :], ALU.mult).then_inc(proj_free[u % 2], 1)
                if name == "ab":
                    evacuated(dve, "ac")
                    evacuated(dve, "ab")
                    for j in range(BJ):
                        st.link(dve.tensor_scalar(axb[:, j, :], ca[:, j, 0:T], ch[:, j, 0:1], None, ALU.mult))
                        for i in range(1, CA_W):
                            st.link(stt(axb[:, j, :], ca[:, j, i:i + T], ch[:, j, i:i + 1], axb[:, j, :], ALU.mult, ALU.add))
                        st.link(dve.tensor_tensor(axb[:, j, :], axb[:, j, :], ab[:, j, :], ALU.mult))
                        st.link(dve.tensor_copy(yh[:, 0, j, :], axb[:, j, :]))
                        st.mark(lo(yl[:, 0, j, :], axb[:, j, :], yh[:, 0, j, :]))
                if name == "fv":
                    dve.wait_ge(S["unit_used"], u + 1)
                    dve.wait_ge(S["bf_in"], 16)
                    dve.wait_ge(proj_free[u % 2], 2 * (u // 2 + 1))
                    for t in range(NT):
                        st.mark(dve.tensor_tensor(ff[:, 0, t, :], bank[4 + t][:, BW:BW + NH], bf[:, :], ALU.add))
                    st.done()
                    stt(ff[:, 1, :, :], ff[:, 0, :, :], -1.0, ff[:, 0, :, :], ALU.mult, ALU.max).then_inc(S["ff_abs"], 1)
                if u + 2 < NP:
                    split_lo(u + 2, KC * PROJ[u + 2][2])
                else:
                    for part in range(2):
                        x_lo_part(u + 2 - NP, part)
                if u >= 1:
                    conv_taps(10)
                if name == "sk":
                    dve.wait_ge(S["ff_ln"], 2)
                    st.link(stt(ff[:, 3, :, :], ff[:, 0, :, :], 0.0, ff[:, 2, :, :], ALU.min, ALU.subtract))
                    for h in range(NH):
                        dve.tensor_copy(fbc[:, h, :, :], ff[:, 3, :, h:h + 1].to_broadcast([P, NT, P])).then_inc(S["fbc_ready"], 1)
                    conv_taps(2 * CF_W)
                    st.done()
                    dve.sem_inc(S["ln_in"], 1)
                if name == "fq":
                    dve.wait_ge(S["ln_mean"], 1)
                    for j in range(BJ):
                        dve.tensor_tensor(sg[:, j, :], sg[:, j, :], bank[0][:, :], ALU.subtract).then_inc(S["ln_cent"], 1)
            dve.wait_ge(S["dq_psum"], 1)
            st.link(dve.tensor_copy(dq[:, :, :], bank[2][:, 0:NT * NH].rearrange("p (t h) -> p t h", h=NH)))
            dve.sem_inc(S["dq_out"], 1)
            dve.wait_ge(S["ln_root"], 1)
            for j in range(BJ):
                dve.tensor_tensor(sg[:, j, :], sg[:, j, :], ab[:, 1, :], ALU.mult).then_inc(S["ln_norm"], 1)
            for j in range(BJ):
                dve.wait_ge(S["ln_act"], j + 1)
                st.link(dve.tensor_copy(yh[:, 3, j, :], axb[:, j, :]))
                st.mark(lo(yl[:, 3, j, :], axb[:, j, :], yh[:, 3, j, :]))
            st.done()
            dve.sem_inc(S["y_ready"], 1)
            dve.wait_ge(S["dc_out"], NH)
            for n in range(STEPS + 1):
                if n < STEPS:
                    h, kt, q0 = stick_step(n)
                    dve.wait_ge(S["z_psum"], n + 1)
                    dve.tensor_scalar(tmp[:, q0:], bank[0][:, q0:], CAP, None, ALU.min).then_inc(S["sp_min"], 1)
                    h, qt, m = fox_step(n)
                    sm = small[:, n % 2, :]
                    dve.wait_ge(S["l_psum"], n + 1)
                    if n >= 1:
                        dve.wait_ge(S["pt_psum"], n)
                    st.link(dve.tensor_tensor_reduce(out=lg[:, 0:m], in0=bank[1][:, 0:m], in1=dcum[:, h, 0:m], scale=1.0,
                                                     scalar=-3e38, op0=ALU.subtract, op1=ALU.max, accum_out=sm[:, 0:1]))
                    dve.sem_inc(S["l_max"], 1)
                    st.link(dve.tensor_tensor(sm[:, 1:2], sm[:, 0:1], dq[:, qt, h:h + 1], ALU.add))
                    dve.tensor_tensor(sm[:, 2:3], dq[:, qt, h:h + 1], sm[:, 1:2], ALU.subtract).then_inc(S["l_bias"], 1)
                    g, d = x_tile(n)
                    b, c = gp[:, n % 2, :], gs[:, n % 2, :]
                    dve.wait_ge(S["xg_neg"], n + 1)
                    dve.tensor_scalar(b, c, CAP, None, ALU.min).then_inc(S["xg_min"], 1)
                    h, kt, q0 = stick_step(n)
                    dve.wait_ge(S["sp_ln"], n + 1)
                    if kt == NT - 1 and h:
                        dve.wait_ge(S["acc_done"], h * NT)
                    stt(sp[:, kt, q0:], bank[0][:, q0:], 0.0, tmp[:, q0:], ALU.add, ALU.max).then_inc(S["sp_max"], 1)
                    dve.wait_ge(S["l_exp"], n + 1)
                    st.link(dve.reciprocal(sm[:, 4:5], sm[:, 3:4]))
                    dve.tensor_scalar(lg[:, 0:m], lg[:, 0:m], sm[:, 4:5], None, ALU.mult).then_inc(S["l_norm"], 1)
                    dve.wait_ge(S["xg_ln"], n + 1)
                    dve.tensor_tensor(b, b, c, ALU.max).then_inc(S["xg_max"], 1)
                    k, part = (n + 3) // 2, (n + 1) % 2
                    if n >= 1 and k <= NX:
                        x_lo_part(k, part)
                    dve.wait_ge(S["xg_exp"], n + 1)
                    dve.wait_ge(S["xb_ps"], n + 1)
                    if g == 0:
                        dve.tensor_tensor(hsum[:, d, :], c, bank[5][:, :], ALU.mult).then_inc(S["xg_free"], 1)
                    else:
                        dve.tensor_tensor(b, c, bank[5][:, :], ALU.mult).then_inc(S["xg_free"], 1)
                        dve.wait_ge(S["xg_free"], n + 1)
                        dve.tensor_tensor(hsum[:, d, :], hsum[:, d, :], b, ALU.add)
                if n and n % NT == 0:
                    head_lo("o", 1, n // NT - 1)
                    head_lo("fo", 2, n // NT - 1)

            def gate_lo(g, cg):
                s = (GATE0 + cg) % 2
                dve.wait_ge(S["hi_ready"], g * CG + LOOP0 + cg + 1)
                lo(wl[:, s, :], raw[:, s, :], wh[:, s, :]).then_inc(S["split_ready"], 1)

            def gate_sum(g, cg):
                for m in range(2):
                    d = g * KC + (2 * cg + m)
                    dve.wait_ge(S["gate_mul"], d + (1 - KC))
                    dve.wait_ge(S["br_ps"], d + (BR0 + 1 - KC))
                    dve.tensor_tensor(gp[:, m, :], gs[:, m, :], bank[2 + m][:, :], ALU.mult).then_inc(S["gate_free"], 1)
                    dve.wait_ge(S["gate_free"], d + (3 - KC))
                    dve.tensor_tensor(hsum[:, 2 * cg + m, :], hsum[:, 2 * cg + m, :], gp[:, m, :], ALU.add).then_inc(S["h_add"], 1)

            dve.sem_inc(S["gate_free"], 2)
            with dve.Fori(1, NB - 1) as g:
                for cg in range(CG):
                    gate_lo(g, cg + 1)
                    gate_sum(g, cg)
            for c in range(KC):
                dve.wait_ge(S["h_hi"], c + 1)
                lo(xl[:, c, :], hsum[:, c, :], xh[:, c, :]).then_inc(S["h_split"], 1)
            dve.sem_inc(S["e_split"], SC)
            dve.wait_ge(S["wr_in"], 32)
            st.mark(dve.tensor_tensor(wr[:, :, :], wr[:, :, :], gffn_t[:, :].unsqueeze(2).to_broadcast([P, KC, NG + NE]), ALU.mult))
            st.done()
            dve.sem_inc(S["wr_ready"], 1)

            def half_lo(c, i, n):
                unit = n // 2
                dve.wait_ge(S["e_hi"], c * (HPE * NE) + i * (4 * HPE) + n + 1)
                lo(ewl[n % HS][:, :], eraw[:, unit % RS, (n % 2) * HU:(n % 2 + 1) * HU], ewh[n % HS][:, :]).then_inc(S["e_split"], 1)

            def router_input(cg):
                c = 2 * cg + 1
                dve.wait_ge(S["xt2_ps"], c + 1)
                dve.tensor_copy(xt2[:, c, :], bank[5][:, :]).then_inc(S["xt2_b"], 1)
            for cg in range(CG):
                if cg >= 1:
                    split_lo(OUT0 + cg, KC * UC)
                    residual(cg - 1)
                    router_input(cg - 1)
                    for n in range(2 * cg - 2, min(2 * cg, EARLY)):
                        half_lo(0, 0, n)
            residual(CG - 1)
            dve.wait_ge(S["sq2"], NT * CG)
            dve.reduce_sum(stat[:, 0, :], sq_part[:, :, :], AX.X).then_inc(S["sq2_sum"], 1)
            router_input(CG - 1)
            dve.wait_ge(S["root2"], 1)
            dve.reciprocal(stat[:, 2, :], stat[:, 1, :]).then_inc(S["recip2"], 1)
            half_lo(0, 0, EARLY)
            dve.wait_ge(S["recip2"], 1)
            dve.wait_ge(S["lg_ps"], 1)
            st.link(dve.tensor_tensor(rl[:, :, :], bank[6][:, 0:NT * (NG + NE)].rearrange("p (t n) -> p t n", t=NT),
                                      stat[:, 2, :].unsqueeze(2).to_broadcast([P, NT, NG + NE]), ALU.mult))

            def first_max(src, n, top, eq, score, best, hot):
                st.link(dve.reduce_max(top, src, AX.X))
                st.link(dve.tensor_tensor(eq, src, top.unsqueeze(2).to_broadcast([P, NT, n]), ALU.is_equal))
                st.link(dve.tensor_tensor(score, eq, from_last[:, 0:n].unsqueeze(1).to_broadcast([P, NT, n]), ALU.mult))
                st.link(dve.reduce_max(best, score, AX.X))
                st.link(dve.tensor_tensor(hot, score, best.unsqueeze(2).to_broadcast([P, NT, n]), ALU.is_equal))

            gl, el = rl[:, :, 0:NG], rl[:, :, NG:]
            first_max(gl, NG, rs[:, 0, :], rg[:, 0, :, :], rg[:, 1, :, :], rs[:, 1, :], rg[:, 4, :, :])
            dve.tensor_tensor(rg[:, 2, :, :], gl, rs[:, 0, :].unsqueeze(2).to_broadcast([P, NT, NG]), ALU.subtract).then_inc(S["lg_d"], 1)
            st.link(dve.tensor_scalar(rg[:, 5, :, :], rg[:, 4, :, :], -1.0, -FAR, ALU.add, ALU.mult))
            for t in range(NT):
                st.mark(dve.tensor_tensor(re[:, 0, t, :].rearrange("p (g e) -> p g e", g=NG), el[:, t, :].rearrange("p (g e) -> p g e", g=NG),
                                          rg[:, 5, t, :].unsqueeze(2).to_broadcast([P, NG, EG]), ALU.add))
            st.done()
            first_max(re[:, 0, :, :], NE, rs[:, 2, :], re[:, 1, :, :], re[:, 2, :, :], rs[:, 1, :], ro[:, 0, :, :])
            st.link(stt(re[:, 3, :, :], ro[:, 0, :, :], 2 * FAR, re[:, 0, :, :], ALU.mult, ALU.add))
            first_max(re[:, 3, :, :], NE, rs[:, 3, :], re[:, 1, :, :], re[:, 2, :, :], rs[:, 1, :], ro[:, 1, :, :])
            dve.tensor_tensor(rs[:, 4, :], rs[:, 3, :], rs[:, 2, :], ALU.subtract).then_inc(S["lg_e"], 1)
            dve.tensor_tensor(rmask[:, :, :], ro[:, 0, :, :], ro[:, 1, :, :], ALU.add).then_inc(S["m_ready"], 1)
            dve.wait_ge(S["lg_act"], 1)
            st.link(dve.reduce_sum(rs[:, 6, :], rg[:, 3, :, :], AX.X))
            st.link(dve.reciprocal(rs[:, 7, :], rs[:, 6, :]))
            dve.wait_ge(S["lg_act"], 2)
            st.link(dve.tensor_scalar(rs[:, 8, :], rs[:, 5, :], 1.0, None, ALU.add))
            st.link(dve.reciprocal(rs[:, 9, :], rs[:, 8, :]))
            st.link(dve.tensor_tensor(cw[:, 0, :], rs[:, 9, :], rs[:, 7, :], ALU.mult))
            st.link(dve.tensor_tensor(cw[:, 1, :], cw[:, 0, :], rs[:, 5, :], ALU.mult))
            for j in range(2):
                st.mark(dve.tensor_tensor(rv[:, :, j, :], ro[:, j, :, :], row_no[:, :, j:j + 1].to_broadcast([P, NT, NE]), ALU.mult))
            dve.wait_ge(S["rank_ps"], 1)
            for j in range(2):
                st.link(dve.tensor_tensor(re[:, 1 + j, :, :], bank[7][:, 0:NT * NE].rearrange("p (t e) -> p t e", e=NE), ro[:, j, :, :], ALU.mult))
                st.link(dve.reduce_sum(rank[:, :, j:j + 1], re[:, 1 + j, :, :], AX.X))

            def slot_table(n, halves=()):
                for t in range(NT):
                    for j in range(2):
                        ins = dve.tensor_scalar(hot[:, t, j, :], slot_no[:, :], rank[:, t, j:j + 1], None, ALU.is_equal)
                ins.then_inc(S["hot_ready"], 1)
                for k in halves:
                    half_lo(0, 0, k)
                dve.wait_ge(S["slot_ps"], n)
                dve.tensor_scalar(slots[:, :], bank[7][:, 256:256 + NE], float(UNUSED), None, ALU.add).then_inc(S["slots_in"], 1)
                dve.wait_ge(S["slots_in"], n)
                dve.tensor_scalar(toks[:, :], slots[:, :], 1, None, ALU.arith_shift_right).then_inc(S["idx_ready"], 1)

            slot_table(1, (EARLY + 1, EARLY + 2))
            st.link(dve.reduce_max(rs[:, 10, 0:1], bank[7][:, NT * NE:(NT + 1) * NE], AX.X))
            dve.tensor_copy(flag[:, :], rs[:, 10, 0:1]).then_inc(S["flag_ready"], 1)

            def x_lo(E):
                for b in range(2):
                    dve.wait_ge(S["xe_h"], E * 2 + b + 1)
                    lo(xgl[:, 4 * b:4 * b + 4, :], bank[b][:, :].rearrange("p (c s) -> p c s", s=P), xgh[:, 4 * b:4 * b + 4, :]).then_inc(S["xe_l"], 1)

            def start_pass(c, done=0):
                for n in range(done, 8):
                    half_lo(c, 0, n)
                x_lo(c * NE)
                x_lo(c * NE + 1)
                for n in range(8, 10):
                    half_lo(c, 0, n)

            def four(c, i, last=False):
                for q in range(4):
                    E = c * NE + i * 4 + q
                    n = 4 + HPE * (q + 1)
                    halves = range(n, n + (HPE if not last or q < 2 else 2 if q == 2 else 0))
                    dve.wait_ge(S["silu"], E + 1)
                    dve.tensor_tensor(hid[:, :], act_g[:, :], bank[2 + q % 2][:, FE:2 * FE], ALU.mult).then_inc(S["hid_r"], 1)
                    for k in halves[0:2]:
                        half_lo(c, i, k)
                    dve.wait_ge(S["ht_h"], E + 1)
                    lo(hidl[:, :, :], bank[4][:, 0:FE].rearrange("p (m s) -> p m s", s=P), hidh[:, :, :]).then_inc(S["ht_l"], 1)
                    for k in halves[2:4]:
                        half_lo(c, i, k)
                    if not (last and q >= 2):
                        x_lo(E + 2)
                    for k in halves[4:6]:
                        half_lo(c, i, k)

            start_pass(0, EARLY + 3)
            with dve.Fori(0, LOOPS - 1) as i:
                four(0, i)
            four(0, LOOPS - 1, last=True)
            dve.wait_ge(S["flag_ready"], 1)
            most = dve.value_load(flag[0:1, 0:1], min_val=0, max_val=T)
            with dve.If(most > P):
                with dve.Fori(1, NT) as c:
                    dve.tensor_scalar(rank[:, :, :], rank[:, :, :], float(-P), None, ALU.add).then_inc(S["rank_ready"], 1)
                    dve.wait_ge(S["rank_ready"], c)
                    dve.wait_ge(S["ye_free"], c * NE + 2)
                    slot_table(c + 1)
                    start_pass(c)
                    with dve.Fori(0, LOOPS - 1) as i:
                        four(c, i)
                    four(c, LOOPS - 1, last=True)
            dve.wait_ge(S["gfin_in"], 16)
            for t in range(NT + 1):
                if t < NT:
                    dve.wait_ge(y_in[t][0], 16)
                    st.link(stt(x2[:, t, :], yt[:, t, 0, :], cw[:, 0, t:t + 1], x2[:, t, :], ALU.mult, ALU.add))
                    dve.wait_ge(y_in[t][1], 16)
                    stt(x2[:, t, :], yt[:, t, 1, :], cw[:, 1, t:t + 1], x2[:, t, :], ALU.mult, ALU.add).then_inc(S["comb"], 1)
                if t >= 1:
                    u = t - 1
                    dve.wait_ge(S["root3"], t)
                    dve.reciprocal(stat[:, 2, u:u + 1], stat[:, 1, u:u + 1]).then_inc(S["recip3"], 1)
                    if u >= POOL_TILES:
                        dve.wait_ge(S["recip3"], t)
                        stt(yt[:, u, 0, :], x2[:, u, :], stat[:, 2, u:u + 1], gfin[:, :], ALU.mult, ALU.mult).then_inc(S["fin_last"], 1)

        @block.tensor
        def _(pe):
            def passes(dst, pairs, start=True, stop=True):
                seq = []
                for lh, ll, rh, rlo in pairs:
                    seq += [(lh, rh), (lh, rlo), (ll, rh)]
                for n, (a, b) in enumerate(seq):
                    last = nc.tensor.matmul(dst, a, b, start=start and n == 0, stop=stop and n == len(seq) - 1)
                return last

            pe.wait_ge(S["consts"], 1)
            for t in range(NT):
                pe.wait_ge(S["xn_ready"], t + 1)
                for c in range(KC):
                    last = nc.tensor.transpose(bank[(c + 4) % 8][:, t * P:(t + 1) * P],
                                               xt[:, t, :].rearrange("p (n c) -> p c n", c=KC)[:, c, :], ident[:, :])
                    if t == NT - 1:
                        last.then_inc(S["xt_psum"], 1)

            def parameter_rows():
                pe.wait_ge(S["small_in"], N_SMALL)
                for j in range(BJ):
                    nc.tensor.transpose(bank[0][:, j * NROW:(j + 1) * NROW], rows[0:NROW, j * P:(j + 1) * P], ident[0:NROW, 0:NROW])
                n = (NB + 1) * KC
                nc.tensor.transpose(bank[0][:, P:P + n], gb_rows[0:n, :], ident[0:n, 0:n]).then_inc(S["tabs_psum"], 1)

            def cumulative(h, dst):
                for t in range(NT):
                    last = nc.tensor.matmul(dst[:, t * P:], fbc[:, h, t, :], causal[:, 0:T - t * P], start=t == 0, stop=t == NT - 1)
                last.then_inc(S["dc_psum"], 1)

            for u, (name, _, cols) in enumerate(PROJ):
                s = u % 2
                pe.wait_ge(S["split_ready"], u + 1)
                if u == 1:
                    parameter_rows()
                if u >= 2:
                    pe.wait_ge(proj_free[s], 2 * (u // 2))
                if name in ("fv", "sv"):
                    pe.wait_ge(proj_free[1 - s], 2 * ((u - 1) // 2 + 1))
                if name == "sv":
                    pe.wait_ge(S["ff_abs"], 1)
                wv = [w[:, s, 0:KC * cols].rearrange("p (c n) -> p c n", c=KC) for w in (wh, wl)]
                if name in ("sv", "fv"):
                    for t in range(NT):
                        tok = slice(t * P, (t + 1) * P)
                        dst = bank[4 + 2 * s + t // 2][:, (t % 2) * UC:(t % 2) * UC + cols] if name == "sv" else bank[4 + t][:, 0:cols]
                        last = passes(dst, [(xh[:, c, tok], xl[:, c, tok], wv[0][:, c, :], wv[1][:, c, :]) for c in range(KC)])
                else:
                    for j in range(BJ):
                        f = slice(j * P, (j + 1) * P)
                        if u == 0 and j == 0:
                            for c in range(KC):
                                pe.wait_ge(S["xt_ready"], max(c + 1, 2))
                                passes(bank[4][:, :], [(wv[0][:, c, f], wv[1][:, c, f], xh[:, c, :], xl[:, c, :])], start=c == 0, stop=c == KC - 1)
                            continue
                        last = passes(bank[4 + 2 * s + j][:, :], [(wv[0][:, c, f], wv[1][:, c, f], xh[:, c, :], xl[:, c, :]) for c in range(KC)])
                last.then_inc(S["unit_used"], 1)
                if name == "fq":
                    pe.wait_ge(S["ln_in"], 1)
                    for j in range(BJ):
                        last = nc.tensor.matmul(bank[0][:, :], avg[:, :], sg[:, j, :], start=j == 0, stop=j == BJ - 1)
                    last.then_inc(S["ln_mean"], 1)
                    pe.wait_ge(S["fbc_ready"], NH)
                    for h in range(NH - 1):
                        cumulative(h, bank[1 + h])
            pe.wait_ge(S["dc_out"], 1)
            cumulative(NH - 1, bank[1])
            pe.wait_ge(S["dc_out"], 2)
            for t in range(NT):
                for t2 in range(t + 1):
                    last = nc.tensor.matmul(bank[2][:, t * NH:(t + 1) * NH], causal[:, 0:P] if t2 == t else causal[:, P:2 * P],
                                            ff[:, 3, t2, :], start=t2 == 0, stop=t2 == t)
            last.then_inc(S["dq_psum"], 1)
            pe.wait_ge(S["ln_sq"], BJ)
            for j in range(BJ):
                last = nc.tensor.matmul(bank[0][:, :], avg[:, :], axb[:, j, :], start=j == 0, stop=j == BJ - 1)
            last.then_inc(S["ln_var"], 1)
            for name in ("sq", "sk", "sv", "fq", "fk", "fv"):
                evacuated(pe, name)
            def x_products():
                for n in range(STEPS):
                    g, d = x_tile(n)
                    s = (GATE0 + n // 2) % 2
                    f = slice(n % 2 * P, (n % 2 + 1) * P)
                    gate_w = [w[:, s, 0:KC * UC].rearrange("p (c n) -> p c n", c=KC) for w in (wh, wl)]
                    br_w = [w[:, s, KC * UC:UNIT].rearrange("p (c n) -> p c n", c=BJ) for w in (wh, wl)]
                    pe.wait_ge(S["split_ready"], GATE0 + n // 2 + 1)
                    if n >= 2:
                        pe.wait_ge(S["xg_neg"], n - 1)
                    for c in range(KC):
                        for q, (a, b) in enumerate(((gate_w[0], xh), (gate_w[0], xl), (gate_w[1], xh))):
                            last = nc.tensor.matmul(bank[6 + n % 2][:, :], a[:, c, f], b[:, c, :], start=c == 0 and q == 0, stop=c == KC - 1 and q == 2)
                            if c == KC - 1 and q == 2:
                                last.then_inc(S["xg_ps"], 1)
                            yield
                    if n:
                        pe.wait_ge(S["xg_free"], n)
                    if n == KC:
                        pe.wait_ge(S["y_ready"], 1)
                    for j in range(BJ):
                        for q, (a, b) in enumerate(((br_w[0], yh), (br_w[0], yl), (br_w[1], yh))):
                            last = nc.tensor.matmul(bank[5][:, :], a[:, j, f], b[:, g, j, :], start=j == 0 and q == 0, stop=j == BJ - 1 and q == 2)
                            if j == BJ - 1 and q == 2:
                                last.then_inc(S["xb_ps"], 1)
                            yield

            products = x_products()
            PER_TILE = 3 * (KC + BJ)

            def gates(count):
                for _ in range(count):
                    next(products, None)

            gates(PER_TILE)
            pe.wait_ge(S["dc_out"], NH)
            pe.wait_ge(S["dq_out"], 1)
            pe.wait_ge(S["ln_root"], 1)
            for n in range(STEPS + 1):
                if n < STEPS:
                    h, kt, q0 = stick_step(n)
                    j, r = head_rows(h)
                    if n >= 1:
                        pe.wait_ge(S["w_exp"], n)
                    nc.tensor.matmul(bank[0][:, q0:], k_s[r:r + HD, j, kt * P:(kt + 1) * P], q_s[r:r + HD, j, q0:],
                                     start=True, stop=True).then_inc(S["z_psum"], 1)
                    h, qt, m = fox_step(n)
                    if n >= 1:
                        pe.wait_ge(S["l_max"], n)
                    nc.tensor.matmul(bank[1][:, 0:m], q_f[r:r + HD, j, qt * P:(qt + 1) * P], k_f[r:r + HD, j, 0:m], start=True, stop=True)
                    nc.tensor.matmul(bank[1][:, m - P:m], identb[:, :], maskb[:, :], start=False, stop=True,
                                     skip_group_check=True).then_inc(S["l_psum"], 1)
                    gates(PER_TILE // 3)
                if n >= 1:
                    h, kt, q0 = stick_step(n - 1)
                    j, r = head_rows(h)
                    pe.wait_ge(S["w_mask"], n)
                    if kt == NT - 1 and h:
                        pe.wait_ge(S["o_split"], h)
                    nc.tensor.matmul(bank[3][:, q0:], sv[:, kt, j * P:(j + 1) * P], wts[:, q0:],
                                     start=kt == NT - 1, stop=kt == 0, skip_group_check=True).then_inc(S["wv_done"], 1)
                    h, qt, m = fox_step(n - 1)
                    pe.wait_ge(S["pt_out"], n)
                    if qt == 0 and h:
                        pe.wait_ge(S["fo_split"], h)
                    for kt in range(qt + 1):
                        last = nc.tensor.matmul(bank[4][:, qt * P:(qt + 1) * P], fv[:, kt, j * P:(j + 1) * P], pt[:, kt, :],
                                                start=kt == 0, stop=kt == qt)
                    last.then_inc(S["fo_psum"], 1)
                if n < STEPS:
                    gates(PER_TILE // 3)
                    h, kt, q0 = stick_step(n)
                    pe.wait_ge(S["sp_mask"], n + 1)
                    last = nc.tensor.matmul(bank[0][:, q0:], neg_tri[:, :], sp[:, kt, q0:], start=False, stop=True, skip_group_check=True)
                    for k2 in range(kt + 1, NT):
                        last = nc.tensor.matmul(bank[0][:, k2 * P:], neg_one[:, :], sp[:, k2, k2 * P:], start=False, stop=True, skip_group_check=True)
                    last.then_inc(S["acc_done"], 1)
                    h, qt, m = fox_step(n)
                    pe.wait_ge(S["l_norm"], n + 1)
                    for kt in range(qt + 1):
                        last = nc.tensor.transpose(bank[2][:, kt * P:(kt + 1) * P], lg[:, kt * P:(kt + 1) * P], ident[:, :])
                    last.then_inc(S["pt_psum"], 1)
                    gates(PER_TILE // 3)
            yh_f = yh[:, :, :, :].rearrange("p g j t -> p (g j t)")
            yl_f = yl[:, :, :, :].rearrange("p g j t -> p (g j t)")
            pe.sem_inc(S["br_ps"], BR0)
            with pe.Fori(1, NB - 1) as g:
                for cg in range(CG):
                    s = (GATE0 + cg) % 2
                    pe.wait_ge(S["split_ready"], g * CG + LOOP0 + cg + 1)
                    gate_w = [w[:, s, 0:KC * UC].rearrange("p (c n) -> p c n", c=KC) for w in (wh, wl)]
                    br_w = [w[:, s, KC * UC:UNIT].rearrange("p (c n) -> p c n", c=BJ) for w in (wh, wl)]
                    for m in range(2):
                        d = g * KC + (2 * cg + m)
                        f = slice(m * P, (m + 1) * P)
                        pe.wait_ge(S["gate_free"], d + (1 - KC))
                        passes(bank[m][:, :], [(gate_w[0][:, c, f], gate_w[1][:, c, f], xh[:, c, :], xl[:, c, :])
                                               for c in range(KC)]).then_inc(S["gate_ps"], 1)
                        if m == 0:
                            pe.wait_ge(S["o_split"], NH)
                            pe.wait_ge(S["fo_split"], NH)
                        last = passes(bank[2 + m][:, :], [(br_w[0][:, j, f], br_w[1][:, j, f],
                                                           yh_f[:, bass.ds(g * (BJ * T) + j * T, T)],
                                                           yl_f[:, bass.ds(g * (BJ * T) + j * T, T)]) for j in range(BJ)])
                        last.then_inc(S["br_ps"], 1)

            NR = NG + NE

            def router_part(cg):
                pe.wait_ge(S["x2_ready"], 2 * (cg + 1))
                for n in range(2):
                    c = 2 * cg + n
                    if cg:
                        pe.wait_ge(S["xt2_b" if n else "xt2_a"], cg)
                    for t in range(NT):
                        last = nc.tensor.transpose(bank[4 + n][:, t * P:(t + 1) * P], x2[:, t, c * P:(c + 1) * P], ident[:, :])
                    last.then_inc(S["xt2_ps"], 1)
                for n in range(2):
                    c = 2 * cg + n
                    pe.wait_ge(S["xt2_b" if n else "xt2_a"], cg + 1)
                    for t in range(NT):
                        last = nc.tensor.matmul(bank[6][:, t * NR:(t + 1) * NR], xt2[:, c, t * P:(t + 1) * P], wr[:, c, :],
                                                start=c == 0 and t == 0, stop=c == KC - 1, skip_group_check=True)
                return last

            pe.sem_inc(S["e_used"], HS)
            pe.wait_ge(S["wr_ready"], 1)
            for cg in range(CG):
                u = OUT0 + cg
                s = u % 2
                pe.wait_ge(S["split_ready"], u + 1)
                if cg >= 2:
                    pe.wait_ge(S["x2_ready"], 2 * (cg - 1))
                wv = [w[:, s, 0:KC * UC].rearrange("p (c n) -> p c n", c=KC) for w in (wh, wl)]
                for t in range(NT):
                    tok = slice(t * P, (t + 1) * P)
                    if cg == 0 and t == 0:
                        for c in range(KC):
                            pe.wait_ge(S["h_split"], c + 1)
                            passes(bank[0][:, 0:UC], [(xh[:, c, tok], xl[:, c, tok], wv[0][:, c, :], wv[1][:, c, :])], start=c == 0, stop=c == KC - 1)
                        continue
                    last = passes(bank[2 * (cg % 2) + t // 2][:, (t % 2) * UC:(t % 2 + 1) * UC],
                                  [(xh[:, c, tok], xl[:, c, tok], wv[0][:, c, :], wv[1][:, c, :]) for c in range(KC)])
                    if t % 2:
                        last.then_inc(S["out_ps"], 1)
                if cg:
                    router_part(cg - 1)
            router_part(CG - 1).then_inc(S["lg_ps"], 1)
            pe.wait_ge(S["m_ready"], 1)
            for t in range(NT):
                for t2 in range(t + 1):
                    nc.tensor.matmul(bank[7][:, t * NE:(t + 1) * NE], strictb[:, :] if t2 == t else oneb[:, :], rmask[:, t2, :], start=t2 == 0, stop=t2 == t)
            for t in range(NT):
                last = nc.tensor.matmul(bank[7][:, NT * NE:(NT + 1) * NE], oneb[:, :], rmask[:, t, :], start=t == 0, stop=t == NT - 1)
            last.then_inc(S["rank_ps"], 1)

            def x_transposes(c, i, q):
                pe.wait_ge(g_full[q % XG], (c * (NE // XG) + i * (4 // XG) + q // XG + 1) * 16)
                for k in range(KC):
                    last = nc.tensor.transpose(bank[k // 4][:, (k % 4) * P:(k % 4 + 1) * P],
                                               xg[:, q % XG, :].rearrange("p (n c) -> p c n", c=KC)[:, k, :], ident[:, :])
                    if k % 4 == 3:
                        last.then_inc(S["xt_ps"], 1)

            def product(c, i, n, q, col):
                for half in range(2):
                    pe.wait_ge(S["e_split"], c * (HPE * NE) + i * (4 * HPE) + (n + half + SC + 1))
                    wv = [w[(n + half) % HS][:, :].rearrange("p (c f) -> p c f", f=FE) for w in (ewh, ewl)]
                    passes(bank[2 + q % 2][:, col:col + FE],
                           [(xgh[:, 4 * half + k, :], xgl[:, 4 * half + k, :], wv[0][:, k, :], wv[1][:, k, :]) for k in range(4)],
                           start=half == 0, stop=half == 1).then_inc(S["e_used"], 1)

            def start_pass(c):
                pe.wait_ge(S["hot_ready"], c + 1)
                for n in range(2 * NT):
                    last = nc.tensor.matmul(bank[7][:, 256:256 + NE], hot[:, n // 2, n % 2, :], rv[:, n // 2, n % 2, :], start=n == 0, stop=n == 2 * NT - 1)
                last.then_inc(S["slot_ps"], 1)
                x_transposes(c, 0, 0)
                pe.wait_ge(S["xe_l"], c * (2 * NE) + 2)
                if not isinstance(c, int):
                    pe.wait_ge(S["hid_r"], c * NE)
                product(c, 0, 0, 0, 0)
                product(c, 0, 2, 0, FE)
                x_transposes(c, 0, 1)

            def four(c, i, last=False):
                for q in range(4):
                    E = c * NE + i * 4 + q
                    n = 4 + HPE * q
                    ahead = not (last and q == 3)
                    if ahead:
                        pe.wait_ge(S["xe_l"], E * 2 + 4)
                        product(c, i, n, q + 1, 0)
                    pe.wait_ge(S["hid_r"], E + 1)
                    for m in range(FE // P):
                        ins = nc.tensor.transpose(bank[4][:, m * P:(m + 1) * P], hid[:, :].rearrange("p (n m) -> p m n", m=FE // P)[:, m, :], ident[:, :])
                    ins.then_inc(S["ht_ps"], 1)
                    if ahead:
                        product(c, i, n + 2, q + 1, FE)
                    if not (last and q >= 2):
                        x_transposes(c, i, q + 2)
                    pe.wait_ge(S["ht_l"], E + 1)
                    pe.wait_ge(S["y_out"], E * 2 + 2)
                    d = n + 4 if ahead else n
                    for m in range(FE // P):
                        pe.wait_ge(S["e_split"], c * (HPE * NE) + i * (4 * HPE) + (d + m + SC + 1))
                        for b in range(2):
                            ins = passes(bank[5 + b][:, :], [(hidh[:, m, :], hidl[:, m, :], ewh[(d + m) % HS][:, b * T:(b + 1) * T],
                                                              ewl[(d + m) % HS][:, b * T:(b + 1) * T])], start=m == 0, stop=m == FE // P - 1)
                        ins.then_inc(S["e_used"], 1)

            start_pass(0)
            with pe.Fori(0, LOOPS - 1) as i:
                four(0, i)
            four(0, LOOPS - 1, last=True)
            pe.wait_ge(S["flag_ready"], 1)
            most = pe.value_load(flag[0:1, 0:1], min_val=0, max_val=T)
            with pe.If(most > P):
                with pe.Fori(1, NT) as c:
                    start_pass(c)
                    with pe.Fori(0, LOOPS - 1) as i:
                        four(c, i)
                    four(c, LOOPS - 1, last=True)


_INS = ["x", "mix_norm_g", "w_in", "b_forget", "conv_a_w", "conf_dw_w", "conf_dw_b", "conf_ln_g", "conf_ln_b",
        "w_branch", "w_gate", "b_gate", "w_out", "ffn_norm_g", "w_router_group", "w_router_expert",
        "w_expert_gate", "w_expert_up", "w_expert_down", "final_norm_g"]


def kernel(**inputs):
    import concourse.bacc as _bacc
    from concourse.bass_utils import run_bass_kernel_spmd as _run

    nc = _bacc.Bacc("TRN2", target_bir_lowering=False, num_devices=1)
    arrays, args = {}, []
    for name in _INS:
        a = np.ascontiguousarray(inputs[name])
        arrays[f"in_{name}"] = a
        args.append(nc.dram_tensor(f"in_{name}", a.shape, mybir.dt.from_np(a.dtype), kind="ExternalInput").ap())
    shape = inputs["x"].shape
    args.append(nc.dram_tensor("out_0", shape, F32, kind="ExternalOutput").ap())
    hybrid_trunk(nc, *args)
    r = _run(nc, [arrays], core_ids=[0])
    return r.results[0]["out_0"]
```
